# Optimizing a Trainium2 kernel written in Bass

```python
import jax
import jax.numpy as jnp
from jax import lax
import numpy as np
import math
import jax, jax.numpy as jnp

D_MODEL = 1024
BATCH = 1
SEQ = 256
DEPTH = 1

HEAD_DIM = 64
RWKV_HEADS = 8
RWKV_DIM = RWKV_HEADS * HEAD_DIM
LORA_W = 64
LORA_A = 64
LORA_G = 128
RWKV_COLS = 3 * RWKV_DIM + LORA_W + LORA_A + LORA_G
ATTN_PATTERNS = ((128, 1), (512, 4), (2048, 16))
ATTN_HEADS_PER_GROUP = 4
ATTN_HEADS = ATTN_HEADS_PER_GROUP * len(ATTN_PATTERNS)
ATTN_DIM = ATTN_HEADS * HEAD_DIM
ATTN_COLS = 3 * ATTN_DIM
ATTN_OUT_DIM = ATTN_HEADS_PER_GROUP * HEAD_DIM
ROT_DIM = HEAD_DIM // 4
ROPE_THETA = 500000.0
N_BRANCH = 2
IN_COLS = RWKV_COLS + ATTN_COLS + N_BRANCH * D_MODEL
MOE_GROUPS = 4
EXPERTS_PER_GROUP = 8
N_EXPERTS = MOE_GROUPS * EXPERTS_PER_GROUP
TOP_K_INNER = 2
D_EXPERT = D_MODEL // 2
MOE_BLOCK = 128
NORM_EPS = 1e-6
GN_EPS = 64e-5


def rmsnorm(x, g, eps=NORM_EPS):
    xf = x.astype(jnp.float32)
    y = xf * lax.rsqrt(jnp.mean(xf * xf, axis=-1, keepdims=True) + eps)
    return (y * g.astype(jnp.float32)).astype(x.dtype)

def partial_rope(t, positions):
    half = ROT_DIM // 2
    inv_freq = ROPE_THETA ** (-(jnp.arange(half, dtype=jnp.float32) * (2.0 / ROT_DIM)))
    ang = positions.astype(jnp.float32)[:, :, None] * inv_freq
    cos = jnp.cos(ang)[:, :, None, :]
    sin = jnp.sin(ang)[:, :, None, :]
    t1 = t[..., :half].astype(jnp.float32)
    t2 = t[..., half:ROT_DIM].astype(jnp.float32)
    rot = jnp.concatenate([t1 * cos - t2 * sin, t2 * cos + t1 * sin], axis=-1).astype(t.dtype)
    return jnp.concatenate([rot, t[..., ROT_DIM:]], axis=-1)

def wkv7_scan(r, w, k, v, a, b, reverse):
    B, T, H, N = r.shape
    seq = tuple(t.astype(jnp.float32).transpose(1, 0, 2, 3) for t in (r, w, k, v, a, b))

    def step(S, inp):
        r_t, w_t, k_t, v_t, a_t, b_t = inp
        sa = jnp.einsum('bhij,bhj->bhi', S, a_t)
        S = S * w_t[:, :, None, :] + sa[..., None] * b_t[:, :, None, :] + v_t[..., None] * k_t[:, :, None, :]
        return S, jnp.einsum('bhij,bhj->bhi', S, r_t)

    S0 = jnp.zeros((B, H, N, N), jnp.float32)
    _, y = lax.scan(step, S0, seq, reverse=reverse)
    return y.transpose(1, 0, 2, 3)

def rwkv7_branch(u, mu_prev, mu_next, w_decay0, w_decay_up, a_gate0, a_gate_up, g_up,
                 k_k, k_a, r_k, gn_w, gn_b):
    B, T, _ = u.shape
    H, N = RWKV_HEADS, HEAD_DIM
    u_prev = jnp.pad(u, ((0, 0), (1, 0), (0, 0)))[:, :T]
    u_next = jnp.pad(u, ((0, 0), (0, 1), (0, 0)))[:, 1:]
    u = u + mu_prev * (u_prev - u) + mu_next * (u_next - u)
    c = [int(i) for i in np.cumsum([0, RWKV_DIM, RWKV_DIM, RWKV_DIM, LORA_W, LORA_A, LORA_G])]
    r, k, v, xw, xa, xg = (u[..., c[i]:c[i + 1]] for i in range(6))

    def heads(t):
        return t.reshape(B, T, H, N)

    g = jax.nn.sigmoid(xg) @ g_up
    kk = heads(k * k_k).astype(jnp.float32)
    kk = kk / jnp.maximum(jnp.sqrt(jnp.sum(kk * kk, axis=-1, keepdims=True)), 1e-12)
    rh, vh = heads(r), heads(v)
    wkv = 0.0
    bonus = 0.0
    for d, reverse in enumerate((False, True)):
        w_log = -jax.nn.softplus(-(w_decay0[d] + jnp.tanh(xw) @ w_decay_up[d]).astype(jnp.float32)) - 0.5
        decay = jnp.exp(-jnp.exp(w_log))
        a = jax.nn.sigmoid(a_gate0[d] + xa @ a_gate_up[d])
        kd = heads(k * (1.0 + (a - 1.0) * k_a))
        ah = heads(a).astype(jnp.float32)
        wkv = wkv + wkv7_scan(rh, heads(decay), kd, vh, -kk, kk * ah, reverse)
        bonus = bonus + jnp.sum(rh * kd * r_k, axis=-1, keepdims=True) * vh
    mean = jnp.mean(wkv, axis=-1, keepdims=True)
    var = jnp.mean(jnp.square(wkv - mean), axis=-1, keepdims=True)
    y = ((wkv - mean) * lax.rsqrt(var + GN_EPS)).reshape(B, T, RWKV_DIM) * gn_w + gn_b
    y = y + bonus.reshape(B, T, RWKV_DIM).astype(jnp.float32)
    return (y * g).astype(u.dtype)

def banded_attention(q, k, v, band):
    B, H, L, Dh = q.shape
    nb = -(-L // band)
    Lp = nb * band
    qb = jnp.pad(q, ((0, 0), (0, 0), (0, Lp - L), (0, 0))).reshape(B, H, nb, band, Dh)

    def windows(t):
        tb = jnp.pad(t, ((0, 0), (0, 0), (band, Lp - L + band), (0, 0))).reshape(B, H, nb + 2, band, Dh)
        return jnp.concatenate([tb[:, :, :-2], tb[:, :, 1:-1], tb[:, :, 2:]], axis=3)

    kw, vw = windows(k), windows(v)
    s = jnp.einsum('bhnqd,bhnkd->bhnqk', qb, kw, preferred_element_type=jnp.float32) * (Dh ** -0.5)
    qpos = jnp.arange(nb)[:, None, None] * band + jnp.arange(band)[None, :, None]
    kpos = (jnp.arange(nb)[:, None, None] - 1) * band + jnp.arange(3 * band)[None, None, :]
    mask = (jnp.abs(kpos - qpos) <= band) & (kpos >= 0) & (kpos < L)
    s = jnp.where(mask, s, -jnp.inf)
    lse = jax.nn.logsumexp(s, axis=-1)
    p = jnp.exp(s - lse[..., None])
    o = jnp.einsum('bhnqk,bhnkd->bhnqd', p, vw.astype(jnp.float32))
    o = o.reshape(B, H, Lp, Dh)[:, :, :L].astype(v.dtype)
    return o, lse.reshape(B, H, Lp)[:, :, :L]

def dilated_window_attention(q, k, v, dilation, band):
    B, H, T, Dh = q.shape
    L = T // dilation

    def to_sub(t):
        return t.reshape(B, H, L, dilation, Dh).transpose(0, 1, 3, 2, 4).reshape(B, H * dilation, L, Dh)

    o, lse = banded_attention(to_sub(q), to_sub(k), to_sub(v), band)
    o = o.reshape(B, H, dilation, L, Dh).transpose(0, 1, 3, 2, 4).reshape(B, H, T, Dh)
    lse = lse.reshape(B, H, dilation, L).transpose(0, 1, 3, 2).reshape(B, H, T)
    return o, lse

def dilated_attention_branch(u, positions, q_norm_g, k_norm_g):
    B, T, _ = u.shape
    q = u[..., :ATTN_DIM].reshape(B, T, ATTN_HEADS, HEAD_DIM)
    k = u[..., ATTN_DIM:2 * ATTN_DIM].reshape(B, T, ATTN_HEADS, HEAD_DIM)
    v = u[..., 2 * ATTN_DIM:].reshape(B, T, ATTN_HEADS, HEAD_DIM)
    q = partial_rope(rmsnorm(q, q_norm_g), positions)
    k = partial_rope(rmsnorm(k, k_norm_g), positions)
    q, k, v = (t.transpose(0, 2, 1, 3) for t in (q, k, v))
    outs, lses = [], []
    for gi, (window, dilation) in enumerate(ATTN_PATTERNS):
        hs = slice(gi * ATTN_HEADS_PER_GROUP, (gi + 1) * ATTN_HEADS_PER_GROUP)
        o, l = dilated_window_attention(q[:, hs], k[:, hs], v[:, hs], dilation, window // (2 * dilation))
        outs.append(o)
        lses.append(l)
    alpha = jax.nn.softmax(jnp.stack(lses), axis=0)
    o = jnp.sum(alpha[..., None] * jnp.stack(outs).astype(jnp.float32), axis=0)
    return o.transpose(0, 2, 1, 3).reshape(B, T, ATTN_OUT_DIM).astype(u.dtype)

def hier_moe(h, w_router_group, b_router_group, w_router_expert, b_router_expert, w_gate, w_up, w_down):
    N, D = h.shape
    tok_idx = jnp.arange(N, dtype=jnp.int32)
    grp_logits = (h @ w_router_group).astype(jnp.float32) + b_router_group.astype(jnp.float32)
    grp_probs = jax.nn.softmax(grp_logits, axis=-1)
    grp = jnp.argmax(grp_logits, axis=-1).astype(jnp.int32)
    grp_p = grp_probs[tok_idx, grp][:, None]
    exp_logits = ((h @ w_router_expert).astype(jnp.float32)
                  + b_router_expert.astype(jnp.float32)).reshape(N, MOE_GROUPS, EXPERTS_PER_GROUP)
    exp_logits = exp_logits[tok_idx, grp]
    top_v, top_i = lax.top_k(exp_logits, TOP_K_INNER)
    gate = grp_p * jax.nn.softmax(top_v, axis=-1)
    eid = (grp[:, None] * EXPERTS_PER_GROUP + top_i).reshape(-1)
    tok = jnp.repeat(tok_idx, TOP_K_INNER)
    wts = gate.reshape(-1)
    A = N * TOP_K_INNER
    order = jnp.argsort(eid)
    e_sorted = eid[order]
    counts = jnp.bincount(eid, length=N_EXPERTS)
    padded = (counts + MOE_BLOCK - 1) // MOE_BLOCK * MOE_BLOCK
    pad_end = jnp.cumsum(padded)
    pad_start = pad_end - padded
    start = jnp.cumsum(counts) - counts
    dest = pad_start[e_sorted] + jnp.arange(A, dtype=jnp.int32) - start[e_sorted]
    M = (-(-A // MOE_BLOCK) + N_EXPERTS) * MOE_BLOCK
    n_blk = M // MOE_BLOCK
    row_tok = jnp.full((M,), N, jnp.int32).at[dest].set(tok[order])
    row_w = jnp.zeros((M,), jnp.float32).at[dest].set(wts[order])
    blk_e = jnp.minimum(jnp.searchsorted(pad_end, jnp.arange(n_blk, dtype=jnp.int32) * MOE_BLOCK, side='right'),
                        N_EXPERTS - 1)
    h_pad = jnp.concatenate([h, jnp.zeros((1, D), h.dtype)], axis=0)
    xb = h_pad[row_tok].reshape(n_blk, MOE_BLOCK, D)

    def expert_block(args):
        xblk, e = args
        return (jax.nn.silu(xblk @ w_gate[e]) * (xblk @ w_up[e])) @ w_down[e]

    yb = lax.map(expert_block, (xb, blk_e)).reshape(M, D)
    y = jnp.zeros((N + 1, D), h.dtype).at[row_tok].add(yb * row_w[:, None].astype(h.dtype))
    return y[:N]

def hybrid_layer(x, positions, norm1_g, w_in, mu_prev, mu_next, w_decay0, w_decay_up, a_gate0, a_gate_up,
                 g_up, k_k, k_a, r_k, gn_w, gn_b, w_rwkv_out, q_norm_g, k_norm_g, w_attn_out, b_merge, w_out,
                 norm2_g, w_router_group, b_router_group, w_router_expert, b_router_expert, w_gate, w_up, w_down):
    B, T, D = x.shape
    h = rmsnorm(x, norm1_g)
    proj = h @ w_in
    u_rwkv = proj[..., :RWKV_COLS]
    u_attn = proj[..., RWKV_COLS:RWKV_COLS + ATTN_COLS]
    gate_logits = proj[..., RWKV_COLS + ATTN_COLS:].reshape(B, T, N_BRANCH, D) + b_merge
    y_rwkv = rwkv7_branch(u_rwkv, mu_prev, mu_next, w_decay0, w_decay_up, a_gate0, a_gate_up, g_up,
                          k_k, k_a, r_k, gn_w, gn_b) @ w_rwkv_out
    y_attn = dilated_attention_branch(u_attn, positions, q_norm_g, k_norm_g) @ w_attn_out
    gates = jax.nn.sigmoid(gate_logits)
    x = x + (gates[:, :, 0] * y_rwkv + gates[:, :, 1] * y_attn) @ w_out
    h2 = rmsnorm(x, norm2_g)
    moe = hier_moe(h2.reshape(B * T, D), w_router_group, b_router_group, w_router_expert, b_router_expert,
                   w_gate, w_up, w_down)
    return x + moe.reshape(B, T, D)

def first_inputs(seed: int = 0) -> dict:
    key = jax.random.key(seed)
    ks = iter(jax.random.split(key, 32))

    def nrm(shape, scale):
        return scale * jax.random.normal(next(ks), shape, jnp.float32)

    def unif(shape, lo, hi):
        return jax.random.uniform(next(ks), shape, dtype=jnp.float32, minval=lo, maxval=hi)

    L = DEPTH
    x = nrm((BATCH, SEQ, D_MODEL), 1.0)
    positions = (jnp.arange(SEQ, dtype=jnp.int32)[None, :]
                 + jax.random.randint(next(ks), (BATCH, 1), 0, 1024, dtype=jnp.int32))
    return {
        'x': x,
        'positions': positions,
        'norm1_g': 1.0 + nrm((L, D_MODEL), 0.02),
        'w_in': nrm((L, D_MODEL, IN_COLS), D_MODEL ** -0.5),
        'mu_prev': unif((L, RWKV_COLS), 0.0, 0.5),
        'mu_next': unif((L, RWKV_COLS), 0.0, 0.5),
        'w_decay0': unif((L, 2, RWKV_DIM), -5.0, -1.0),
        'w_decay_up': nrm((L, 2, LORA_W, RWKV_DIM), 0.5 * LORA_W ** -0.5),
        'a_gate0': nrm((L, 2, RWKV_DIM), 0.1),
        'a_gate_up': nrm((L, 2, LORA_A, RWKV_DIM), LORA_A ** -0.5),
        'g_up': nrm((L, LORA_G, RWKV_DIM), LORA_G ** -0.5),
        'k_k': 0.85 + nrm((L, RWKV_DIM), 0.05),
        'k_a': 1.0 + nrm((L, RWKV_DIM), 0.05),
        'r_k': nrm((L, RWKV_HEADS, HEAD_DIM), 0.1),
        'gn_w': 1.0 + nrm((L, RWKV_DIM), 0.02),
        'gn_b': nrm((L, RWKV_DIM), 0.02),
        'w_rwkv_out': nrm((L, RWKV_DIM, D_MODEL), RWKV_DIM ** -0.5),
        'q_norm_g': 1.0 + nrm((L, HEAD_DIM), 0.02),
        'k_norm_g': 1.0 + nrm((L, HEAD_DIM), 0.02),
        'w_attn_out': nrm((L, ATTN_OUT_DIM, D_MODEL), ATTN_OUT_DIM ** -0.5),
        'b_merge': nrm((L, N_BRANCH, D_MODEL), 0.02),
        'w_out': nrm((L, D_MODEL, D_MODEL), D_MODEL ** -0.5),
        'norm2_g': 1.0 + nrm((L, D_MODEL), 0.02),
        'w_router_group': nrm((L, D_MODEL, MOE_GROUPS), D_MODEL ** -0.5),
        'b_router_group': nrm((L, MOE_GROUPS), 0.01),
        'w_router_expert': nrm((L, D_MODEL, N_EXPERTS), D_MODEL ** -0.5),
        'b_router_expert': nrm((L, N_EXPERTS), 0.01),
        'w_gate': nrm((L, N_EXPERTS, D_MODEL, D_EXPERT), D_MODEL ** -0.5),
        'w_up': nrm((L, N_EXPERTS, D_MODEL, D_EXPERT), D_MODEL ** -0.5),
        'w_down': nrm((L, N_EXPERTS, D_EXPERT, D_MODEL), D_EXPERT ** -0.5),
    }

def first_block(x, positions, norm1_g, w_in, mu_prev, mu_next, w_decay0, w_decay_up, a_gate0, a_gate_up,
              g_up, k_k, k_a, r_k, gn_w, gn_b, w_rwkv_out, q_norm_g, k_norm_g, w_attn_out, b_merge, w_out,
              norm2_g, w_router_group, b_router_group, w_router_expert, b_router_expert, w_gate, w_up, w_down):
    for l in range(DEPTH):
        x = hybrid_layer(x, positions, norm1_g[l], w_in[l], mu_prev[l], mu_next[l], w_decay0[l], w_decay_up[l],
                         a_gate0[l], a_gate_up[l], g_up[l], k_k[l], k_a[l], r_k[l], gn_w[l], gn_b[l],
                         w_rwkv_out[l], q_norm_g[l], k_norm_g[l], w_attn_out[l], b_merge[l], w_out[l],
                         norm2_g[l], w_router_group[l], b_router_group[l], w_router_expert[l],
                         b_router_expert[l], w_gate[l], w_up[l], w_down[l])
    return x


DEPTH_2 = 2

DIFF_HEADS = 4
DIFF_VDIM = 2 * HEAD_DIM
SB_HEADS = 8
DIFF_WIDTH = DIFF_HEADS * DIFF_VDIM
SB_WIDTH = SB_HEADS * HEAD_DIM
MIX_WIDTH = DIFF_WIDTH + SB_WIDTH
DIFF_QK = DIFF_HEADS * 2 * HEAD_DIM
SB_QK = SB_HEADS * HEAD_DIM
IN_WIDTH = 2 * DIFF_QK + DIFF_WIDTH + 2 * SB_QK + SB_WIDTH
Q_BLOCK = 128

PEER_HEADS = 8
N_KEYS = 128
N_EXPERTS_2 = N_KEYS * N_KEYS
PEER_TOPK = 16
HALF_Q = 128
QUERY_DIM = 2 * HALF_Q
TOKEN_CHUNK = 128

DEEPNORM_ALPHA = (2.0 * DEPTH_2) ** 0.25
DEEPNORM_BETA = (8.0 * DEPTH_2) ** -0.25
LN_EPS = 1e-5
RMS_EPS = 1e-5


def layer_norm(h, g, b):
    hf = h.astype(jnp.float32)
    mu = jnp.mean(hf, axis=-1, keepdims=True)
    var = jnp.mean(jnp.square(hf - mu), axis=-1, keepdims=True)
    y = (hf - mu) * lax.rsqrt(var + LN_EPS) * g.astype(jnp.float32) + b.astype(jnp.float32)
    return y.astype(h.dtype)

def alibi_slopes():
    return jnp.asarray([2.0 ** (-8.0 * (i + 1) / DIFF_HEADS) for i in range(DIFF_HEADS)], jnp.float32)

def token_mixer(h, w_in, lq1, lk1, lq2, lk2, subln_g, w_o, layer):
    B, S, _ = h.shape
    proj = h @ w_in
    s1 = DIFF_QK
    s2 = s1 + DIFF_QK
    s3 = s2 + DIFF_WIDTH
    s4 = s3 + SB_QK
    s5 = s4 + SB_QK
    dq, dk, dv, sq, sk, sv = jnp.split(proj, [s1, s2, s3, s4, s5], axis=-1)
    dq = dq.reshape(B, S, DIFF_HEADS, 2, HEAD_DIM).transpose(0, 2, 3, 1, 4)
    dk = dk.reshape(B, S, DIFF_HEADS, 2, HEAD_DIM).transpose(0, 2, 3, 1, 4)
    dv = dv.reshape(B, S, DIFF_HEADS, DIFF_VDIM).transpose(0, 2, 1, 3)
    sq = sq.reshape(B, S, SB_HEADS, HEAD_DIM).transpose(0, 2, 1, 3)
    sk = sk.reshape(B, S, SB_HEADS, HEAD_DIM).transpose(0, 2, 1, 3)
    sv = sv.reshape(B, S, SB_HEADS, HEAD_DIM).transpose(0, 2, 1, 3)

    lambda_init = 0.8 - 0.6 * math.exp(-0.3 * layer)
    lam = (jnp.exp(jnp.sum(lq1.astype(jnp.float32) * lk1.astype(jnp.float32)))
           - jnp.exp(jnp.sum(lq2.astype(jnp.float32) * lk2.astype(jnp.float32)))
           + lambda_init)
    slopes = alibi_slopes()[None, :, None, None, None]
    scale = HEAD_DIM ** -0.5

    diff_out, sb_out = [], []
    for blk in range(S // Q_BLOCK):
        q0 = blk * Q_BLOCK
        kv_len = q0 + Q_BLOCK
        t_pos = q0 + jnp.arange(Q_BLOCK)
        s_pos = jnp.arange(kv_len)
        dist = (t_pos[:, None] - s_pos[None, :]).astype(jnp.float32)

        sc = jnp.einsum('bhmqd,bhmkd->bhmqk', dq[:, :, :, q0:kv_len], dk[:, :, :, :kv_len]).astype(jnp.float32) * scale
        sc = jnp.where(dist >= 0, sc - slopes * dist, -jnp.inf)
        p = jax.nn.softmax(sc, axis=-1)
        attn = p[:, :, 0] - lam * p[:, :, 1]
        diff_out.append(jnp.einsum('bhqk,bhkd->bhqd', attn.astype(dv.dtype), dv[:, :, :kv_len]))

        z = jnp.einsum('bgqd,bgkd->bgqk', sq[:, :, q0:kv_len], sk[:, :, :kv_len]).astype(jnp.float32) * scale
        strict = dist > 0
        log_fail = jnp.where(strict, jax.nn.log_sigmoid(-z), 0.0)
        log_later = lax.cumsum(log_fail, axis=3, reverse=True) - log_fail
        w = jnp.where(strict, jnp.exp(jax.nn.log_sigmoid(z) + log_later), 0.0)
        sb_out.append(jnp.einsum('bgqk,bgkd->bgqd', w.astype(sv.dtype), sv[:, :, :kv_len]))

    diff = jnp.concatenate(diff_out, axis=2).astype(jnp.float32)
    diff = diff * lax.rsqrt(jnp.mean(jnp.square(diff), axis=-1, keepdims=True) + RMS_EPS)
    diff = diff * subln_g.astype(jnp.float32) * (1.0 - lambda_init)
    diff = diff.astype(h.dtype).transpose(0, 2, 1, 3).reshape(B, S, DIFF_WIDTH)
    sb = jnp.concatenate(sb_out, axis=2).transpose(0, 2, 1, 3).reshape(B, S, SB_WIDTH)
    mixed = jnp.concatenate([diff, sb.astype(h.dtype)], axis=-1)
    return mixed @ w_o

def peer_ffn(h, w_query, sub_keys, expert_u, expert_v):
    B, S, D = h.shape
    T = B * S
    xt = h.reshape(T, D)
    q = (xt @ w_query).reshape(T, PEER_HEADS, 2, HALF_Q).astype(jnp.float32)
    scores = jnp.einsum('thpc,hpnc->thpn', q, sub_keys.astype(jnp.float32))
    top_s, top_i = lax.top_k(scores, PEER_TOPK)
    cand_s = top_s[:, :, 0, :, None] + top_s[:, :, 1, None, :]
    cand_i = top_i[:, :, 0, :, None] * N_KEYS + top_i[:, :, 1, None, :]
    cand_s = cand_s.reshape(T, PEER_HEADS, PEER_TOPK * PEER_TOPK)
    cand_i = cand_i.reshape(T, PEER_HEADS, PEER_TOPK * PEER_TOPK)
    best_s, best_pos = lax.top_k(cand_s, PEER_TOPK)
    idx = jnp.take_along_axis(cand_i, best_pos, axis=-1)
    gate = jax.nn.softmax(best_s, axis=-1)
    n_sel = PEER_HEADS * PEER_TOPK
    n_chunks = T // TOKEN_CHUNK

    def expert_chunk(args):
        xc, ic, gc = args
        u = expert_u[ic]
        act = jax.nn.gelu(jnp.einsum('cd,ced->ce', xc, u).astype(jnp.float32), approximate=False)
        v = expert_v[ic]
        return jnp.einsum('ce,ced->cd', (gc * act).astype(v.dtype), v)

    y = lax.map(expert_chunk, (xt.reshape(n_chunks, TOKEN_CHUNK, D),
                               idx.reshape(n_chunks, TOKEN_CHUNK, n_sel),
                               gate.reshape(n_chunks, TOKEN_CHUNK, n_sel)))
    return y.reshape(B, S, D).astype(h.dtype)

def second_inputs(seed: int = 0) -> dict:
    key = jax.random.key(seed)
    ks = jax.random.split(key, 16)
    f32 = jnp.float32
    beta = DEEPNORM_BETA
    col_scale = np.concatenate([np.ones(2 * DIFF_QK), np.full(DIFF_WIDTH, beta),
                                np.ones(2 * SB_QK), np.full(SB_WIDTH, beta)]).astype(np.float32)
    x = jax.random.normal(ks[0], (BATCH, SEQ, D_MODEL), f32)
    w_in = jax.random.normal(ks[1], (DEPTH_2, D_MODEL, IN_WIDTH), f32) * (D_MODEL ** -0.5) * jnp.asarray(col_scale)
    lam_q1 = 0.1 * jax.random.normal(ks[2], (DEPTH_2, HEAD_DIM), f32)
    lam_k1 = 0.1 * jax.random.normal(ks[3], (DEPTH_2, HEAD_DIM), f32)
    lam_q2 = 0.1 * jax.random.normal(ks[4], (DEPTH_2, HEAD_DIM), f32)
    lam_k2 = 0.1 * jax.random.normal(ks[5], (DEPTH_2, HEAD_DIM), f32)
    subln_g = 1.0 + 0.02 * jax.random.normal(ks[6], (DEPTH_2, DIFF_VDIM), f32)
    w_o = jax.random.normal(ks[7], (DEPTH_2, MIX_WIDTH, D_MODEL), f32) * (MIX_WIDTH ** -0.5) * beta
    ln1_g = 1.0 + 0.02 * jax.random.normal(ks[8], (DEPTH_2, D_MODEL), f32)
    ln1_b = 0.02 * jax.random.normal(ks[9], (DEPTH_2, D_MODEL), f32)
    w_query = jax.random.normal(ks[10], (DEPTH_2, D_MODEL, PEER_HEADS * QUERY_DIM), f32) * (D_MODEL ** -0.5)
    sub_keys = jax.random.normal(ks[11], (DEPTH_2, PEER_HEADS, 2, N_KEYS, HALF_Q), f32) * (HALF_Q ** -0.5)
    expert_u = jax.random.normal(ks[12], (DEPTH_2, N_EXPERTS_2, D_MODEL), f32) * (D_MODEL ** -0.5) * beta
    expert_v = jax.random.normal(ks[13], (DEPTH_2, N_EXPERTS_2, D_MODEL), f32) * beta
    ln2_g = 1.0 + 0.02 * jax.random.normal(ks[14], (DEPTH_2, D_MODEL), f32)
    ln2_b = 0.02 * jax.random.normal(ks[15], (DEPTH_2, D_MODEL), f32)
    return {"x": x, "w_in": w_in, "lam_q1": lam_q1, "lam_k1": lam_k1, "lam_q2": lam_q2,
            "lam_k2": lam_k2, "subln_g": subln_g, "w_o": w_o, "ln1_g": ln1_g, "ln1_b": ln1_b,
            "w_query": w_query, "sub_keys": sub_keys, "expert_u": expert_u, "expert_v": expert_v,
            "ln2_g": ln2_g, "ln2_b": ln2_b}

def second_block(x, w_in, lam_q1, lam_k1, lam_q2, lam_k2, subln_g, w_o, ln1_g, ln1_b,
              w_query, sub_keys, expert_u, expert_v, ln2_g, ln2_b):
    h = x
    for l in range(DEPTH_2):
        mix = token_mixer(h, w_in[l], lam_q1[l], lam_k1[l], lam_q2[l], lam_k2[l], subln_g[l], w_o[l], l)
        h = layer_norm(DEEPNORM_ALPHA * h + mix, ln1_g[l], ln1_b[l])
        ffn = peer_ffn(h, w_query[l], sub_keys[l], expert_u[l], expert_v[l])
        h = layer_norm(DEEPNORM_ALPHA * h + ffn, ln2_g[l], ln2_b[l])
    return h


def setup_inputs(seed=0):
    out = dict(first_inputs(seed))
    for name, value in second_inputs(seed + 1).items():
        if name != "x":
            out[name + "_2"] = value
    return out


def reference(
    x, positions, norm1_g, w_in, mu_prev, mu_next, w_decay0, w_decay_up, a_gate0, a_gate_up,
    g_up, k_k, k_a, r_k, gn_w, gn_b, w_rwkv_out, q_norm_g, k_norm_g, w_attn_out, b_merge, w_out,
    norm2_g, w_router_group, b_router_group, w_router_expert, b_router_expert, w_gate, w_up,
    w_down, w_in_2, lam_q1_2, lam_k1_2, lam_q2_2, lam_k2_2, subln_g_2, w_o_2, ln1_g_2, ln1_b_2,
    w_query_2, sub_keys_2, expert_u_2, expert_v_2, ln2_g_2, ln2_b_2,
):
    x = first_block(
        x, positions, norm1_g, w_in, mu_prev, mu_next, w_decay0, w_decay_up, a_gate0, a_gate_up,
        g_up, k_k, k_a, r_k, gn_w, gn_b, w_rwkv_out, q_norm_g, k_norm_g, w_attn_out, b_merge,
        w_out, norm2_g, w_router_group, b_router_group, w_router_expert, b_router_expert,
        w_gate, w_up, w_down,
    )
    return second_block(
        x, w_in_2, lam_q1_2, lam_k1_2, lam_q2_2, lam_k2_2, subln_g_2, w_o_2, ln1_g_2, ln1_b_2,
        w_query_2, sub_keys_2, expert_u_2, expert_v_2, ln2_g_2, ln2_b_2,
    )


_drawn_inputs = setup_inputs


def setup_inputs(seed=0):
    import zlib

    import numpy as np

    out = dict(_drawn_inputs(seed))
    spreads = {}
    factors = {'w_decay_up': 2.948,
     'gn_w': 4.825,
     'gn_b': 2.851,
     'q_norm_g': 6.321,
     'k_norm_g': 8.0,
     'b_merge': 5.59,
     'b_router_group': 4.121,
     'b_router_expert': 2.686,
     'subln_g_2': 5.519}
    for name, (base, spread) in spreads.items():
        noise = np.random.default_rng([zlib.crc32(name.encode()), seed]).standard_normal(out[name].shape)
        drawn = base * np.exp(spread * noise) if base else spread * noise
        out[name] = jnp.asarray(drawn.astype(out[name].dtype))
    for name, factor in factors.items():
        out[name] = (out[name] * factor).astype(out[name].dtype)
    return out
```

```python
import math
from contextlib import ExitStack, contextmanager

import numpy as np

import concourse.bass as bass
from concourse import mybir

F32 = mybir.dt.float32
I32 = mybir.dt.int32
U32 = mybir.dt.uint32
ACT = mybir.ActivationFunctionType
ALU = mybir.AluOpType
X = mybir.AxisListType.X

P = 128
T = 256
NT = T // P
D = 1024
KD = D // P
HD = 64
BANKS, BANK = 8, 512

RH = 8
RC = RH * HD
RT = RC // P
RWKV_COLS = 3 * RC + 64 + 64 + 128
RWKV_TILES = RWKV_COLS // P
AH, SLOTS, GROUPS = 12, 4, 3
AC = AH * HD
DILATION = (1, 4, 16)
BAND = 64
DECAY = math.exp(-0.5)
NORM_EPS, GN_EPS = 1e-6, 64e-5
ROT = 16
ROPE_THETA = 500000.0
EXPERTS, MOE_GROUPS, PER_GROUP, DE = 32, 4, 8, 512
LEVELS = (1, 2, 4, 8, 16, 32, 64)

LAYERS = 2
DH = 4
SH = 8
IN2 = 3072
PH, TOPK, NKEYS = 8, 16, 128
ALPHA = (2.0 * LAYERS) ** 0.25
LN_EPS = RMS_EPS = 1e-5
NEG = -1e30



def constants():
    p = np.arange(P)[:, None]
    q = np.arange(P)[None, :]
    c = {"ident": (p == q), "head_ones": (p // HD == q // HD), "ones": np.ones((P, P))}
    for k in LEVELS:
        same = p // (2 * k) == q // (2 * k)
        c[f"low{k}"] = same & (p % (2 * k) >= k) & (q % (2 * k) < k)
        c[f"up{k}"] = same & (p % (2 * k) < k) & (q % (2 * k) >= k)
    c["p<q"], c["p<=q"], c["p>q"], c["p>=q"] = p < q, p <= q, p > q, p >= q
    band = np.zeros((P, NT, GROUPS, T))
    dist = np.zeros((P, NT, T))
    for t in range(NT):
        gap = (t * P + np.arange(P))[:, None] - np.arange(T)[None, :]
        for g, d in enumerate(DILATION):
            ok = (gap % d == 0) & (np.abs(gap) // d <= BAND)
            band[:, t, g] = np.where(ok, 0.0, NEG)
        dist[:, t] = np.where(gap >= 0, gap, -NEG)
    c["band"] = band
    c["dist"] = dist
    half = ROT // 2
    c["inv_freq"] = np.tile(np.float32(ROPE_THETA) ** -(np.arange(half, dtype=np.float32) * np.float32(2.0 / ROT)), (P, 1))
    c["iota"] = np.tile(np.arange(P), (P, 1))
    c["head_of_row"] = (p // TOPK == np.arange(PH)[None, :])
    return {k: np.ascontiguousarray(v.reshape(P, -1).astype(np.float32)) for k, v in c.items()}


SHARED = ("ident", "ones", "p>q", "p<q", "dist", "iota", "head_of_row")


def columns_of(shared):
    at, n = {}, 0
    for k, v in constants().items():
        if (k in SHARED) == shared:
            at[k] = (n, v.shape[1])
            n += v.shape[1]
    return at, n


@contextmanager
def phase(nc, semaphores):
    with ExitStack() as memory:
        number = nc.next_id()
        sems = [nc.alloc_semaphore(f"{name}_{number}") for name in semaphores.split()]
        yield (memory, *sems)
        nc.clear_and_free_semaphores(sems)
        nc.all_engine_barrier()


def chain(eng, sem):
    n = [0]

    def step(ins):
        n[0] += 1
        ins.then_inc(sem, 1)
        eng.wait_ge(sem, n[0])
    return step


def sbuf(nc, memory, name, shape, dtype=F32):
    return memory.enter_context(nc.sbuf_tensor(name, shape, dtype))


def row_at(dram, layer):
    rest = "abcd"[:len(dram.shape) - 1]
    if isinstance(layer, int):
        return dram[layer]
    spaced = " ".join(rest)
    return dram[(bass.ds(layer, 1),) + (slice(None),) * len(rest)].rearrange(
        f"l {spaced} -> (l {rest[0]}) {' '.join(rest[1:])}")



def project(nc, S, name, rows, cols, weights, slabs, norm_scale=None, evacuate=None, before=None):
    PS, C = S["psum"], S["const"]
    RING = 3
    units = []
    for s, (c0, width, form) in enumerate(slabs):
        if form == "columns":
            units += [(s, form, c0 + o, BANK, None) for o in range(0, width, 2 * P)]
        else:
            units += [(s, form, c0, width, a) for a in range(NT)]
    last_of = {u[0]: n for n, u in enumerate(units)}
    by_act = [n % 2 == 1 for n in range(len(units))]
    act_upto = [sum(by_act[:n]) for n in range(len(units) + 1)]
    FIRST_BANK = 4

    with phase(nc, "slab_in0 slab_in1 slab_in2 unit_done squares mean_sq rstd_root rstd_done rows_scaled "
                   "transposed cols_dve cols_act unit_dve unit_act") as (
            memory, slab_in0, slab_in1, slab_in2, unit_done, squares, mean_sq, rstd_root, rstd_done, rows_scaled,
            transposed, cols_dve, cols_act, unit_dve, unit_act):
        ring = sbuf(nc, memory, f"{name}_ring", [P, RING, KD, BANK])
        scaled = sbuf(nc, memory, f"{name}_scaled", [P, NT, D]) if norm_scale is not None else rows
        stat = sbuf(nc, memory, f"{name}_stat", [P, 4, NT])
        slab_in = (slab_in0, slab_in1, slab_in2)
        w = weights.rearrange("(k p) n -> p k n", p=P)

        def banks_of_columns(k):
            return PS[:, k // 2, (k % 2) * T:(k % 2) * T + T]

        with nc.Block() as block:
            @block.sync
            def _(sp):
                for s, (c0, width, form) in enumerate(slabs):
                    if s >= RING:
                        sp.wait_ge(unit_done, last_of[s - RING] + 1)
                    sp.dma_start(ring[:, s % RING, :, 0:width], w[:, :, c0:c0 + width]).then_inc(slab_in[s % RING], 16)

            @block.scalar
            def _(act):
                if norm_scale is not None:
                    for a in range(NT):
                        nc.scalar.activation(scaled[:, a, :], rows[:, a, :], ACT.Square,
                                             accum_out=stat[:, 0, a:a + 1]).then_inc(squares, 1)
                    act.wait_ge(mean_sq, 1)
                    nc.scalar.activation(stat[:, 2, :], stat[:, 1, :], ACT.Sqrt).then_inc(rstd_root, 1)
                act.wait_ge(transposed, KD)
                for k in (2, 3, 6, 7):
                    if norm_scale is None:
                        nc.scalar.activation(cols[:, k, :], banks_of_columns(k), ACT.Copy).then_inc(cols_act, 1)
                    else:
                        nc.scalar.activation(cols[:, k, :], banks_of_columns(k), ACT.Copy,
                                             scale=norm_scale[:, k:k + 1]).then_inc(cols_act, 1)
                for n, (s, form, c0, width, a) in enumerate(units):
                    if by_act[n]:
                        act.wait_ge(unit_done, n + 1)
                        evacuate("act", act, form, PS[:, (n + FIRST_BANK) % BANKS, 0:width], c0, a).then_inc(unit_act, 1)

            @block.vector
            def _(dve):
                if norm_scale is not None:
                    dve.wait_ge(squares, NT)
                    nc.vector.tensor_scalar(stat[:, 1, :], stat[:, 0, :], 1.0 / D, NORM_EPS, ALU.mult,
                                            ALU.add).then_inc(mean_sq, 1)
                    dve.wait_ge(rstd_root, 1)
                    nc.vector.reciprocal(stat[:, 3, :], stat[:, 2, :]).then_inc(rstd_done, 1)
                    dve.wait_ge(rstd_done, 1)
                    for a in range(NT):
                        nc.vector.tensor_scalar(scaled[:, a, :], rows[:, a, :], stat[:, 3, a:a + 1], None,
                                                ALU.mult).then_inc(rows_scaled, 1)
                dve.wait_ge(transposed, KD)
                for k in (0, 1, 4, 5):
                    if norm_scale is None:
                        nc.vector.tensor_copy(cols[:, k, :], banks_of_columns(k)).then_inc(cols_dve, 1)
                    else:
                        nc.vector.tensor_scalar(cols[:, k, :], banks_of_columns(k), norm_scale[:, k:k + 1], None,
                                                ALU.mult).then_inc(cols_dve, 1)
                for n, (s, form, c0, width, a) in enumerate(units):
                    if not by_act[n]:
                        dve.wait_ge(unit_done, n + 1)
                        evacuate("dve", dve, form, PS[:, (n + FIRST_BANK) % BANKS, 0:width], c0, a).then_inc(unit_dve, 1)

            @block.tensor
            def _(pe):
                if norm_scale is not None:
                    pe.wait_ge(rows_scaled, NT)
                for k in range(KD):
                    for a in range(NT):
                        last = nc.tensor.transpose(banks_of_columns(k)[:, a * P:(a + 1) * P],
                                                   scaled[:, a, k * P:(k + 1) * P], C["ident"])
                    last.then_inc(transposed, 1)
                pe.wait_ge(cols_dve, KD // 2)
                pe.wait_ge(cols_act, KD // 2)
                for n, (s, form, c0, width, a) in enumerate(units):
                    bank = PS[:, (n + FIRST_BANK) % BANKS, :]
                    if n == 0 or units[n - 1][0] != s:
                        pe.wait_ge(slab_in[s % RING], 16 * (s // RING + 1))
                    if n >= BANKS:
                        m = n - BANKS
                        if by_act[m]:
                            pe.wait_ge(unit_act, act_upto[m + 1])
                        else:
                            pe.wait_ge(unit_dve, m + 1 - act_upto[m + 1])
                    o = c0 - slabs[s][0]
                    for half in range(2 if form == "columns" else 1):
                        for k in range(KD):
                            if form == "columns":
                                last = nc.tensor.matmul(bank[:, half * T:(half + 1) * T],
                                                        ring[:, s % RING, k, o + half * P:o + (half + 1) * P],
                                                        cols[:, k, :], start=(k == 0), stop=(k == KD - 1))
                            else:
                                last = nc.tensor.matmul(bank[:, 0:width], cols[:, k, a * P:(a + 1) * P],
                                                        ring[:, s % RING, k, 0:width],
                                                        start=(k == 0), stop=(k == KD - 1))
                    last.then_inc(unit_done, 1)



def rwkv_prepare(nc, S):
    PS, C, W, R = S["psum"], S["const"], S["weights"], S["rwkv"]
    u, mixed = S["u_rwkv"], R["mixed"]
    r, k, v = (mixed[:, i * RT:(i + 1) * RT, :] for i in range(3))
    LORA, GATE = 3 * RT, 3 * RT + 1

    with phase(nc, "dve_step act_step mixed_done lora_ready unit_done unit_act key_sq norm_sq norm_done decay_in "
                   "scan_done exp_done bonus_in bonus_done v_done kb_ready kb_rows rows_out kappa_done") as (
            memory, dve_step, act_step, mixed_done, lora_ready, unit_done, unit_act, key_sq, norm_sq, norm_done,
            decay_in, scan_done, exp_done, bonus_in, bonus_done, v_done, kb_ready, kb_rows, rows_out, kappa_done):
        c0 = sbuf(nc, memory, "mix_self", [P, RWKV_TILES])
        tanh_w = sbuf(nc, memory, "tanh_w", [P, T])
        sig_g = sbuf(nc, memory, "sig_g", [P, T])
        sig_w = sbuf(nc, memory, "sig_w", [P, 2, RT, T])
        a_gate = sbuf(nc, memory, "a_gate", [P, 2, RT, T])
        kappa = sbuf(nc, memory, "kappa", [P, RT, T])
        sq = sbuf(nc, memory, "key_squares", [P, RT, T])
        total = sbuf(nc, memory, "decay_sum", [P, 2, RT, T])
        before = sbuf(nc, memory, "decay_before", [P, 2, RT, T])
        norm = before[:, 1]
        mid = sbuf(nc, memory, "decay_mid", [P, 2, RT, NT])
        nmid = sbuf(nc, memory, "decay_negmid", [P, 2, RT, NT])
        grow, back, shrx = R["r"], R["b"], R["a"]
        one_k = sbuf(nc, memory, "one_minus_ka", [P, RT])
        carry_in = sbuf(nc, memory, "carry_exponent", [P, 2, RT])

        units = [("g", 0, c) for c in (0, 2)] + [(kind, d, c) for d in range(2) for kind in "wa" for c in (0, 2)]
        FIRST = (0, 1)
        END = (P - 1, P)

        with nc.Block() as block:
            @block.vector
            def _(dve):
                step = chain(dve, dve_step)
                step(nc.vector.tensor_tensor(c0[:, :], W["mu_prev"], W["mu_next"], ALU.add))
                step(nc.vector.tensor_scalar(c0[:, :], c0[:, :], -1.0, 1.0, ALU.mult, ALU.add))
                order = [LORA, GATE] + list(range(3 * RT))
                for i, (part, to) in enumerate(((order[:2], 1), (order[2:], 2))):
                    for c in part:
                        last = nc.vector.tensor_scalar(mixed[:, c, :], u[:, c, 1:T + 1], c0[:, c:c + 1], None, ALU.mult)
                    step(last)
                    for c in part:
                        last = nc.vector.scalar_tensor_tensor(mixed[:, c, :], u[:, c, 0:T], W["mu_prev"][:, c:c + 1],
                                                              mixed[:, c, :], ALU.mult, ALU.add)
                    step(last)
                    for c in part:
                        last = nc.vector.scalar_tensor_tensor(mixed[:, c, :], u[:, c, 2:T + 2],
                                                              W["mu_next"][:, c:c + 1], mixed[:, c, :],
                                                              ALU.mult, ALU.add)
                    last.then_inc(mixed_done, 1)
                    dve.wait_ge(mixed_done, to)
                for c in range(RT):
                    last = nc.vector.tensor_scalar(kappa[:, c, :], k[:, c, :], W["k_k"][:, c:c + 1], None, ALU.mult)
                step(last)
                nc.vector.tensor_tensor(sq[:, :, :], kappa[:, :, :], kappa[:, :, :], ALU.mult).then_inc(key_sq, 1)
                step(nc.vector.tensor_scalar(one_k[:, :], W["k_a"], -1.0, 1.0, ALU.mult, ALU.add))
                dve.wait_ge(norm_done, 1)
                step(nc.vector.tensor_scalar(norm[:, :, :], norm[:, :, :], 1e-12, None, ALU.max))
                step(nc.vector.reciprocal(norm[:, :, :], norm[:, :, :]))
                nc.vector.tensor_tensor(kappa[:, :, :], kappa[:, :, :], norm[:, :, :], ALU.mult).then_inc(kappa_done, 1)
                for d in range(2):
                    dve.wait_ge(unit_act, 4 + 4 * d)
                    for c in range(RT):
                        for a in range(NT):
                            src, dst = sig_w[:, d, c, a * P:(a + 1) * P], total[:, d, c, a * P:(a + 1) * P]
                            if d:
                                src, dst = src[:, ::-1], dst[:, ::-1]
                            last = nc.vector.tensor_tensor_scan(dst, C["ones"], src, 0.0, ALU.mult, ALU.add)
                    step(last)
                    nc.vector.tensor_tensor(before[:, d, :, :], total[:, d, :, :], sig_w[:, d, :, :], ALU.subtract)
                    m = P // 2 - 1 if d == 0 else P // 2
                    by_chunk = total[:, d, :, :].rearrange("p c (a n) -> p c a n", n=P)
                    step(nc.vector.tensor_scalar(mid[:, d, :, :], by_chunk[:, :, :, m], DECAY, None, ALU.mult))
                    step(nc.vector.tensor_scalar(nmid[:, d, :, :], mid[:, d, :, :], -1.0, None, ALU.mult))
                    f = FIRST[d]
                    step(nc.vector.tensor_tensor(carry_in[:, d, :], mid[:, d, :, f], mid[:, d, :, 1 - f], ALU.subtract))
                    nc.vector.scalar_tensor_tensor(carry_in[:, d, :], total[:, d, :, END[d]], -DECAY, carry_in[:, d, :],
                                                   ALU.mult, ALU.add).then_inc(scan_done, 1)
                for d in range(2):
                    dve.wait_ge(unit_act, 6 + 4 * d)
                    dve.wait_ge(exp_done, 2 * d + 1)
                    dve.wait_ge(kappa_done, 1)
                    step(nc.vector.tensor_tensor(sq[:, :, :], kappa[:, :, :], a_gate[:, d, :, :], ALU.mult))
                    for c in range(RT):
                        last = nc.vector.tensor_scalar(a_gate[:, d, c, :], a_gate[:, d, c, :], W["k_a"][:, c:c + 1],
                                                       one_k[:, c:c + 1], ALU.mult, ALU.add)
                    step(last)
                    step(nc.vector.tensor_tensor(a_gate[:, d, :, :], a_gate[:, d, :, :], k, ALU.mult))
                    step(nc.vector.tensor_tensor(R["k"][:, d, :, :], a_gate[:, d, :, :], back[:, d, :, :], ALU.mult))
                    step(nc.vector.tensor_tensor(R["b"][:, d, :, :], sq[:, :, :], back[:, d, :, :], ALU.mult))
                    nc.vector.tensor_tensor(R["r"][:, d, :, :], r, grow[:, d, :, :], ALU.mult)
                    nc.vector.scalar_tensor_tensor(R["a"][:, d, :, :], kappa[:, :, :], -1.0, shrx[:, d, :, :],
                                                   ALU.mult, ALU.mult).then_inc(kb_ready, 1)
                step(nc.vector.tensor_tensor(sq[:, :, :], a_gate[:, 0, :, :], a_gate[:, 1, :, :], ALU.add))
                step(nc.vector.tensor_tensor(sq[:, :, :], sq[:, :, :], r, ALU.mult))
                for c in range(RT):
                    last = nc.vector.tensor_scalar(sq[:, c, :], sq[:, c, :], W["r_k"][:, c:c + 1], None, ALU.mult)
                last.then_inc(bonus_in, 1)
                dve.wait_ge(bonus_done, 1)
                nc.vector.tensor_tensor(R["bonus"][:, :, :], PS[:, 0:2, :].rearrange("p b (c t) -> p (b c) t", t=T), v,
                                        ALU.mult)

            @block.scalar
            def _(act):
                step = chain(act, act_step)
                act.wait_ge(mixed_done, 1)
                nc.scalar.activation(tanh_w[0:HD, :], mixed[0:HD, LORA, :], ACT.Tanh)
                nc.scalar.activation(sig_g[:, :], mixed[:, GATE, :], ACT.Sigmoid).then_inc(lora_ready, 1)
                for n, (kind, d, c) in enumerate(units):
                    act.wait_ge(unit_done, n + 1)
                    for h in range(2):
                        src = PS[:, n % BANKS, h * T:(h + 1) * T]
                        i = d * RT + c + h
                        if kind == "g":
                            last = nc.scalar.activation(R["gate"][:, c + h, :], src, ACT.Copy)
                        elif kind == "w":
                            last = nc.scalar.activation(sig_w[:, d, c + h, :], src, ACT.Sigmoid,
                                                        bias=W["w_decay0"][:, i:i + 1])
                        else:
                            last = nc.scalar.activation(a_gate[:, d, c + h, :], src, ACT.Sigmoid,
                                                        bias=W["a_gate0"][:, i:i + 1])
                    last.then_inc(unit_act, 1)
                act.wait_ge(norm_sq, 1)
                nc.scalar.activation(norm[:, :, :], PS[:, 4:6, :].rearrange("p b (c t) -> p (b c) t", t=T),
                                     ACT.Sqrt).then_inc(norm_done, 1)
                for d in range(2):
                    act.wait_ge(scan_done, d + 1)
                    for c in range(RT):
                        for a in range(NT):
                            s = slice(a * P, (a + 1) * P)
                            nc.scalar.activation(grow[:, d, c, s], total[:, d, c, s], ACT.Exp, scale=-DECAY,
                                                 bias=mid[:, d, c, a:a + 1])
                            nc.scalar.activation(back[:, d, c, s], total[:, d, c, s], ACT.Exp, scale=DECAY,
                                                 bias=nmid[:, d, c, a:a + 1])
                            last = nc.scalar.activation(shrx[:, d, c, s], before[:, d, c, s], ACT.Exp, scale=-DECAY,
                                                        bias=mid[:, d, c, a:a + 1])
                    last.then_inc(exp_done, 1)
                    nc.scalar.activation(R["carry"][:, d, :], carry_in[:, d, :], ACT.Exp).then_inc(exp_done, 1)
                act.wait_ge(v_done, 1)
                nc.scalar.activation(R["v_rows"][:, :, :], PS[:, 2:4, :], ACT.Copy)
                for d in range(2):
                    act.wait_ge(kb_rows, d + 1)
                    nc.scalar.activation(R["b_rows"][:, d, :], PS[:, 6, :], ACT.Copy)
                    nc.scalar.activation(R["k_rows"][:, d, :], PS[:, 7, :], ACT.Copy).then_inc(rows_out, 1)

            @block.tensor
            def _(pe):
                pe.wait_ge(lora_ready, 1)
                for n, (kind, d, c) in enumerate(units):
                    if n >= BANKS:
                        pe.wait_ge(unit_act, n - BANKS + 1)
                    for h in range(2):
                        out, s = PS[:, n % BANKS, h * T:(h + 1) * T], slice((c + h) * P, (c + h + 1) * P)
                        if kind == "g":
                            last = nc.tensor.matmul(out, W["g_up"][:, s], sig_g[:, :], start=True, stop=True)
                        elif kind == "w":
                            last = nc.tensor.matmul(out, W["lora_up"][0:HD, d, s], tanh_w[0:HD, :],
                                                    start=True, stop=True)
                        else:
                            last = nc.tensor.matmul(out, W["lora_up"][HD:P, d, s], mixed[HD:P, LORA, :],
                                                    start=True, stop=True)
                    last.then_inc(unit_done, 1)
                pe.wait_ge(key_sq, 1)
                pe.wait_ge(unit_act, len(units))
                for c in range(RT):
                    last = nc.tensor.matmul(PS[:, 4 + c // 2, (c % 2) * T:(c % 2 + 1) * T], C["head_ones"], sq[:, c, :],
                                            start=True, stop=True)
                last.then_inc(norm_sq, 1)
                pe.wait_ge(mixed_done, 2)
                for a in range(NT):
                    for c in range(RT):
                        last = nc.tensor.transpose(PS[:, 2 + a, c * P:(c + 1) * P], v[:, c, a * P:(a + 1) * P],
                                                   C["ident"])
                last.then_inc(v_done, 1)
                for d in range(2):
                    pe.wait_ge(kb_ready, d + 1)
                    if d:
                        pe.wait_ge(rows_out, d)
                    s = slice(FIRST[d] * P, (FIRST[d] + 1) * P)
                    for c in range(RT):
                        nc.tensor.transpose(PS[:, 6, c * P:(c + 1) * P], R["b"][:, d, c, s], C["ident"])
                        last = nc.tensor.transpose(PS[:, 7, c * P:(c + 1) * P], R["k"][:, d, c, s], C["ident"])
                    last.then_inc(kb_rows, 1)
                pe.wait_ge(bonus_in, 1)
                for c in range(RT):
                    last = nc.tensor.matmul(PS[:, c // 2, (c % 2) * T:(c % 2 + 1) * T], C["head_ones"], sq[:, c, :],
                                            start=True, stop=True)
                last.then_inc(bonus_done, 1)


def rwkv_scan(nc, S):
    PS, C, R = S["psum"], S["const"], S["rwkv"]
    pairs = [[(d, t, g) for g in range(2)] for d, t in ((0, 0), (1, 1), (0, 1), (1, 0))]
    NL = len(LEVELS) - 1

    with phase(nc, "dve_step products_done l_copied first_done w_done w_copied x_done x_added masked cross_done cross_copied "
                   "rhs_done rhs_copied u_done u_copied state_done state_scaled y_done y_added") as (
            memory, dve_step, products_done, l_copied, first_done, w_done, w_copied, x_done, x_added, masked, cross_done,
            cross_copied, rhs_done, rhs_copied, u_done, u_copied, state_done, state_scaled, y_done, y_added):
        between = sbuf(nc, memory, "between", [P, 2, NL, BANK])
        low = sbuf(nc, memory, "low", [P, 2, BANK])
        x = sbuf(nc, memory, "inv_t", [P, 2, BANK])
        xt = sbuf(nc, memory, "inv", [P, 2, BANK])
        w = sbuf(nc, memory, "half_w", [P, 2, BANK])
        lak = sbuf(nc, memory, "lak", [P, 2, BANK])
        mrb = sbuf(nc, memory, "mrb", [P, 2, BANK])
        mrk = sbuf(nc, memory, "mrk", [P, 2, BANK])
        rhs = sbuf(nc, memory, "rhs", [P, 2, 4 * HD])
        uu = sbuf(nc, memory, "uu", [P, 2, 4 * HD])
        state = sbuf(nc, memory, "state", [P, 2, RT, HD])

        def four(ap):
            return ap.rearrange("p (i n) -> p i n", n=P)

        def mask(name):
            return C[name].unsqueeze(1).to_broadcast([P, 4, P])

        def head(g, i):
            h = 2 * i + g
            return i, slice(g * HD, (g + 1) * HD), slice(h * HD, (h + 1) * HD)

        with nc.Block() as block:
            @block.tensor
            def _(pe):
                for n, pair in enumerate(pairs):
                    first = n < 2
                    for q, (d, t, g) in enumerate(pair):
                        m = 2 * n + q
                        if m >= 2:
                            pe.wait_ge(y_added, m - 1)
                            pe.wait_ge(u_copied, m - 1)
                        ts = slice(t * P, (t + 1) * P)
                        for i in range(4):
                            c, rows, _ = head(g, i)
                            s = slice(i * P, (i + 1) * P)
                            a_, b_ = R["a"][rows, d, c, ts], R["b"][rows, d, c, ts]
                            nc.tensor.matmul(PS[:, 4 * q, s], a_, b_, start=True, stop=True)
                            last = nc.tensor.matmul(PS[:, 4 * q + 1, s], b_, a_, start=True, stop=True)
                        last.then_inc(products_done, 1)
                    for j in range(3):
                        for q, (d, t, g) in enumerate(pair):
                            m = 2 * n + q
                            if j:
                                pe.wait_ge(cross_copied, 3 * 2 * n + 2 * (j - 1) + q + 1)
                            ts = slice(t * P, (t + 1) * P)
                            for i in range(4):
                                c, rows, _ = head(g, i)
                                one, two = (("k", "a"), ("b", "r"), ("k", "r"))[j]
                                last = nc.tensor.matmul(PS[:, 4 * q + 3, i * P:(i + 1) * P], R[one][rows, d, c, ts],
                                                        R[two][rows, d, c, ts], start=True, stop=True)
                            last.then_inc(cross_done, 1)
                    for l in range(NL):
                        for q in range(2):
                            m = 2 * n + q
                            if l == 0:
                                pe.wait_ge(first_done, m + 1)
                                pe.wait_ge(masked, NL * 2 * n + q + 1)
                                pe.wait_ge(l_copied, m + 1)
                            else:
                                pe.wait_ge(masked, NL * 2 * n + 2 * l + q + 1)
                                pe.wait_ge(x_added, NL * 2 * n + 2 * (l - 1) + q + 1)
                            for i in range(4):
                                s = slice(i * P, (i + 1) * P)
                                last = nc.tensor.matmul(PS[:, 4 * q, s], between[:, q, l, s], x[:, q, s],
                                                        start=True, stop=True)
                            last.then_inc(w_done, 1)
                        for q in range(2):
                            pe.wait_ge(w_copied, NL * 2 * n + 2 * l + q + 1)
                            for i in range(4):
                                s = slice(i * P, (i + 1) * P)
                                nc.tensor.matmul(PS[:, 4 * q + 1, s], xt[:, q, s], w[:, q, s], start=True, stop=True)
                                last = nc.tensor.matmul(PS[:, 4 * q + 2, s], w[:, q, s], xt[:, q, s],
                                                        start=True, stop=True)
                            last.then_inc(x_done, 1)
                    for q, (d, t, g) in enumerate(pair):
                        m = 2 * n + q
                        ts = slice(t * P, (t + 1) * P)
                        pe.wait_ge(cross_copied, 3 * 2 * (n + 1) - 2 + q + 1)
                        pe.wait_ge(x_added, NL * 2 * (n + 1) - 2 + q + 1)
                        if not first:
                            pe.wait_ge(state_scaled, 2 * (n - 2) + q + 1)
                        for i in range(4):
                            c, rows, cols = head(g, i)
                            o = PS[:, 4 * q, i * HD:(i + 1) * HD]
                            last = nc.tensor.matmul(o, lak[:, q, i * P:(i + 1) * P], R["v_rows"][:, t, cols],
                                                    start=True, stop=first)
                            if not first:
                                last = nc.tensor.matmul(o, R["a"][rows, d, c, ts], state[rows, d, c, :],
                                                        start=False, stop=True)
                        last.then_inc(rhs_done, 1)
                    for q in range(2):
                        m = 2 * n + q
                        pe.wait_ge(rhs_copied, m + 1)
                        for i in range(4):
                            last = nc.tensor.matmul(PS[:, 4 * q + 1, i * HD:(i + 1) * HD], x[:, q, i * P:(i + 1) * P],
                                                    rhs[:, q, i * HD:(i + 1) * HD], start=True, stop=True)
                        last.then_inc(u_done, 1)
                    for q, (d, t, g) in enumerate(pair):
                        m = 2 * n + q
                        pe.wait_ge(u_copied, m + 1)
                        ts = slice(t * P, (t + 1) * P)
                        for i in range(4):
                            c, rows, cols = head(g, i)
                            if first:
                                o = PS[rows, 4 * q + 2, i * HD:(i + 1) * HD]
                                nc.tensor.matmul(o, R["b_rows"][:, d, cols], uu[:, q, i * HD:(i + 1) * HD],
                                                 start=True, stop=False)
                                last = nc.tensor.matmul(o, R["k_rows"][:, d, cols], R["v_rows"][:, t, cols],
                                                        start=False, stop=True)
                        if first:
                            last.then_inc(state_done, 1)
                        for i in range(4):
                            c, rows, cols = head(g, i)
                            o = PS[rows, 4 * q + 3, i * P:(i + 1) * P]
                            nc.tensor.matmul(o, uu[:, q, i * HD:(i + 1) * HD], mrb[:, q, i * P:(i + 1) * P],
                                             start=True, stop=False)
                            last = nc.tensor.matmul(o, R["v_rows"][:, t, cols], mrk[:, q, i * P:(i + 1) * P],
                                                    start=False, stop=first)
                            if not first:
                                last = nc.tensor.matmul(o, state[rows, d, c, :], R["r"][rows, d, c, ts],
                                                        start=False, stop=True)
                        last.then_inc(y_done, 1)

            @block.scalar
            def _(act):
                for n, pair in enumerate(pairs):
                    for q in range(2):
                        act.wait_ge(products_done, 2 * n + q + 1)
                        if n:
                            act.wait_ge(masked, NL * 2 * n)
                            act.wait_ge(first_done, 2 * n)
                        nc.scalar.activation(low[:, q, :], PS[:, 4 * q, :], ACT.Copy).then_inc(l_copied, 1)
                    for l in range(NL):
                        for q in range(2):
                            act.wait_ge(w_done, NL * 2 * n + 2 * l + q + 1)
                            nc.scalar.activation(w[:, q, :], PS[:, 4 * q, :], ACT.Copy).then_inc(w_copied, 1)
                    for q in range(2):
                        act.wait_ge(rhs_done, 2 * n + q + 1)
                        nc.scalar.activation(rhs[:, q, :], PS[:, 4 * q, 0:4 * HD], ACT.Copy).then_inc(rhs_copied, 1)
                    for q in range(2):
                        act.wait_ge(u_done, 2 * n + q + 1)
                        nc.scalar.activation(uu[:, q, :], PS[:, 4 * q + 1, 0:4 * HD], ACT.Copy).then_inc(u_copied, 1)
                    if n < 2:
                        for q, (d, t, g) in enumerate(pair):
                            act.wait_ge(state_done, 2 * n + q + 1)
                            for i in range(4):
                                c, rows, _ = head(g, i)
                                last = nc.scalar.activation(state[rows, d, c, :],
                                                            PS[rows, 4 * q + 2, i * HD:(i + 1) * HD],
                                                            ACT.Copy, scale=R["carry"][rows, d, c:c + 1])
                            last.then_inc(state_scaled, 1)

            @block.gpsimd
            def _(pool):
                for n, pair in enumerate(pairs):
                    for l in range(NL):
                        for q, (d, t, g) in enumerate(pair):
                            if l == 0:
                                pool.wait_ge(l_copied, 2 * n + q + 1)
                            if n:
                                pool.wait_ge(w_done, NL * 2 * (n - 1) + 2 * l + q + 1)
                            name = ("low", "up")[d] + str(LEVELS[l + 1])
                            nc.gpsimd.tensor_tensor(four(between[:, q, l, :]), four(low[:, q, :]), mask(name),
                                                    ALU.mult).then_inc(masked, 1)

            @block.vector
            def _(dve):
                step = chain(dve, dve_step)
                for n, pair in enumerate(pairs):
                    for q, (d, t, g) in enumerate(pair):
                        m = 2 * n + q
                        dve.wait_ge(products_done, m + 1)
                        lo, up = (("low1", "up1"), ("up1", "low1"))[d]
                        dve.wait_ge(l_copied, m + 1)
                        nc.vector.tensor_tensor(four(xt[:, q, :]), four(low[:, q, :]), mask(lo), ALU.mult)
                        step(nc.vector.tensor_tensor(four(x[:, q, :]), four(PS[:, 4 * q + 1, :]), mask(up), ALU.mult))
                        step(nc.vector.tensor_tensor(four(xt[:, q, :]), four(xt[:, q, :]), mask("ident"), ALU.add))
                        nc.vector.tensor_tensor(four(x[:, q, :]), four(x[:, q, :]), mask("ident"),
                                                ALU.add).then_inc(first_done, 1)
                    for j in range(3):
                        for q, (d, t, g) in enumerate(pair):
                            dve.wait_ge(cross_done, 3 * 2 * n + 2 * j + q + 1)
                            name = (("p<q", "p<=q", "p<=q"), ("p>q", "p>=q", "p>=q"))[d][j]
                            nc.vector.tensor_tensor(four((lak, mrb, mrk)[j][:, q, :]), four(PS[:, 4 * q + 3, :]),
                                                    mask(name), ALU.mult).then_inc(cross_copied, 1)
                    for l in range(NL):
                        for q in range(2):
                            dve.wait_ge(x_done, NL * 2 * n + 2 * l + q + 1)
                            nc.vector.tensor_tensor(xt[:, q, :], xt[:, q, :], PS[:, 4 * q + 2, :], ALU.add)
                            nc.vector.tensor_tensor(x[:, q, :], x[:, q, :], PS[:, 4 * q + 1, :],
                                                    ALU.add).then_inc(x_added, 1)
                    for q, (d, t, g) in enumerate(pair):
                        dve.wait_ge(y_done, 2 * n + q + 1)
                        rows = head(g, 0)[1]
                        out = R["y"][rows, :, t * P:(t + 1) * P]
                        src = PS[rows, 4 * q + 3, :].rearrange("p (c t) -> p c t", t=P)
                        if n < 2:
                            nc.vector.tensor_copy(out, src).then_inc(y_added, 1)
                        else:
                            dve.wait_ge(y_added, 4)
                            nc.vector.tensor_tensor(out, out, src, ALU.add).then_inc(y_added, 1)


def rwkv_finish(nc, S):
    PS, C, W, R = S["psum"], S["const"], S["weights"], S["rwkv"]
    y = R["y"]
    flat = "p b (c t) -> p (b c) t"
    with phase(nc, "dve_step mean_done centred squared var_done root_done") as (
            memory, dve_step, mean_done, centred, squared, var_done, root_done):
        sq = sbuf(nc, memory, "gn_squares", [P, RT, T])
        root = sbuf(nc, memory, "gn_root", [P, RT, T])
        eps = sbuf(nc, memory, "gn_eps", [P, 1])
        mean = sbuf(nc, memory, "gn_mean", [P, RT, T])

        with nc.Block() as block:
            @block.tensor
            def _(pe):
                for c in range(RT):
                    last = nc.tensor.matmul(PS[:, c // 2, (c % 2) * T:(c % 2 + 1) * T], C["head_ones"], y[:, c, :],
                                            start=True, stop=True)
                last.then_inc(mean_done, 1)
                pe.wait_ge(squared, 1)
                for c in range(RT):
                    last = nc.tensor.matmul(PS[:, 2 + c // 2, (c % 2) * T:(c % 2 + 1) * T], C["head_ones"], sq[:, c, :],
                                            start=True, stop=True)
                last.then_inc(var_done, 1)

            @block.scalar
            def _(act):
                act.wait_ge(centred, 1)
                nc.scalar.activation(sq[:, :, :], y[:, :, :], ACT.Square).then_inc(squared, 1)
                act.wait_ge(var_done, 1)
                nc.scalar.activation(root[:, :, :], PS[:, 2:4, :].rearrange(flat, t=T), ACT.Sqrt, scale=1.0 / HD,
                                     bias=eps[:, 0:1]).then_inc(root_done, 1)

            @block.vector
            def _(dve):
                step = chain(dve, dve_step)
                step(nc.vector.memset(eps[:, :], GN_EPS))
                dve.wait_ge(mean_done, 1)
                nc.vector.scalar_tensor_tensor(y[:, :, :], PS[:, 0:2, :].rearrange(flat, t=T), -1.0 / HD, y[:, :, :],
                                               ALU.mult, ALU.add).then_inc(centred, 1)
                dve.wait_ge(root_done, 1)
                step(nc.vector.reciprocal(root[:, :, :], root[:, :, :]))
                step(nc.vector.tensor_tensor(root[:, :, :], root[:, :, :], y[:, :, :], ALU.mult))
                for c in range(RT):
                    last = nc.vector.tensor_scalar(root[:, c, :], root[:, c, :], W["gn_w"][:, c:c + 1],
                                                   W["gn_b"][:, c:c + 1], ALU.mult, ALU.add)
                step(last)
                step(nc.vector.tensor_tensor(root[:, :, :], root[:, :, :], R["bonus"][:, :, :], ALU.add))
                nc.vector.tensor_tensor(y[:, :, :], root[:, :, :], R["gate"][:, :, :], ALU.mult)



def attention(nc, S):
    PS, C, W = S["psum"], S["const"], S["weights"]
    qkv = S["qkv"]
    NH = 2 * AH
    scale = HD ** -0.5
    work = [(s, a) for s in range(SLOTS) for a in range(NT)]

    with phase(nc, "merge_in dve_step act_step squared mean_sq root_done normed angles sines transposed copied scores_done "
                   "masked max_done exp_done probs_t probs_copied_act probs_copied_dve out_done out_scaled out_t act_copied") as (
            memory, merge_in, dve_step, act_step, squared, mean_sq, root_done, normed, angles, sines, transposed, copied,
            scores_done, masked, max_done, exp_done, probs_t, probs_copied_act, probs_copied_dve, out_done, out_scaled,
            out_t, act_copied):
        sq = sbuf(nc, memory, "qk_squares", [P, NT, 2 * AC])
        ss = sbuf(nc, memory, "qk_sums", [P, NT, NH])
        pos = sbuf(nc, memory, "pos", [P, NT])
        ang = sbuf(nc, memory, "angle", [P, 2, NT, ROT // 2])
        turns = sbuf(nc, memory, "turns", [P, 2, NT, ROT // 2])
        turns_i = sbuf(nc, memory, "turns_int", [P, 2, NT, ROT // 2], I32)
        sc = sbuf(nc, memory, "sin_cos", [P, 2, NT, ROT // 2])
        rot = sbuf(nc, memory, "rotated", [P, 4, NH, ROT // 2])
        qk_t = sbuf(nc, memory, "qk_t", [P, NH // 2, T])
        scores = sbuf(nc, memory, "scores", [P, 2, GROUPS, T])
        probs_sb = sbuf(nc, memory, "probs_t", [P, 2, 2 * GROUPS, P])
        top = sbuf(nc, memory, "score_max", [P, 2, len(work)])
        den = sbuf(nc, memory, "den", [P, 2, len(work)])
        out = sbuf(nc, memory, "attn_rows", [P, NT, SLOTS * HD])
        TWO_PI = 2 * math.pi
        p1 = 6.28125
        p2 = float(np.float32(np.floor((TWO_PI - p1) * 2 ** 20) / 2 ** 20))
        p3 = TWO_PI - p1 - p2

        with nc.Block() as block:
            @block.sync
            def _(sp):
                sp.dma_start(S["w_rwkv_out"][:, :, :], S["dram"]["w_rwkv_out"].rearrange("(k p) n -> p k n", p=P)).then_inc(merge_in, 16)
                sp.dma_start(S["w_attn_out"][:, :, :], S["dram"]["w_attn_out"].rearrange("(k p) n -> p k n", p=P)).then_inc(merge_in, 16)
                sp.dma_start(S["w_out"][:, :, :], S["dram"]["w_out"].rearrange("(k p) n -> p k n", p=P)).then_inc(merge_in, 16)
                sp.wait_ge(merge_in, 48)

            @block.scalar
            def _(act):
                step = chain(act, act_step)
                nc.scalar.activation(sq[:, :, :], qkv[:, :, 0:2 * AC], ACT.Square).then_inc(squared, 1)
                act.wait_ge(angles, 1)
                nc.scalar.activation(sc[:, :, :, :], ang[:, :, :, :], ACT.Sin).then_inc(sines, 1)
                act.wait_ge(mean_sq, 1)
                nc.scalar.activation(ss[:, :, :], ss[:, :, :], ACT.Sqrt).then_inc(root_done, 1)
                for a in range(NT):
                    act.wait_ge(transposed, 3 * (a + 1))
                    for b in range(3):
                        last = nc.scalar.activation(qk_t[:, 4 * b:4 * b + 4, a * P:(a + 1) * P],
                                                    PS[:, 3 * a + b, :].rearrange("p (c t) -> p c t", t=P), ACT.Copy)
                    last.then_inc(copied, 1)
                for n, (s, a) in enumerate(work):
                    act.wait_ge(max_done, n + 1)
                    nc.scalar.activation(scores[:, n % 2, :, :], scores[:, n % 2, :, :], ACT.Exp, scale=scale,
                                         bias=top[:, 1, n:n + 1], accum_out=den[:, 0, n:n + 1]).then_inc(exp_done, 1)
                    act.wait_ge(probs_t, n + 1)
                    nc.scalar.activation(probs_sb[:, n % 2, 0:4, :],
                                         PS[:, 4 + n % 2, :].rearrange("p (c t) -> p c t", t=P),
                                         ACT.Copy).then_inc(probs_copied_act, 1)
                act.wait_ge(out_t, 1)
                nc.scalar.activation(S["attn_cols"][:, :, :], PS[:, 0, :].rearrange("p (c t) -> p c t", t=T), ACT.Copy)

            @block.vector
            def _(dve):
                step = chain(dve, dve_step)
                step(nc.vector.tensor_copy(pos[:, :], W["positions"]))
                for a in range(NT):
                    nc.vector.tensor_scalar(ang[:, 0, a, :], C["inv_freq"], pos[:, a:a + 1], None, ALU.mult)
                    last = nc.vector.tensor_scalar(ang[:, 1, a, :], C["inv_freq"], pos[:, a:a + 1], None, ALU.mult)
                step(last)
                step(nc.vector.tensor_scalar(turns[:, 0], ang[:, 0], 1 / TWO_PI, None, ALU.mult))
                step(nc.vector.tensor_scalar(turns[:, 1], ang[:, 1], 1 / TWO_PI, 0.25, ALU.mult, ALU.add))
                step(nc.vector.tensor_copy(turns_i[:, :, :, :], turns[:, :, :, :]))
                step(nc.vector.tensor_copy(turns[:, :, :, :], turns_i[:, :, :, :]))
                for part in (p1, p2, p3):
                    step(nc.vector.scalar_tensor_tensor(ang[:, :, :, :], turns[:, :, :, :], -part, ang[:, :, :, :],
                                                        ALU.mult, ALU.add))
                step(nc.vector.tensor_scalar(ang[:, 1], ang[:, 1], math.pi / 2, None, ALU.add))
                for above, by in ((math.pi, -TWO_PI), (-math.pi, TWO_PI)):
                    op = ALU.is_gt if above > 0 else ALU.is_lt
                    step(nc.vector.tensor_scalar(turns[:, :, :, :], ang[:, :, :, :], above, by, op, ALU.mult))
                    step(nc.vector.tensor_tensor(ang[:, :, :, :], ang[:, :, :, :], turns[:, :, :, :], ALU.add))
                nc.vector.tensor_scalar(ang[:, :, :, :], ang[:, :, :, :], 3.1415925, -3.1415925, ALU.min,
                                        ALU.max).then_inc(angles, 1)
                dve.wait_ge(squared, 1)
                for a in range(NT):
                    last = nc.vector.tensor_reduce(ss[:, a, :], sq[:, a, :].rearrange("p (h d) -> p h d", d=HD), X,
                                                   ALU.add)
                step(last)
                nc.vector.tensor_scalar(ss[:, :, :], ss[:, :, :], 1.0 / HD, NORM_EPS, ALU.mult,
                                        ALU.add).then_inc(mean_sq, 1)
                dve.wait_ge(root_done, 1)
                step(nc.vector.reciprocal(ss[:, :, :], ss[:, :, :]))
                dve.wait_ge(sines, 1)
                for a in range(NT):
                    v = qkv[:, a, 0:2 * AC].rearrange("p (h d) -> p h d", d=HD)
                    step(nc.vector.tensor_tensor(v, v, ss[:, a, :].unsqueeze(2).to_broadcast([P, NH, HD]), ALU.mult))
                    for i, g in enumerate((W["q_norm_g"], W["k_norm_g"])):
                        part = v[:, i * AH:(i + 1) * AH, :]
                        last = nc.vector.tensor_tensor(part, part, g.unsqueeze(1).to_broadcast([P, AH, HD]), ALU.mult)
                    step(last)
                    t1, t2 = v[:, :, 0:ROT // 2], v[:, :, ROT // 2:ROT]
                    sin = sc[:, 0, a, :].unsqueeze(1).to_broadcast([P, NH, ROT // 2])
                    cos = sc[:, 1, a, :].unsqueeze(1).to_broadcast([P, NH, ROT // 2])
                    for i, (x1, f) in enumerate(((t1, cos), (t2, sin), (t2, cos), (t1, sin))):
                        last = nc.vector.tensor_tensor(rot[:, i, :, :], x1, f, ALU.mult)
                    step(last)
                    nc.vector.tensor_tensor(t1, rot[:, 0, :, :], rot[:, 1, :, :], ALU.subtract)
                    nc.vector.tensor_tensor(t2, rot[:, 2, :, :], rot[:, 3, :, :], ALU.add).then_inc(normed, 1)
                    dve.wait_ge(normed, a + 1)
                def finish(n):
                    s, a = work[n]
                    dve.wait_ge(probs_t, n + 1)
                    nc.vector.tensor_copy(probs_sb[:, n % 2, 4:6, :],
                                          PS[:, 6, 2 * P * (n % 2):2 * P * (n % 2 + 1)].rearrange("p (c t) -> p c t", t=P)
                                          ).then_inc(probs_copied_dve, 1)
                    step(nc.vector.reciprocal(den[:, 1, n:n + 1], den[:, 0, n:n + 1]))
                    dve.wait_ge(out_done, n + 1)
                    nc.vector.tensor_scalar(out[:, a, s * HD:(s + 1) * HD], PS[:, 7, (n % 2) * HD:(n % 2 + 1) * HD],
                                            den[:, 1, n:n + 1], None, ALU.mult).then_inc(out_scaled, 1)

                for n, (s, a) in enumerate(work):
                    dve.wait_ge(scores_done, n + 1)
                    src = PS[:, 2 * (n % 2):2 * (n % 2) + 2, :].rearrange("p b (g t) -> p (b g) t", t=T)[:, 0:GROUPS, :]
                    if n >= 2:
                        dve.wait_ge(probs_t, n - 1)
                    step(nc.vector.tensor_tensor(scores[:, n % 2, :, :], src, C["band"][:, a], ALU.add))
                    step(nc.vector.tensor_reduce(top[:, 0, n:n + 1], scores[:, n % 2, :, :].rearrange("p g t -> p (g t)"),
                                                 X, ALU.max))
                    nc.vector.tensor_scalar(top[:, 1, n:n + 1], top[:, 0, n:n + 1], -scale, None,
                                            ALU.mult).then_inc(max_done, 1)
                    if n:
                        finish(n - 1)
                finish(len(work) - 1)

            @block.tensor
            def _(pe):
                for a in range(NT):
                    pe.wait_ge(normed, a + 1)
                    for b in range(3):
                        for c in range(4):
                            last = nc.tensor.transpose(PS[:, 3 * a + b, c * P:(c + 1) * P],
                                                       qkv[:, a, (4 * b + c) * P:(4 * b + c + 1) * P], C["ident"])
                        last.then_inc(transposed, 1)

                def score(n):
                    s, a = work[n]
                    if n == 0:
                        pe.wait_ge(copied, NT)
                    if n >= 2:
                        pe.wait_ge(max_done, n - 1)
                    for g in range(GROUPS):
                        h = g * SLOTS + s
                        rows = slice((h % 2) * HD, (h % 2 + 1) * HD)
                        last = nc.tensor.matmul(PS[:, 2 * (n % 2) + g // 2, (g % 2) * T:(g % 2 + 1) * T],
                                                qk_t[rows, h // 2, a * P:(a + 1) * P], qk_t[rows, AH // 2 + h // 2, :],
                                                start=True, stop=True)
                    last.then_inc(scores_done, 1)

                score(0)
                for n, (s, a) in enumerate(work):
                    if n + 1 < len(work):
                        score(n + 1)
                    pe.wait_ge(exp_done, n + 1)
                    if n >= 2:
                        pe.wait_ge(probs_copied_act, n - 1)
                        pe.wait_ge(probs_copied_dve, n - 1)
                    for i in range(2 * GROUPS):
                        to = (PS[:, 4 + n % 2, i * P:(i + 1) * P] if i < 4 else
                              PS[:, 6, (2 * (n % 2) + i - 4) * P:(2 * (n % 2) + i - 3) * P])
                        last = nc.tensor.transpose(to, scores[:, n % 2, i // 2, (i % 2) * P:(i % 2 + 1) * P], C["ident"])
                    last.then_inc(probs_t, 1)
                    pe.wait_ge(probs_copied_act, n + 1)
                    pe.wait_ge(probs_copied_dve, n + 1)
                    if n:
                        pe.wait_ge(out_scaled, n)
                    for i in range(2 * GROUPS):
                        h = (i // 2) * SLOTS + s
                        c0 = 2 * AC + h * HD
                        last = nc.tensor.matmul(PS[:, 7, (n % 2) * HD:(n % 2 + 1) * HD], probs_sb[:, n % 2, i, :],
                                                qkv[:, i % 2, c0:c0 + HD], start=(i == 0), stop=(i == 2 * GROUPS - 1))
                    last.then_inc(out_done, 1)
                pe.wait_ge(out_scaled, len(work))
                for a in range(NT):
                    for c in range(2):
                        last = nc.tensor.transpose(PS[:, 0, c * T + a * P:c * T + (a + 1) * P],
                                                   out[:, a, c * P:(c + 1) * P], C["ident"])
                last.then_inc(out_t, 1)


def merge(nc, S):
    PS, R = S["psum"], S["rwkv"]
    gates = S["gates"]
    with phase(nc, "both_done gated added x_done") as (memory, both_done, gated, added, x_done):
        merged = sbuf(nc, memory, "merged", [P, KD, T])
        other = sbuf(nc, memory, "merged_attn", [P, KD, T])

        with nc.Block() as block:
            @block.tensor
            def _(pe):
                for k in range(KD):
                    if k >= 4:
                        pe.wait_ge(added, k - 3)
                    s = slice(k * P, (k + 1) * P)
                    for c in range(RT):
                        nc.tensor.matmul(PS[:, k % 4, 0:T], S["w_rwkv_out"][:, c, s], R["y"][:, c, :],
                                         start=(c == 0), stop=(c == RT - 1))
                    for c in range(2):
                        last = nc.tensor.matmul(PS[:, k % 4, T:2 * T], S["w_attn_out"][:, c, s],
                                                S["attn_cols"][:, c, :], start=(c == 0), stop=(c == 1))
                    last.then_inc(both_done, 1)
                pe.wait_ge(added, KD)
                for a in range(NT):
                    for h in range(2):
                        for k in range(KD):
                            last = nc.tensor.matmul(PS[:, 4 + 2 * a + h, :], merged[:, k, a * P:(a + 1) * P],
                                                    S["w_out"][:, k, h * BANK:(h + 1) * BANK],
                                                    start=(k == 0), stop=(k == KD - 1))
                        last.then_inc(x_done, 1)

            @block.vector
            def _(dve):
                for k in range(KD):
                    dve.wait_ge(both_done, k + 1)
                    nc.vector.tensor_tensor(merged[:, k, :], PS[:, k % 4, 0:T], gates[:, k, :], ALU.mult)
                    nc.vector.tensor_tensor(other[:, k, :], PS[:, k % 4, T:2 * T], gates[:, KD + k, :],
                                            ALU.mult).then_inc(gated, 1)
                    dve.wait_ge(gated, k + 1)
                    nc.vector.tensor_tensor(merged[:, k, :], merged[:, k, :], other[:, k, :],
                                            ALU.add).then_inc(added, 1)
                for a in range(NT):
                    for h in range(2):
                        dve.wait_ge(x_done, 2 * a + h + 1)
                        o = S["x"][:, a, h * BANK:(h + 1) * BANK]
                        nc.vector.tensor_tensor(o, o, PS[:, 4 + 2 * a + h, :], ALU.add)



def route(nc, S):
    PS, C, W = S["psum"], S["const"], S["weights"]
    N = MOE_GROUPS + EXPERTS
    with phase(nc, "dve_step logits_done exp_ready exp_done exp2_ready exp2_done combined spread spread_out") as (
            memory, dve_step, logits_done, exp_ready, exp_done, exp2_ready, exp2_done, combined, spread, spread_out):
        logits = sbuf(nc, memory, "logits", [P, NT, N])
        grp = sbuf(nc, memory, "group_logits", [P, NT, 8])
        best = sbuf(nc, memory, "group_best", [P, NT, 8])
        index = sbuf(nc, memory, "group_index", [P, NT, 8], U32)
        chosen = sbuf(nc, memory, "group_chosen", [P, NT, 8])
        ex = sbuf(nc, memory, "group_exp", [P, NT, 8])
        gp = sbuf(nc, memory, "group_prob", [P, NT, 4])
        mine = sbuf(nc, memory, "expert_logits", [P, NT, EXPERTS])
        hot = sbuf(nc, memory, "expert_hot", [P, NT, EXPERTS])
        comb = sbuf(nc, memory, "combine", [P, NT, EXPERTS])
        top = sbuf(nc, memory, "expert_top", [P, NT, 8])
        ti = sbuf(nc, memory, "expert_top_i", [P, NT, 8], U32)
        tf = sbuf(nc, memory, "expert_top_f", [P, NT, 8])
        with nc.Block() as block:
            @block.tensor
            def _(pe):
                for a in range(NT):
                    for k in range(KD):
                        last = nc.tensor.matmul(PS[:, a, 0:N], S["h_cols"][:, k, a * P:(a + 1) * P],
                                                W["router"][:, k, :], start=(k == 0), stop=(k == KD - 1))
                last.then_inc(logits_done, 1)
                pe.wait_ge(combined, 1)
                for e in range(0, EXPERTS, 2):
                    b = (e // 2) % BANKS
                    if e // 2 >= BANKS:
                        pe.wait_ge(spread_out, e // 2 - BANKS + 1)
                    for i in range(2):
                        for a in range(NT):
                            last = nc.tensor.matmul(PS[:, b, i * T + a * P:i * T + (a + 1) * P],
                                                    comb[:, a, e + i:e + i + 1].to_broadcast([P, P]), C["ident"],
                                                    start=True, stop=True)
                    last.then_inc(spread, 1)

            @block.scalar
            def _(act):
                act.wait_ge(exp_ready, 1)
                for a in range(NT):
                    last = nc.scalar.activation(ex[:, a, 0:4], grp[:, a, 0:4], ACT.Exp, bias=gp[:, a, 0:1],
                                                accum_out=gp[:, a, 1:2])
                last.then_inc(exp_done, 1)
                act.wait_ge(exp2_ready, 1)
                nc.scalar.activation(gp[:, :, 2:3], gp[:, :, 2:3], ACT.Exp).then_inc(exp2_done, 1)
                for n in range(EXPERTS // 2):
                    act.wait_ge(spread, n + 1)
                    nc.scalar.activation(S["spread"][:, 2 * n:2 * n + 2, :],
                                         PS[:, n % BANKS, :].rearrange("p (e t) -> p e t", t=T),
                                         ACT.Copy).then_inc(spread_out, 1)

            @block.vector
            def _(dve):
                step = chain(dve, dve_step)
                step(nc.vector.memset(grp[:, :, :], NEG))
                dve.wait_ge(logits_done, 1)
                for a in range(NT):
                    last = nc.vector.tensor_tensor(logits[:, a, :], PS[:, a, 0:N], W["router_bias"], ALU.add)
                step(last)
                step(nc.vector.tensor_copy(grp[:, :, 0:4], logits[:, :, 0:4]))
                for a in range(NT):
                    step(nc.vector.max(best[:, a, :], grp[:, a, :]))
                    step(nc.vector.max_index(index[:, a, :], best[:, a, :], grp[:, a, :]))
                step(nc.vector.tensor_copy(chosen[:, :, :], index[:, :, :]))
                nc.vector.tensor_scalar(gp[:, :, 0:1], best[:, :, 0:1], -1.0, None, ALU.mult).then_inc(exp_ready, 1)
                for a in range(NT):
                    step(nc.vector.tensor_scalar(hot[:, a, 0:4], C["iota"][:, 0:4], chosen[:, a, 0:1], NEG,
                                                 ALU.not_equal, ALU.mult))
                    step(nc.vector.tensor_tensor(
                        mine[:, a, :].rearrange("p (g e) -> p g e", e=PER_GROUP),
                        logits[:, a, 4:N].rearrange("p (g e) -> p g e", e=PER_GROUP),
                        hot[:, a, 0:4].unsqueeze(2).to_broadcast([P, 4, PER_GROUP]), ALU.add))
                    step(nc.vector.max(top[:, a, :], mine[:, a, :]))
                    step(nc.vector.max_index(ti[:, a, :], top[:, a, :], mine[:, a, :]))
                step(nc.vector.tensor_copy(tf[:, :, :], ti[:, :, :]))
                dve.wait_ge(exp_done, 1)
                nc.vector.tensor_tensor(gp[:, :, 2:3], top[:, :, 1:2], top[:, :, 0:1],
                                        ALU.subtract).then_inc(exp2_ready, 1)
                dve.wait_ge(exp2_done, 1)
                step(nc.vector.tensor_scalar(gp[:, :, 3:4], gp[:, :, 2:3], 1.0, None, ALU.add))
                step(nc.vector.tensor_tensor(gp[:, :, 3:4], gp[:, :, 3:4], gp[:, :, 1:2], ALU.mult))
                step(nc.vector.reciprocal(gp[:, :, 3:4], gp[:, :, 3:4]))
                step(nc.vector.tensor_tensor(gp[:, :, 2:3], gp[:, :, 2:3], gp[:, :, 3:4], ALU.mult))
                for a in range(NT):
                    nc.vector.tensor_scalar(comb[:, a, :], C["iota"][:, 0:EXPERTS], tf[:, a, 0:1], gp[:, a, 3:4],
                                            ALU.is_equal, ALU.mult)
                    step(nc.vector.tensor_scalar(hot[:, a, :], C["iota"][:, 0:EXPERTS], tf[:, a, 1:2], gp[:, a, 2:3],
                                                 ALU.is_equal, ALU.mult))
                    last = nc.vector.tensor_tensor(comb[:, a, :], comb[:, a, :], hot[:, a, :], ALU.add)
                last.then_inc(combined, 1)


def experts(nc, S):
    PS = S["psum"]
    FC = DE // P
    wg, wu, wd = (S["dram"][n] for n in ("w_gate", "w_up", "w_down"))

    with phase(nc, "gu_in0 gu_in1 down_in0 down_in1 zeroed cleared gu_done silu_done act_up act_done down_done") as (
            memory, gu_in0, gu_in1, down_in0, down_in1, zeroed, cleared, gu_done, silu_done, act_up, act_done,
            down_done):
        w_gu = sbuf(nc, memory, "w_gate_up", [P, 2, 2, KD, DE])
        w_dn = sbuf(nc, memory, "w_down_e", [P, 2, FC, D])
        zero = sbuf(nc, memory, "zeros", [P, BANK])
        silu = sbuf(nc, memory, "silu", [P, 2, FC, T])
        hid = sbuf(nc, memory, "hidden", [P, 2, FC, T])
        gu_in, down_in = (gu_in0, gu_in1), (down_in0, down_in1)
        h = S["h_cols"]

        def expert(w, e, chunks):
            return w[bass.ds(e, 1), :, :].rearrange("o (k p) n -> p (o k) n", p=P) if not isinstance(e, int) else \
                w[e].rearrange("(k p) n -> p k n", p=P)

        with nc.Block() as block:
            @block.sync
            def _(sp):
                def load(e, b):
                    sp.dma_start(w_gu[:, b, 0, :, :], expert(wg, e, KD)).then_inc(gu_in[b], 16)
                    sp.dma_start(w_gu[:, b, 1, :, :], expert(wu, e, KD)).then_inc(gu_in[b], 16)
                for b in range(2):
                    load(b, b)
                    sp.dma_start(w_dn[:, b, :, :], expert(wd, b, FC)).then_inc(down_in[b], 16)
                with sp.Fori(1, EXPERTS // 2) as i:
                    for b in range(2):
                        sp.wait_ge(gu_done, (i * 2 + (b - 1)) * 2)
                        load(i * 2 + b, b)
                        sp.wait_ge(down_done, i * 2 + (b - 1))
                        sp.dma_start(w_dn[:, b, :, :], expert(wd, i * 2 + b, FC)).then_inc(down_in[b], 16)

            @block.tensor
            def _(pe):
                pe.wait_ge(zeroed, 1)
                for b in range(4):
                    last = nc.tensor.matmul(PS[:, 4 + b, :], zero[:, 0:P], zero[:, :], start=True, stop=False,
                                            skip_group_check=True)

                def gate_up(b):
                    for f in range(FC):
                        for j in range(2):
                            for k in range(KD):
                                last = nc.tensor.matmul(PS[:, f, j * T:(j + 1) * T],
                                                        w_gu[:, b, j, k, f * P:(f + 1) * P], h[:, k, :],
                                                        start=(k == 0), stop=(k == KD - 1))
                        if f % 2:
                            last.then_inc(gu_done, 1)

                def down(b):
                    for a in range(NT):
                        for n in range(2):
                            for f in range(FC):
                                last = nc.tensor.matmul(PS[:, 4 + 2 * a + n, :], hid[:, b, f, a * P:(a + 1) * P],
                                                        w_dn[:, b, f, n * BANK:(n + 1) * BANK], start=False,
                                                        stop=False, skip_group_check=True)
                    last.then_inc(down_done, 1)

                pe.wait_ge(gu_in[0], 32)
                gate_up(0)
                with pe.Fori(0, EXPERTS // 2 - 1) as i:
                    pe.wait_ge(gu_in[1], i * 32 + 32)
                    pe.wait_ge(act_up, i * 4 + 2)
                    gate_up(1)
                    pe.wait_ge(down_in[0], i * 16 + 16)
                    pe.wait_ge(act_done, i * 4 + 2)
                    down(0)
                    pe.wait_ge(gu_in[0], i * 32 + 64)
                    pe.wait_ge(act_up, i * 4 + 4)
                    gate_up(0)
                    pe.wait_ge(down_in[1], i * 16 + 16)
                    pe.wait_ge(act_done, i * 4 + 4)
                    down(1)
                pe.wait_ge(gu_in[1], EXPERTS // 2 * 32)
                pe.wait_ge(act_up, 2 * EXPERTS - 2)
                gate_up(1)
                pe.wait_ge(down_in[0], EXPERTS // 2 * 16)
                pe.wait_ge(act_done, 2 * EXPERTS - 2)
                down(0)
                pe.wait_ge(down_in[1], EXPERTS // 2 * 16)
                pe.wait_ge(act_done, 2 * EXPERTS)
                down(1)

            @block.scalar
            def _(act):
                with act.Fori(0, EXPERTS // 2) as i:
                    for b in range(2):
                        for half in range(2):
                            n = i * 4 + (2 * b + half)
                            act.wait_ge(gu_done, n + 1)
                            nc.scalar.activation(silu[:, b, 2 * half:2 * half + 2, :],
                                                 PS[:, 2 * half:2 * half + 2, 0:T], ACT.Silu).then_inc(silu_done, 1)

            @block.vector
            def _(dve):
                nc.vector.memset(zero[:, :], 0.0).then_inc(zeroed, 1)
                with dve.Fori(0, EXPERTS // 2) as i:
                    for b in range(2):
                        for half in range(2):
                            n = i * 4 + (2 * b + half)
                            s = slice(2 * half, 2 * half + 2)
                            dve.wait_ge(silu_done, n + 1)
                            nc.vector.tensor_tensor(silu[:, b, s, :], silu[:, b, s, :], PS[:, s, T:2 * T],
                                                    ALU.mult).then_inc(act_up, 1)
                            dve.wait_ge(act_up, n + 1)
                            share = S["spread"][:, bass.ds(i * 2 + b, 1), :].to_broadcast([P, 2, T])
                            nc.vector.tensor_tensor(hid[:, b, s, :], silu[:, b, s, :], share,
                                                    ALU.mult).then_inc(act_done, 1)
                dve.wait_ge(down_done, EXPERTS)
                for a in range(NT):
                    for n in range(2):
                        o = S["x"][:, a, n * BANK:(n + 1) * BANK]
                        nc.vector.tensor_tensor(o, o, PS[:, 4 + 2 * a + n, :], ALU.add)



def differential(nc, S):
    PS, C, L = S["psum"], S["const"], S["layer"]
    scale = HD ** -0.5
    work = [(h, a) for h in range(DH) for a in range(NT)]
    with phase(nc, "dve_step act_step lam_in lam_exp scores_done masked max_done exp_done mixed_done probs_t "
                   "probs_copied out_done squared root_done finished") as (
            memory, dve_step, act_step, lam_in, lam_exp, scores_done, masked, max_done, exp_done, mixed_done, probs_t,
            probs_copied, out_done, squared, root_done, finished):
        prod = sbuf(nc, memory, "lam_products", [P, 2, HD])
        lam = sbuf(nc, memory, "lam", [P, 4])
        sc = sbuf(nc, memory, "diff_scores", [P, 2, 2, T])
        top = sbuf(nc, memory, "diff_max", [P, 2, len(work), 2])
        den = sbuf(nc, memory, "diff_den", [P, 2, len(work), 2])
        pt = sbuf(nc, memory, "diff_probs_t", [P, 2, NT, P])
        o = sbuf(nc, memory, "diff_out", [P, 2, P])
        sq = sbuf(nc, memory, "diff_sq", [P, 2, P])
        ss = sbuf(nc, memory, "diff_ss", [P, len(work)])
        eps = sbuf(nc, memory, "diff_eps", [P, 1])

        with nc.Block() as block:
            @block.tensor
            def _(pe):
                def score(n):
                    h, a = work[n]
                    if n >= 2:
                        pe.wait_ge(masked, n - 1)
                    for m in range(2):
                        rows = slice(m * HD, (m + 1) * HD)
                        last = nc.tensor.matmul(PS[:, 2 * (n % 2) + m, 0:(a + 1) * P],
                                                S["dqk"][rows, h, a * P:(a + 1) * P],
                                                S["dqk"][rows, DH + h, 0:(a + 1) * P], start=True, stop=True)
                    last.then_inc(scores_done, 1)

                score(0)
                for n, (h, a) in enumerate(work):
                    if n + 1 < len(work):
                        score(n + 1)
                    pe.wait_ge(mixed_done, n + 1)
                    if n >= 2:
                        pe.wait_ge(probs_copied, n - 1)
                    for i in range(a + 1):
                        last = nc.tensor.transpose(PS[:, 4 + n % 2, i * P:(i + 1) * P],
                                                   sc[:, n % 2, 0, i * P:(i + 1) * P], C["ident"])
                    last.then_inc(probs_t, 1)
                    pe.wait_ge(probs_copied, n + 1)
                    if n >= 2:
                        pe.wait_ge(finished, n - 1)
                    for i in range(a + 1):
                        last = nc.tensor.matmul(PS[:, 6 + n % 2, 0:P], pt[:, n % 2, i, :],
                                                S["dv"][:, i, h * P:(h + 1) * P], start=(i == 0), stop=(i == a))
                    last.then_inc(out_done, 1)

            @block.scalar
            def _(act):
                step = chain(act, act_step)
                act.wait_ge(lam_in, 1)
                nc.scalar.activation(lam[:, 0:2], lam[:, 0:2], ACT.Exp).then_inc(lam_exp, 1)
                for n, (h, a) in enumerate(work):
                    act.wait_ge(max_done, n + 1)
                    for m in range(2):
                        last = nc.scalar.activation(sc[:, n % 2, m, 0:(a + 1) * P], sc[:, n % 2, m, 0:(a + 1) * P],
                                                    ACT.Exp, scale=scale, bias=top[:, 1, n, m:m + 1],
                                                    accum_out=den[:, 0, n, m:m + 1])
                    last.then_inc(exp_done, 1)
                    act.wait_ge(probs_t, n + 1)
                    nc.scalar.activation(pt[:, n % 2, 0:a + 1, :],
                                         PS[:, 4 + n % 2, 0:(a + 1) * P].rearrange("p (i q) -> p i q", q=P),
                                         ACT.Copy).then_inc(probs_copied, 1)
                act.wait_ge(squared, 1)
                nc.scalar.activation(ss[:, :], ss[:, :], ACT.Sqrt, scale=1.0 / P, bias=eps[:, 0:1]).then_inc(root_done, 1)

            @block.vector
            def _(dve):
                step = chain(dve, dve_step)
                step(nc.vector.memset(eps[:, :], RMS_EPS))
                for m in range(2):
                    step(nc.vector.tensor_tensor(prod[:, m, :], L["lam"][:, 2 * m, :], L["lam"][:, 2 * m + 1, :], ALU.mult))
                nc.vector.tensor_reduce(lam[:, 0:2], prod[:, :, :], X, ALU.add).then_inc(lam_in, 1)
                dve.wait_ge(lam_exp, 1)
                step(nc.vector.tensor_tensor(lam[:, 2:3], lam[:, 1:2], lam[:, 0:1], ALU.subtract))
                step(nc.vector.tensor_tensor(lam[:, 3:4], lam[:, 2:3], L["lambda_init"][:, 0:1], ALU.subtract))

                def finish(n):
                    h, a = work[n]
                    dve.wait_ge(out_done, n + 1)
                    to = S["mixed"][:, a, h * P:(h + 1) * P]
                    step(nc.vector.tensor_copy(to, PS[:, 6 + n % 2, 0:P]))
                    step(nc.vector.tensor_tensor(sq[:, n % 2, :], to, to, ALU.mult))
                    nc.vector.tensor_reduce(ss[:, n:n + 1], sq[:, n % 2, :], X, ALU.add).then_inc(finished, 1)

                for n, (h, a) in enumerate(work):
                    w = (a + 1) * P
                    dve.wait_ge(scores_done, n + 1)
                    if n >= 2:
                        dve.wait_ge(probs_t, n - 1)
                    slope = 2.0 ** (-8.0 * (h + 1) / DH)
                    for m in range(2):
                        last = nc.vector.scalar_tensor_tensor(sc[:, n % 2, m, 0:w], C["dist"][:, a, 0:w],
                                                              -slope / scale, PS[:, 2 * (n % 2) + m, 0:w],
                                                              ALU.mult, ALU.add)
                    last.then_inc(masked, 1)
                    dve.wait_ge(masked, n + 1)
                    step(nc.vector.tensor_reduce(top[:, 0, n, :], sc[:, n % 2, :, 0:w], X, ALU.max))
                    nc.vector.tensor_scalar(top[:, 1, n, :], top[:, 0, n, :], -scale, None, ALU.mult).then_inc(max_done, 1)
                    if n:
                        finish(n - 1)
                    dve.wait_ge(exp_done, n + 1)
                    step(nc.vector.reciprocal(den[:, 1, n, :], den[:, 0, n, :]))
                    step(nc.vector.tensor_tensor(den[:, 1, n, 1:2], den[:, 1, n, 1:2], lam[:, 3:4], ALU.mult))
                    step(nc.vector.tensor_scalar(sc[:, n % 2, 0, 0:w], sc[:, n % 2, 0, 0:w], den[:, 1, n, 0:1], None, ALU.mult))
                    nc.vector.scalar_tensor_tensor(sc[:, n % 2, 0, 0:w], sc[:, n % 2, 1, 0:w], den[:, 1, n, 1:2],
                                                   sc[:, n % 2, 0, 0:w], ALU.mult, ALU.add).then_inc(mixed_done, 1)
                finish(len(work) - 1)
                dve.wait_ge(finished, len(work))
                nc.vector.tensor_scalar(ss[:, :], ss[:, :], 1.0, None, ALU.mult).then_inc(squared, 1)
                dve.wait_ge(root_done, 1)
                step(nc.vector.reciprocal(ss[:, :], ss[:, :]))
                for n, (h, a) in enumerate(work):
                    to = S["mixed"][:, a, h * P:(h + 1) * P]
                    last = nc.vector.scalar_tensor_tensor(to, to, ss[:, n:n + 1], L["subln_g"], ALU.mult, ALU.mult)
                step(last)
                nc.vector.tensor_scalar(S["mixed"][:, :, 0:DH * P], S["mixed"][:, :, 0:DH * P],
                                        L["lambda_init"][:, 1:2], None, ALU.mult)


def stick_breaking(nc, S):
    PS, C = S["psum"], S["const"]
    scale = HD ** -0.5
    B3 = 3 * P
    with phase(nc, "dve_step act_step z_done abs_done log_done fail_done later_done logw_done w_exp w_done out_done") as (
            memory, dve_step, act_step, z_done, abs_done, log_done, fail_done, later_done, logw_done, w_exp, w_done, out_done):
        z = sbuf(nc, memory, "sb_abs", [P, 2, B3])
        l = sbuf(nc, memory, "sb_log", [P, 2, B3])
        fail = sbuf(nc, memory, "sb_fail", [P, 2, B3])
        lw = sbuf(nc, memory, "sb_logw", [P, 2, B3])

        def diagonal(ap, n):
            return ap[:, n % 2, :].rearrange("p (b q) -> p b q", q=P)[:, 0:3:2, :]

        with nc.Block() as block:
            @block.tensor
            def _(pe):
                def logits(h):
                    rows = slice((h % 2) * HD, (h % 2 + 1) * HD)
                    c = h // 2
                    if h >= 2:
                        pe.wait_ge(logw_done, h - 1)
                    nc.tensor.matmul(PS[:, h % 2, 0:T], S["sqk"][rows, SH // 2 + c, 0:P], S["sqk"][rows, c, :],
                                     start=True, stop=True)
                    nc.tensor.matmul(PS[:, h % 2, T:B3], S["sqk"][rows, SH // 2 + c, P:T], S["sqk"][rows, c, P:T],
                                     start=True, stop=True).then_inc(z_done, 1)

                def times_v(h):
                    pe.wait_ge(w_done, h + 1)
                    s = slice(h * HD, (h + 1) * HD)
                    nc.tensor.matmul(PS[:, 4, s], lw[:, h % 2, 0:P], S["sv"][:, 0, s], start=True, stop=True)
                    nc.tensor.matmul(PS[:, 5, s], lw[:, h % 2, P:T], S["sv"][:, 0, s], start=True, stop=False)
                    nc.tensor.matmul(PS[:, 5, s], lw[:, h % 2, T:B3], S["sv"][:, 1, s], start=False,
                                     stop=True).then_inc(out_done, 1)

                logits(0)
                for h in range(SH):
                    if h + 1 < SH:
                        logits(h + 1)
                    pe.wait_ge(fail_done, h + 1)
                    o = PS[:, 2 + h % 2, :]
                    nc.tensor.matmul(o[:, 0:P], C["p>q"], fail[:, h % 2, 0:P], start=True, stop=True)
                    nc.tensor.matmul(o[:, P:T], C["p>q"], fail[:, h % 2, P:T], start=True, stop=False)
                    nc.tensor.matmul(o[:, P:T], C["ones"], fail[:, h % 2, T:B3], start=False, stop=True)
                    nc.tensor.matmul(o[:, T:B3], C["p>q"], fail[:, h % 2, T:B3], start=True,
                                     stop=True).then_inc(later_done, 1)
                    if h:
                        times_v(h - 1)
                times_v(SH - 1)

            @block.scalar
            def _(act):
                step = chain(act, act_step)
                for h in range(SH):
                    act.wait_ge(z_done, h + 1)
                    if h >= 2:
                        act.wait_ge(logw_done, h - 1)
                    step(nc.scalar.activation(z[:, h % 2, :], PS[:, h % 2, 0:B3], ACT.Abs))
                    step(nc.scalar.activation(z[:, h % 2, :], z[:, h % 2, :], ACT.Exp, scale=-scale))
                    nc.scalar.activation(l[:, h % 2, :], z[:, h % 2, :], ACT.Ln, bias=1.0).then_inc(log_done, 1)
                    if h:
                        act.wait_ge(logw_done, h)
                        nc.scalar.activation(lw[:, (h - 1) % 2, :], lw[:, (h - 1) % 2, :], ACT.Exp).then_inc(w_exp, 1)
                act.wait_ge(logw_done, SH)
                nc.scalar.activation(lw[:, (SH - 1) % 2, :], lw[:, (SH - 1) % 2, :], ACT.Exp).then_inc(w_exp, 1)
                act.wait_ge(out_done, SH)
                for a in range(NT):
                    nc.scalar.activation(S["mixed"][:, a, DH * P:D], PS[:, 4 + a, :], ACT.Copy)

            @block.vector
            def _(dve):
                step = chain(dve, dve_step)
                before = C["p<q"].unsqueeze(1).to_broadcast([P, 2, P])

                def weights(h):
                    dve.wait_ge(w_exp, h + 1)
                    nc.vector.tensor_tensor(diagonal(lw, h), diagonal(lw, h), before, ALU.mult).then_inc(w_done, 1)

                for h in range(SH):
                    zp = PS[:, h % 2, 0:B3]
                    dve.wait_ge(log_done, h + 1)
                    if h >= 2:
                        dve.wait_ge(later_done, h - 1)
                    step(nc.vector.tensor_scalar(fail[:, h % 2, :], zp, 0.0, scale, ALU.max, ALU.mult))
                    step(nc.vector.tensor_tensor(fail[:, h % 2, :], fail[:, h % 2, :], l[:, h % 2, :], ALU.add))
                    nc.vector.tensor_tensor(diagonal(fail, h), diagonal(fail, h), before, ALU.mult).then_inc(fail_done, 1)
                    if h >= 2:
                        dve.wait_ge(out_done, h - 1)
                    step(nc.vector.tensor_scalar(lw[:, h % 2, :], zp, 0.0, scale, ALU.min, ALU.mult))
                    step(nc.vector.tensor_tensor(lw[:, h % 2, :], lw[:, h % 2, :], l[:, h % 2, :], ALU.subtract))
                    dve.wait_ge(later_done, h + 1)
                    nc.vector.tensor_tensor(lw[:, h % 2, :], lw[:, h % 2, :], PS[:, 2 + h % 2, 0:B3],
                                            ALU.subtract).then_inc(logw_done, 1)
                    if h:
                        weights(h - 1)
                weights(SH - 1)


def layer_norm(dve, act, nc, step, act_step_done, rows, stats, psum_halves, g, b, ready, root_ready, root_done):
    for a in range(NT):
        for n in range(2):
            s = slice(n * BANK, (n + 1) * BANK)
            ready(a, n)
            step(nc.vector.scalar_tensor_tensor(rows[:, a, s], rows[:, a, s], ALPHA, psum_halves(a, n), ALU.mult, ALU.add))
            step(nc.vector.bn_stats(stats[:, a, 6 * n:6 * n + 6], rows[:, a, s]))
        step(nc.vector.bn_aggr(stats[:, a, 12:14], stats[:, a, 0:12]))
    nc.vector.tensor_scalar(stats[:, :, 14:15], stats[:, :, 13:14], LN_EPS, None, ALU.add).then_inc(root_ready, 1)
    dve.wait_ge(root_done, 1)
    step(nc.vector.reciprocal(stats[:, :, 15:16], stats[:, :, 14:15]))
    for a in range(NT):
        step(nc.vector.tensor_scalar(rows[:, a, :], rows[:, a, :], stats[:, a, 12:13], stats[:, a, 15:16], ALU.subtract,
                                     ALU.mult))
        step(nc.vector.tensor_tensor(rows[:, a, :], rows[:, a, :], g, ALU.mult))
        step(nc.vector.tensor_tensor(rows[:, a, :], rows[:, a, :], b, ALU.add))


def mix_out(nc, S, layer):
    PS, C, L = S["psum"], S["const"], S["layer"]
    with phase(nc, "dve_step weights_in transposed copied_dve copied_act products root_ready root_done") as (
            memory, dve_step, weights_in, transposed, copied_dve, copied_act, products, root_ready, root_done):
        w = sbuf(nc, memory, "w_o", [P, KD, D])
        cols = sbuf(nc, memory, "mixed_cols", [P, KD, T])
        stats = sbuf(nc, memory, "ln_stats", [P, NT, 16])
        src = row_at(S["dram"]["w_o_2"], layer).rearrange("(k p) n -> p k n", p=P)
        with nc.Block() as block:
            @block.sync
            def _(sp):
                sp.dma_start(w[:, :, :], src).then_inc(weights_in, 16)

            @block.tensor
            def _(pe):
                for k in range(KD):
                    for a in range(NT):
                        last = nc.tensor.transpose(PS[:, k // 2, (k % 2) * T + a * P:(k % 2) * T + (a + 1) * P],
                                                   S["mixed"][:, a, k * P:(k + 1) * P], C["ident"])
                    if k % 2:
                        last.then_inc(transposed, 1)
                pe.wait_ge(weights_in, 16)
                pe.wait_ge(copied_dve, 2)
                pe.wait_ge(copied_act, 2)
                for a in range(NT):
                    for n in range(2):
                        for k in range(KD):
                            last = nc.tensor.matmul(PS[:, 4 + 2 * a + n, :], cols[:, k, a * P:(a + 1) * P],
                                                    w[:, k, n * BANK:(n + 1) * BANK], start=(k == 0), stop=(k == KD - 1))
                        last.then_inc(products, 1)

            @block.scalar
            def _(act):
                for j in (1, 3):
                    act.wait_ge(transposed, j + 1)
                    nc.scalar.activation(cols[:, 2 * j:2 * j + 2, :], PS[:, j, :].rearrange("p (k t) -> p k t", t=T),
                                         ACT.Copy).then_inc(copied_act, 1)
                act.wait_ge(root_ready, 1)
                nc.scalar.activation(stats[:, :, 14:15], stats[:, :, 14:15], ACT.Sqrt).then_inc(root_done, 1)

            @block.vector
            def _(dve):
                step = chain(dve, dve_step)
                for j in (0, 2):
                    dve.wait_ge(transposed, j + 1)
                    nc.vector.tensor_copy(cols[:, 2 * j:2 * j + 2, :],
                                          PS[:, j, :].rearrange("p (k t) -> p k t", t=T)).then_inc(copied_dve, 1)
                layer_norm(dve, None, nc, step, None, S["x"], stats, lambda a, n: PS[:, 4 + 2 * a + n, :],
                           L["ln1_g"], L["ln1_b"], lambda a, n: dve.wait_ge(products, 2 * a + n + 1), root_ready, root_done)


def peer_select(nc, S):
    PS, C = S["psum"], S["const"]
    HP = 2 * PH
    with phase(nc, "keys_in dve_step scores_done scores_out exp_ready exp_done gates_done idx_t idx_out gates_t "
                   "gates_out") as (
            memory, keys_in, dve_step, scores_done, scores_out, exp_ready, exp_done, gates_done, idx_t, idx_out,
            gates_t, gates_out):
        keys = sbuf(nc, memory, "sub_keys_t", [P, HP, NKEYS])
        sc = sbuf(nc, memory, "key_scores", [P, HP, NKEYS])
        val = sbuf(nc, memory, "key_best", [P, HP, TOPK])
        idx = sbuf(nc, memory, "key_index", [P, HP, TOPK], U32)
        idx_f = sbuf(nc, memory, "key_index_f", [P, NT, 2, PH, TOPK])
        cand = sbuf(nc, memory, "candidates", [P, PH, TOPK * TOPK])
        rest = sbuf(nc, memory, "rest", [P, PH, TOPK * TOPK])
        best = sbuf(nc, memory, "cand_best", [P, PH, TOPK])
        gate = sbuf(nc, memory, "gates_rows", [P, NT, TOPK, PH, TOPK])
        stat = sbuf(nc, memory, "cand_stat", [P, 2, PH])
        with nc.Block() as block:
            @block.sync
            def _(sp):
                sp.dma_start(keys[:, :, :], S["keys_src"]).then_inc(keys_in, 16)

            @block.tensor
            def _(pe):
                pe.wait_ge(keys_in, 16)
                for a in range(NT):
                    if a:
                        pe.wait_ge(scores_out, a)
                    for i in range(HP):
                        last = nc.tensor.matmul(PS[:, i // 4, (i % 4) * P:(i % 4 + 1) * P],
                                                S["q_cols"][:, i, a * P:(a + 1) * P], keys[:, i, :], start=True, stop=True)
                    last.then_inc(scores_done, 1)
                for a in range(NT):
                    pe.wait_ge(gates_done, a + 1)
                    for half in range(2):
                        last = nc.tensor.transpose(PS[:, 4, half * T + a * P:half * T + (a + 1) * P],
                                                   idx_f[:, a, half, :, :], C["ident"])
                    last.then_inc(idx_t, 1)
                for a in range(NT):
                    for r in range(0, TOPK, 4):
                        n = a * 4 + r // 4
                        if n >= 2:
                            pe.wait_ge(gates_out, n - 1)
                        for j in range(4):
                            last = nc.tensor.transpose(PS[:, 5 + n % 2, j * P:(j + 1) * P], gate[:, a, r + j, :, :],
                                                       C["ident"])
                        last.then_inc(gates_t, 1)

            @block.scalar
            def _(act):
                for a in range(NT):
                    act.wait_ge(scores_done, a + 1)
                    if a:
                        act.wait_ge(gates_done, a)
                    nc.scalar.activation(sc[:, :, :], PS[:, 0:4, :].rearrange("p b (i n) -> p (b i) n", n=NKEYS),
                                         ACT.Copy).then_inc(scores_out, 1)
                    act.wait_ge(exp_ready, a + 1)
                    nc.scalar.activation(cand[:, :, :], cand[:, :, :], ACT.Exp).then_inc(exp_done, 1)
                act.wait_ge(idx_t, NT)
                nc.scalar.activation(S["idx_cols"][:, :, :], PS[:, 4, :].rearrange("p (h t) -> p h t", t=T),
                                     ACT.Copy).then_inc(idx_out, 1)
                for n in range(NT * 4):
                    a, r = n // 4, n % 4 * 4
                    act.wait_ge(gates_t, n + 1)
                    nc.scalar.activation(S["gate_cols"][:, r:r + 4, a * P:(a + 1) * P],
                                         PS[:, 5 + n % 2, :].rearrange("p (r t) -> p r t", t=P),
                                         ACT.Copy).then_inc(gates_out, 1)

            @block.vector
            def _(dve):
                step = chain(dve, dve_step)
                for a in range(NT):
                    dve.wait_ge(scores_out, a + 1)
                    for i in range(HP):
                        last = nc.vector.max(val[:, i, 0:8], sc[:, i, :])
                    step(last)
                    for i in range(HP):
                        last = nc.vector.max_index(idx[:, i, 0:8], val[:, i, 0:8], sc[:, i, :])
                    step(last)
                    for i in range(HP):
                        last = nc.vector.match_replace(sc[:, i, :], val[:, i, 0:8], sc[:, i, :], NEG)
                    step(last)
                    for i in range(HP):
                        last = nc.vector.max(val[:, i, 8:16], sc[:, i, :])
                    step(last)
                    for i in range(HP):
                        last = nc.vector.max_index(idx[:, i, 8:16], val[:, i, 8:16], sc[:, i, :])
                    step(last)
                    step(nc.vector.tensor_copy(idx_f[:, a, :, :, :].rearrange("p h e k -> p e h k"),
                                               idx[:, :, :].rearrange("p (e h) k -> p e h k", h=2)))
                    v = val[:, :, :].rearrange("p (e h) k -> p e h k", h=2)
                    for e in range(PH):
                        last = nc.vector.tensor_tensor(cand[:, e, :].rearrange("p (r s) -> p r s", s=TOPK),
                                                       v[:, e, 0, :].unsqueeze(2).to_broadcast([P, TOPK, TOPK]),
                                                       v[:, e, 1, :].unsqueeze(1).to_broadcast([P, TOPK, TOPK]), ALU.add)
                    step(last)
                    for e in range(PH):
                        last = nc.vector.max(best[:, e, 0:8], cand[:, e, :])
                    step(last)
                    for e in range(PH):
                        last = nc.vector.match_replace(rest[:, e, :], best[:, e, 0:8], cand[:, e, :], NEG)
                    step(last)
                    for e in range(PH):
                        last = nc.vector.max(best[:, e, 8:16], rest[:, e, :])
                    step(last)
                    for e in range(PH):
                        last = nc.vector.match_replace(rest[:, e, :], best[:, e, 8:16], rest[:, e, :], NEG)
                    step(last)
                    step(nc.vector.tensor_tensor(rest[:, :, :], rest[:, :, :], cand[:, :, :], ALU.not_equal))
                    nc.vector.tensor_tensor(cand[:, :, :], cand[:, :, :],
                                            best[:, :, 0:1].to_broadcast([P, PH, TOPK * TOPK]),
                                            ALU.subtract).then_inc(exp_ready, 1)
                    dve.wait_ge(exp_done, a + 1)
                    g = gate[:, a, :, :, :].rearrange("p r e s -> p e r s")
                    step(nc.vector.tensor_tensor(cand[:, :, :], cand[:, :, :], rest[:, :, :], ALU.mult))
                    step(nc.vector.tensor_reduce(stat[:, 0, :], cand[:, :, :], X, ALU.add))
                    step(nc.vector.reciprocal(stat[:, 1, :], stat[:, 0, :]))
                    nc.vector.tensor_tensor(g, cand[:, :, :].rearrange("p e (r s) -> p e r s", s=TOPK),
                                            stat[:, 1, :].unsqueeze(2).unsqueeze(3).to_broadcast([P, PH, TOPK, TOPK]),
                                            ALU.mult).then_inc(gates_done, 1)
                    dve.wait_ge(gates_done, a + 1)


def peer_spread(nc, S):
    PS, C = S["psum"], S["const"]
    G4 = 4
    STEPS = T // G4
    with phase(nc, "hot_done diag_done r_done r_out g_done g_out") as (
            memory, hot_done, diag_done, r_done, r_out, g_done, g_out):
        hot_i = sbuf(nc, memory, "hot_i", [P, 2, G4, P])
        hot_j = sbuf(nc, memory, "hot_j", [P, 2, G4, P])
        diag = sbuf(nc, memory, "diag", [P, 2, G4, PH, TOPK])
        r = sbuf(nc, memory, "r_rows", [P, 2, G4, P])
        iota = C["iota"].unsqueeze(1).to_broadcast([P, G4, P])
        mask = C["head_of_row"].unsqueeze(1).unsqueeze(3).to_broadcast([P, G4, PH, TOPK])

        with nc.Block() as block:
            @block.vector
            def _(dve):
                def build(i, b):
                    t0 = i * (2 * G4) + b * G4
                    gates = S["gate_cols"][:, :, bass.ds(t0, G4)].rearrange("p r t -> p t r").unsqueeze(2) \
                        .to_broadcast([P, G4, PH, TOPK])
                    nc.vector.tensor_tensor(diag[:, b], gates, mask, ALU.mult)
                    for hot, half in ((hot_j, 1), (hot_i, 0)):
                        index = S["idx_cols"][:, half, bass.ds(t0, G4)].unsqueeze(2).to_broadcast([P, G4, P])
                        last = nc.vector.tensor_tensor(hot[:, b], iota, index, ALU.is_equal)
                    last.then_inc(hot_done, 1)

                for b in range(2):
                    build(0, b)
                with dve.Fori(1, STEPS // 2) as i:
                    for b in range(2):
                        dve.wait_ge(g_done, i * 2 + (b - 1))
                        build(i, b)

            @block.tensor
            def _(pe):
                def first(n, b, again=True):
                    pe.wait_ge(hot_done, n + 1)
                    if again:
                        pe.wait_ge(r_out, n - 1)
                    for j in range(G4):
                        last = nc.tensor.matmul(PS[:, b, j * P:(j + 1) * P],
                                                diag[:, b, j, :, :].rearrange("p e r -> p (e r)"), hot_j[:, b, j, :],
                                                start=True, stop=True)
                    last.then_inc(r_done, 1)

                def second(n, b, again=True):
                    pe.wait_ge(r_out, n + 1)
                    if again:
                        pe.wait_ge(g_out, n - 1)
                    for j in range(G4):
                        last = nc.tensor.matmul(PS[:, 2 + b, j * P:(j + 1) * P], hot_i[:, b, j, :], r[:, b, j, :],
                                                start=True, stop=True)
                    last.then_inc(g_done, 1)

                first(0, 0, again=False)
                first(1, 1, again=False)
                second(0, 0, again=False)
                first(2, 0)
                second(1, 1, again=False)
                with pe.Fori(1, STEPS // 2 - 1) as i:
                    first(i * 2 + 1, 1)
                    second(i * 2, 0)
                    first(i * 2 + 2, 0)
                    second(i * 2 + 1, 1)
                first(STEPS - 1, 1)
                second(STEPS - 2, 0)
                second(STEPS - 1, 1)

            @block.scalar
            def _(act):
                def take_r(n, b):
                    act.wait_ge(r_done, n + 1)
                    nc.scalar.activation(r[:, b, :, :], PS[:, b, :].rearrange("p (t j) -> p t j", j=P),
                                         ACT.Copy).then_inc(r_out, 1)

                def take_g(n, b):
                    act.wait_ge(g_done, n + 1)
                    nc.scalar.activation(S["all_gates"][:, :, bass.ds(n * G4, G4)].rearrange("p j t -> p t j"),
                                         PS[:, 2 + b, :].rearrange("p (t j) -> p t j", j=P), ACT.Copy).then_inc(g_out, 1)

                take_r(0, 0)
                with act.Fori(0, STEPS // 2 - 1) as i:
                    take_r(i * 2 + 1, 1)
                    take_g(i * 2, 0)
                    take_r(i * 2 + 2, 0)
                    take_g(i * 2 + 1, 1)
                take_r(STEPS - 1, 1)
                take_g(STEPS - 2, 0)
                take_g(STEPS - 1, 1)


def peer_experts(nc, S, layer):
    PS, C, L = S["psum"], S["const"], S["layer"]
    with phase(nc, "u_in0 u_in1 v_in0 v_in1 dve_step zeroed a_done a_out hid_done y_done root_ready root_done") as (
            memory, u_in0, u_in1, v_in0, v_in1, dve_step, zeroed, a_done, a_out, hid_done, y_done, root_ready, root_done):
        u = sbuf(nc, memory, "u_t", [P, 2, KD, P])
        v = sbuf(nc, memory, "v", [P, 2, D])
        zero = sbuf(nc, memory, "zeros2", [P, BANK])
        act_h = sbuf(nc, memory, "gelu", [P, 2, T])
        hid = sbuf(nc, memory, "hid2", [P, 2, T])
        stats = sbuf(nc, memory, "ln_stats2", [P, NT, 16])
        u_in, v_in = (u_in0, u_in1), (v_in0, v_in1)
        ud, vd = S["u_src"], S["v_src"]
        h = S["h_cols"]
        N = NKEYS

        with nc.Block() as block:
            @block.sync
            def _(sp):
                for b in range(2):
                    sp.dma_start(u[:, b, :, :], ud(b)).then_inc(u_in[b], 16)
                    sp.dma_start(v[:, b, :], vd(b)).then_inc(v_in[b], 16)
                with sp.Fori(1, N // 2) as i:
                    for b in range(2):
                        sp.wait_ge(a_done, i * 2 + (b - 1))
                        sp.dma_start(u[:, b, :, :], ud(i * 2 + b)).then_inc(u_in[b], 16)
                        sp.wait_ge(y_done, i * 2 + (b - 1))
                        sp.dma_start(v[:, b, :], vd(i * 2 + b)).then_inc(v_in[b], 16)

            @block.tensor
            def _(pe):
                pe.wait_ge(zeroed, 1)
                for b in range(4):
                    nc.tensor.matmul(PS[:, 4 + b, :], zero[:, 0:P], zero[:, :], start=True, stop=False,
                                     skip_group_check=True)

                def hidden(b):
                    for k in range(KD):
                        last = nc.tensor.matmul(PS[:, b, 0:T], u[:, b, k, :], h[:, k, :], start=(k == 0), stop=(k == KD - 1))
                    last.then_inc(a_done, 1)

                def back(b):
                    for a in range(NT):
                        for n in range(2):
                            last = nc.tensor.matmul(PS[:, 4 + 2 * a + n, :], hid[:, b, a * P:(a + 1) * P],
                                                    v[:, b, n * BANK:(n + 1) * BANK], start=False, stop=False,
                                                    skip_group_check=True)
                    last.then_inc(y_done, 1)

                pe.wait_ge(u_in[0], 16)
                hidden(0)
                with pe.Fori(0, N // 2 - 1) as i:
                    pe.wait_ge(u_in[1], i * 16 + 16)
                    hidden(1)
                    pe.wait_ge(v_in[0], i * 16 + 16)
                    pe.wait_ge(hid_done, i * 2 + 1)
                    back(0)
                    pe.wait_ge(u_in[0], i * 16 + 32)
                    hidden(0)
                    pe.wait_ge(v_in[1], i * 16 + 16)
                    pe.wait_ge(hid_done, i * 2 + 2)
                    back(1)
                pe.wait_ge(u_in[1], N * 8)
                hidden(1)
                pe.wait_ge(v_in[0], N * 8)
                pe.wait_ge(hid_done, N - 1)
                back(0)
                pe.wait_ge(v_in[1], N * 8)
                pe.wait_ge(hid_done, N)
                back(1)

            @block.scalar
            def _(act):
                with act.Fori(0, N // 2) as i:
                    for b in range(2):
                        act.wait_ge(a_done, i * 2 + b + 1)
                        nc.scalar.activation(act_h[:, b, :], PS[:, b, 0:T], ACT.Gelu).then_inc(a_out, 1)
                act.wait_ge(root_ready, 1)
                nc.scalar.activation(stats[:, :, 14:15], stats[:, :, 14:15], ACT.Sqrt).then_inc(root_done, 1)

            @block.vector
            def _(dve):
                step = chain(dve, dve_step)
                nc.vector.memset(zero[:, :], 0.0).then_inc(zeroed, 1)
                with dve.Fori(0, N // 2) as i:
                    for b in range(2):
                        dve.wait_ge(a_out, i * 2 + b + 1)
                        gates = S["all_gates"][:, bass.ds(i * 2 + b, 1), :].rearrange("p o t -> p (o t)")
                        nc.vector.tensor_tensor(hid[:, b, :], act_h[:, b, :], gates, ALU.mult).then_inc(hid_done, 1)
                layer_norm(dve, None, nc, step, None, S["x"], stats, lambda a, n: PS[:, 4 + 2 * a + n, :],
                           L["ln2_g"], L["ln2_b"], lambda a, n: dve.wait_ge(y_done, N), root_ready, root_done)



def program(nc, dram, out):
    with ExitStack() as whole:
        psum = whole.enter_context(nc.psum_tensor("psum", [P, BANKS, BANK], F32))
        at, n = columns_of(shared=True)
        const = sbuf(nc, whole, "constants", [P, n])
        x = sbuf(nc, whole, "x", [P, NT, D])
        h_cols = sbuf(nc, whole, "h_cols", [P, KD, T])
        C = {k: const[:, a:a + n] for k, (a, n) in at.items()}
        C["dist"] = C["dist"].rearrange("p (a t) -> p a t", a=NT)
        S = {"psum": psum, "const": C, "x": x, "h_cols": h_cols, "dram": dram, "const_all": const}

        first_block(nc, S)
        second_block(nc, S)

        with phase(nc, "stored") as (memory, stored):
            with nc.Block() as block:
                @block.sync
                def _(sp):
                    sp.dma_start(out.rearrange("o (a p) d -> p (o a) d", p=P), x[:, :, :]).then_inc(stored, 16)
                    sp.wait_ge(stored, 16)


def first_block(nc, S):
    dram = S["dram"]
    with ExitStack() as memory:
        at, n = columns_of(shared=False)
        const = sbuf(nc, memory, "constants_first", [P, n])
        S["const"].update({k: const[:, a:a + n] for k, (a, n) in at.items()})
        S["const"]["band"] = S["const"]["band"].rearrange("p (a g t) -> p a g t", a=NT, g=GROUPS)
        small = {"norm1_g": [P, KD], "norm2_g": [P, KD], "mu_prev": [P, RWKV_TILES], "mu_next": [P, RWKV_TILES],
                 "w_decay0": [P, 2 * RT], "a_gate0": [P, 2 * RT], "k_k": [P, RT], "k_a": [P, RT], "r_k": [P, RT],
                 "gn_w": [P, RT], "gn_b": [P, RT], "b_merge": [P, 2 * KD], "g_up": [P, RC],
                 "router": [P, KD, MOE_GROUPS + EXPERTS]}
        buf = {k: sbuf(nc, memory, f"{k}_sb", s) for k, s in small.items()}
        buf["lora_up"] = sbuf(nc, memory, "lora_up_sb", [P, 2, RC])
        buf["positions"] = sbuf(nc, memory, "positions_sb", [P, NT], I32)
        rows = {"q_norm_g": HD, "k_norm_g": HD}
        for k, n in rows.items():
            buf[k] = sbuf(nc, memory, f"{k}_sb", [P, n])
        buf["router_bias"] = sbuf(nc, memory, "router_bias_sb", [P, MOE_GROUPS + EXPERTS])
        S["weights"] = {k: v[:, :] if len(v.shape) == 2 else v for k, v in buf.items()}
        W = S["weights"]

        with phase(nc, "const_in loaded") as (_, const_in, loaded):
            with nc.Block() as block:
                @block.sync
                def _(sp):
                    sp.dma_start(S["x"][:, :, :], dram["x"].rearrange("(a p) d -> p a d", p=P)).then_inc(loaded, 16)
                    sp.dma_start(buf["norm1_g"][:, :], dram["norm1_g"]).then_inc(loaded, 16)
                    sp.dma_start(S["const_all"][:, :], dram["constants"]).then_inc(loaded, 16)
                    sp.dma_start(const[:, :], dram["constants_first"]).then_inc(loaded, 16)
                    n = 4
                    for k in small:
                        if k not in ("norm1_g", "router"):
                            sp.dma_start(buf[k][:, :], dram[k]).then_inc(loaded, 16)
                            n += 1
                    sp.dma_start(buf["router"][:, :, 0:MOE_GROUPS], dram["w_router_group"]).then_inc(loaded, 16)
                    sp.dma_start(buf["router"][:, :, MOE_GROUPS:], dram["w_router_expert"]).then_inc(loaded, 16)
                    sp.dma_start(buf["lora_up"][0:HD, :, :], dram["w_decay_up"].rearrange("d k n -> k d n")).then_inc(loaded, 16)
                    sp.dma_start(buf["lora_up"][HD:P, :, :], dram["a_gate_up"].rearrange("d k n -> k d n")).then_inc(loaded, 16)
                    sp.dma_start(buf["positions"][:, :], dram["positions"]).then_inc(loaded, 16)
                    for k in rows:
                        sp.dma_start(buf[k][:, :], dram[k].partition_broadcast(P)).then_inc(loaded, 16)
                    sp.dma_start(buf["router_bias"][:, 0:MOE_GROUPS], dram["b_router_group"].partition_broadcast(P)).then_inc(loaded, 16)
                    sp.dma_start(buf["router_bias"][:, MOE_GROUPS:], dram["b_router_expert"].partition_broadcast(P)).then_inc(loaded, 16)
                    n += 9
                    sp.wait_ge(loaded, 16 * n)

        with ExitStack() as mixers:
            R = {}
            S["rwkv"] = R
            R["y"] = sbuf(nc, mixers, "rwkv_y", [P, RT, T])
            R["bonus"] = sbuf(nc, mixers, "rwkv_bonus", [P, RT, T])
            R["gate"] = sbuf(nc, mixers, "rwkv_gate", [P, RT, T])
            S["gates"] = sbuf(nc, mixers, "branch_gates", [P, 2 * KD, T])
            S["qkv"] = sbuf(nc, mixers, "qkv", [P, NT, 3 * AC])
            with ExitStack() as rwkv:
                for k in "abkr":
                    R[k] = sbuf(nc, rwkv, f"rwkv_{k}", [P, 2, RT, T])
                R["v_rows"] = sbuf(nc, rwkv, "rwkv_v_rows", [P, NT, RC])
                R["b_rows"] = sbuf(nc, rwkv, "rwkv_b_rows", [P, 2, RC])
                R["k_rows"] = sbuf(nc, rwkv, "rwkv_k_rows", [P, 2, RC])
                R["carry"] = sbuf(nc, rwkv, "rwkv_carry", [P, 2, RT])
                with ExitStack() as raw:
                    u = S["u_rwkv"] = sbuf(nc, raw, "u_rwkv", [P, RWKV_TILES, T + 2])
                    with phase(nc, "") as (_,):
                        with nc.Block() as block:
                            @block.vector
                            def _(dve):
                                nc.vector.memset(u[:, :, 0:1], 0.0)
                                nc.vector.memset(u[:, :, T + 1:T + 2], 0.0)

                    A0 = RWKV_COLS
                    G0 = RWKV_COLS + 3 * AC
                    slabs = ([(c, 512, "columns") for c in (0, 512, 1024)] + [(1536, 256, "columns")] +
                             [(A0 + c, 512, "rows") for c in range(0, 2048, 512)] + [(A0 + 2048, 256, "rows")] +
                             [(G0 + c, 512, "columns") for c in range(0, 2048, 512)])

                    def evacuate(name, eng, form, bank, c0, a):
                        if form == "rows":
                            out = S["qkv"][:, a, c0 - A0:c0 - A0 + bank.shape[-1]]
                            return (nc.vector.tensor_copy(out, bank) if name == "dve"
                                    else nc.scalar.activation(out, bank, ACT.Copy))
                        two = bank.rearrange("p (c t) -> p c t", t=T)
                        if c0 < A0:
                            out = u[:, c0 // P:c0 // P + 2, 1:T + 1]
                            return (nc.vector.tensor_copy(out, two) if name == "dve"
                                    else nc.scalar.activation(out, two, ACT.Copy))
                        g = (c0 - G0) // P
                        out = S["gates"][:, g:g + 2, :]
                        bias = W["b_merge"][:, g:g + 2].unsqueeze(2).to_broadcast([P, 2, T])
                        if name == "dve":
                            return nc.vector.tensor_tensor(out, two, bias, ALU.add)
                        nc.scalar.activation(out[:, 0, :], two[:, 0, :], ACT.Identity, bias=W["b_merge"][:, g:g + 1])
                        return nc.scalar.activation(out[:, 1, :], two[:, 1, :], ACT.Identity,
                                                    bias=W["b_merge"][:, g + 1:g + 2])

                    project(nc, S, "in1", S["x"], S["h_cols"], dram["w_in"], slabs, norm_scale=W["norm1_g"],
                            evacuate=evacuate)
                    with phase(nc, "") as (_,):
                        with nc.Block() as block:
                            @block.scalar
                            def _(act):
                                nc.scalar.activation(S["gates"][:, :, :], S["gates"][:, :, :], ACT.Sigmoid)
                    R["mixed"] = sbuf(nc, raw, "mixed_u", [P, RWKV_TILES, T])
                    rwkv_prepare(nc, S)
                rwkv_scan(nc, S)
            rwkv_finish(nc, S)
            with ExitStack() as out_weights:
                S["w_rwkv_out"] = sbuf(nc, out_weights, "w_rwkv_out_sb", [P, RT, D])
                S["w_attn_out"] = sbuf(nc, out_weights, "w_attn_out_sb", [P, 2, D])
                S["w_out"] = sbuf(nc, out_weights, "w_out_sb", [P, KD, D])
                S["attn_cols"] = sbuf(nc, out_weights, "attn_cols", [P, 2, T])
                attention(nc, S)
                merge(nc, S)
        project(nc, S, "norm2", S["x"], S["h_cols"], dram["w_in"], [], norm_scale=W["norm2_g"])
        with ExitStack() as moe:
            S["spread"] = sbuf(nc, moe, "expert_shares", [P, EXPERTS, T])
            route(nc, S)
            experts(nc, S)



def second_block(nc, S):
    dram = S["dram"]
    with nc.Fori(0, LAYERS) as layer:
        def one(name, inner="p n"):
            a, *b = inner.split()
            return dram[name][(bass.ds(layer, 1),) + (slice(None),) * (len(inner.split()))].rearrange(
                f"l {inner} -> (l {a}) {' '.join(b)}")

        with ExitStack() as memory:
            L = S["layer"] = {k: sbuf(nc, memory, f"{k}_row", [P, n]) for k, n in
                              (("ln1_g", D), ("ln1_b", D), ("ln2_g", D), ("ln2_b", D), ("subln_g", 2 * HD),
                               ("lambda_init", 2))}
            lam = sbuf(nc, memory, "lam_rows", [P, 4, HD])
            with phase(nc, "loaded") as (_, loaded):
                with nc.Block() as block:
                    @block.sync
                    def _(sp):
                        for k in ("ln1_g", "ln1_b", "ln2_g", "ln2_b", "subln_g", "lambda_init"):
                            src = dram[k + "_2"][bass.ds(layer, 1), :].rearrange("l n -> (l n)").partition_broadcast(P)
                            sp.dma_start(L[k][:, :], src).then_inc(loaded, 16)
                        for i, k in enumerate(("lam_q1_2", "lam_k1_2", "lam_q2_2", "lam_k2_2")):
                            src = dram[k][bass.ds(layer, 1), :].rearrange("l n -> (l n)").partition_broadcast(P)
                            sp.dma_start(lam[:, i, :], src).then_inc(loaded, 16)
                        sp.wait_ge(loaded, 16 * 10)
            for k in ("ln1_g", "ln1_b", "ln2_g", "ln2_b", "subln_g", "lambda_init"):
                L[k] = L[k][:, :]
            L["lam"] = lam

            with ExitStack() as mixers:
                S["mixed"] = sbuf(nc, mixers, "mixed_rows", [P, NT, D])
                S["dqk"] = sbuf(nc, mixers, "dqk", [P, 2 * DH, T])
                S["sqk"] = sbuf(nc, mixers, "sqk", [P, SH, T])
                S["dv"] = sbuf(nc, mixers, "dv", [P, NT, DH * 2 * HD])
                S["sv"] = sbuf(nc, mixers, "sv", [P, NT, SH * HD])
                slabs = [(0, 512, "columns"), (512, 512, "columns"), (1024, 512, "rows"),
                         (1536, 512, "columns"), (2048, 512, "columns"), (2560, 512, "rows")]

                def evacuate(name, eng, form, bank, c0, a):
                    if form == "rows":
                        to, src = S["dv" if c0 == 1024 else "sv"][:, a, :], bank
                    elif c0 < 1024:
                        to, src = S["dqk"][:, c0 // P:c0 // P + 2, :], bank.rearrange("p (c t) -> p c t", t=T)
                    else:
                        c = (c0 - 1536) // P
                        to, src = S["sqk"][:, c:c + 2, :], bank.rearrange("p (c t) -> p c t", t=T)
                    return nc.vector.tensor_copy(to, src) if name == "dve" else nc.scalar.activation(to, src, ACT.Copy)

                project(nc, S, "in2", S["x"], S["h_cols"], one("w_in_2", "k n"), slabs, evacuate=evacuate)
                differential(nc, S)
                stick_breaking(nc, S)
                mix_out(nc, S, layer)

            with ExitStack() as peer:
                S["idx_cols"] = sbuf(nc, peer, "idx_cols", [P, 2, T])
                S["gate_cols"] = sbuf(nc, peer, "gate_cols", [P, TOPK, T])
                with ExitStack() as query:
                    q = S["q_cols"] = sbuf(nc, query, "q_cols", [P, 2 * PH, T])

                    def evacuate_q(name, eng, form, bank, c0, a):
                        to, src = q[:, c0 // P:c0 // P + 2, :], bank.rearrange("p (c t) -> p c t", t=T)
                        return nc.vector.tensor_copy(to, src) if name == "dve" else nc.scalar.activation(to, src, ACT.Copy)

                    project(nc, S, "query", S["x"], S["h_cols"], one("w_query_2", "k n"),
                            [(c, 512, "columns") for c in range(0, 2048, 512)], evacuate=evacuate_q)
                    S["keys_src"] = one("sub_keys_2", "p e n")
                    peer_select(nc, S)
                S["all_gates"] = sbuf(nc, peer, "all_gates", [P, NKEYS, T])
                peer_spread(nc, S)
                u, v = dram["expert_u_2"], dram["expert_v_2"]
                S["u_src"] = lambda j: u[bass.ds(layer * NKEYS + j, 1), :, :, :].rearrange("j p k i -> (j p) k i")
                S["v_src"] = lambda j: v[bass.ds(layer * NKEYS + j, 1), :, :].rearrange("j i d -> (j i) d")
                peer_experts(nc, S, layer)


def layout(inputs):
    def get(name):
        a = np.asarray(inputs[name])
        return a[0] if name in ONE_LAYER else a

    def channels(a):
        return a.reshape(-1, P).T

    pack = {s: np.concatenate([v for k, v in constants().items() if (k in SHARED) == s], axis=1) for s in (True, False)}
    arrays = {"x": get("x"), "constants": pack[True], "constants_first": pack[False],
              "positions": np.asarray(inputs["positions"]).reshape(NT, P).T}
    for k in ("norm1_g", "norm2_g", "mu_prev", "mu_next", "w_decay0", "a_gate0", "k_k", "k_a", "r_k", "gn_w", "gn_b",
              "b_merge"):
        arrays[k] = channels(get(k))
    for k in ("w_in", "w_decay_up", "a_gate_up", "g_up", "w_rwkv_out", "q_norm_g", "k_norm_g", "w_attn_out", "w_out",
              "b_router_group", "b_router_expert", "w_gate", "w_up", "w_down"):
        arrays[k] = get(k)
    for k in ("w_router_group", "w_router_expert"):
        arrays[k] = get(k).reshape(KD, P, -1).transpose(1, 0, 2)
    for k in ("w_in", "lam_q1", "lam_k1", "lam_q2", "lam_k2", "subln_g", "w_o", "ln1_g", "ln1_b", "w_query", "ln2_g",
              "ln2_b"):
        arrays[k + "_2"] = get(k + "_2")
    init = [0.8 - 0.6 * math.exp(-0.3 * l) for l in range(LAYERS)]
    arrays["lambda_init_2"] = np.array([[i, 1 - i] for i in init], np.float32)
    arrays["sub_keys_2"] = get("sub_keys_2").reshape(LAYERS, 2 * PH, NKEYS, P).transpose(0, 3, 1, 2)
    arrays["expert_u_2"] = get("expert_u_2").reshape(LAYERS, NKEYS, NKEYS, KD, P).transpose(0, 2, 4, 3, 1) \
        .reshape(LAYERS * NKEYS, P, KD, NKEYS)
    arrays["expert_v_2"] = get("expert_v_2").reshape(LAYERS, NKEYS, NKEYS, D).transpose(0, 2, 1, 3) \
        .reshape(LAYERS * NKEYS, NKEYS, D)
    return {k: np.ascontiguousarray(v) for k, v in arrays.items()}


ONE_LAYER = {"x", "norm1_g", "w_in", "mu_prev", "mu_next", "w_decay0", "w_decay_up", "a_gate0", "a_gate_up", "g_up",
             "k_k", "k_a", "r_k", "gn_w", "gn_b", "w_rwkv_out", "q_norm_g", "k_norm_g", "w_attn_out", "b_merge",
             "w_out", "norm2_g", "w_router_group", "b_router_group", "w_router_expert", "b_router_expert", "w_gate",
             "w_up", "w_down"}


def kernel(**inputs):
    import concourse.bacc as bacc
    from concourse.bass_utils import run_bass_kernel_spmd

    nc = bacc.Bacc("TRN2", target_bir_lowering=False, num_devices=1)
    arrays = {f"{k}_dram": v for k, v in layout(inputs).items()}
    dram = {k[:-5]: nc.dram_tensor(k, v.shape, mybir.dt.from_np(v.dtype), kind="ExternalInput").ap()
            for k, v in arrays.items()}
    out = nc.dram_tensor("out_dram", (1, T, D), F32, kind="ExternalOutput").ap()
    program(nc, dram, out)
    result = run_bass_kernel_spmd(nc, [arrays], core_ids=[0])
    return result.results[0]["out_dram"]
```

```python
import math
from contextlib import ExitStack, contextmanager

import numpy as np

import concourse.bass as bass
from concourse import mybir

F32 = mybir.dt.float32
I32 = mybir.dt.int32
U32 = mybir.dt.uint32
ACT = mybir.ActivationFunctionType
ALU = mybir.AluOpType
X = mybir.AxisListType.X

P = 128
T = 256
NT = T // P
D = 1024
KD = D // P
HD = 64
BANKS, BANK = 8, 512

RH = 8
RC = RH * HD
RT = RC // P
RWKV_COLS = 3 * RC + 64 + 64 + 128
RWKV_TILES = RWKV_COLS // P
AH, SLOTS, GROUPS = 12, 4, 3
AC = AH * HD
DILATION = (1, 4, 16)
BAND = 64
DECAY = math.exp(-0.5)
NORM_EPS, GN_EPS = 1e-6, 64e-5
ROT = 16
ROPE_THETA = 500000.0
EXPERTS, MOE_GROUPS, PER_GROUP, DE = 32, 4, 8, 512
CHOSEN = 2
OVERFLOW = CHOSEN * T // (P + 1)
LEVELS = (1, 2, 4, 8, 16, 32, 64)

LAYERS = 2
DH = 4
SH = 8
PH, TOPK, NKEYS = 8, 16, 128
ALPHA = (2.0 * LAYERS) ** 0.25
LN_EPS = RMS_EPS = 1e-5
NEG = -1e30



def constants():
    p = np.arange(P)[:, None]
    q = np.arange(P)[None, :]
    c = {"ident": (p == q), "head_ones": (p // HD == q // HD), "ones": np.ones((P, P))}
    for k in LEVELS:
        same = p // (2 * k) == q // (2 * k)
        c[f"low{k}"] = same & (p % (2 * k) >= k) & (q % (2 * k) < k)
        c[f"up{k}"] = same & (p % (2 * k) < k) & (q % (2 * k) >= k)
    c["p<q"], c["p<=q"], c["p>q"], c["p>=q"] = p < q, p <= q, p > q, p >= q
    band = np.zeros((P, NT, GROUPS, T))
    dist = np.zeros((P, NT, T))
    for t in range(NT):
        gap = (t * P + np.arange(P))[:, None] - np.arange(T)[None, :]
        for g, d in enumerate(DILATION):
            ok = (gap % d == 0) & (np.abs(gap) // d <= BAND)
            band[:, t, g] = np.where(ok, 0.0, NEG)
        dist[:, t] = np.where(gap >= 0, gap, -NEG)
    c["band"] = band
    c["dist"] = dist
    half = ROT // 2
    c["inv_freq"] = np.tile(np.float32(ROPE_THETA) ** -(np.arange(half, dtype=np.float32) * np.float32(2.0 / ROT)), (P, 1))
    c["iota"] = np.tile(np.arange(P), (P, 1))
    c["head_of_row"] = (p // TOPK == np.arange(PH)[None, :])
    return {k: np.ascontiguousarray(v.reshape(P, -1).astype(np.float32)) for k, v in c.items()}


ALWAYS, MIXERS, FIRST = "constants", "constants_mixers", "constants_first"


def pack_of(name):
    return {"ident": ALWAYS, "iota": ALWAYS, "head_of_row": ALWAYS,
            "ones": MIXERS, "p>q": MIXERS, "p<q": MIXERS, "dist": MIXERS}.get(name, FIRST)


def columns_of(pack):
    at, n = {}, 0
    for k, v in constants().items():
        if pack_of(k) == pack:
            at[k] = (n, v.shape[1])
            n += v.shape[1]
    return at, n


def place_constants(nc, S, memory, pack):
    at, n = columns_of(pack)
    buffer = sbuf(nc, memory, f"{pack}_{nc.next_id()}", [P, n])
    C = S["const"]
    C.update({k: buffer[:, a:a + n] for k, (a, n) in at.items()})
    if pack == MIXERS:
        C["dist"] = C["dist"].rearrange("p (a t) -> p a t", a=NT)
    if pack == FIRST:
        C["band"] = C["band"].rearrange("p (a g t) -> p a g t", a=NT, g=GROUPS)
    return buffer


@contextmanager
def phase(nc, semaphores):
    with ExitStack() as memory:
        number = nc.next_id()
        sems = [nc.alloc_semaphore(f"{name}_{number}") for name in semaphores.split()]
        yield (memory, *sems)
        nc.clear_and_free_semaphores(sems)
        nc.all_engine_barrier()


def chain(eng, sem):
    n = [0]

    def step(ins):
        n[0] += 1
        ins.then_inc(sem, 1)
        eng.wait_ge(sem, n[0])
    return step


def sbuf(nc, memory, name, shape, dtype=F32):
    return memory.enter_context(nc.sbuf_tensor(name, shape, dtype))


F32R = mybir.dt.float32r


def r32(ap):
    return ap.bitcast(F32R)


def carve(tensor):
    flat = tensor[:, :, :].rearrange("p a b -> p (a b)")
    at = [0]

    def take(shape):
        n = math.prod(shape[1:])
        ap = flat[:, at[0]:at[0] + n]
        at[0] += n
        names = "abcdef"[:len(shape) - 1]
        sizes = {k: v for k, v in zip(names[1:], shape[2:])}
        return ap if len(shape) == 2 else ap.rearrange(f"p ({' '.join(names)}) -> p {' '.join(names)}", **sizes)
    return take



def project(nc, S, name, rows, weights, slabs, cols=None, norm_scale=None, evacuate=None, scaled=None, loads=(),
            raw=None):
    PS, C = S["psum"], S["const"]
    WIDE = 2 * P
    slabs = [(c, form) for c0, width, form in slabs for c in range(c0, c0 + width, WIDE)]
    RING = 2
    units = []
    for s, (c0, form) in enumerate(slabs):
        units += [(s, form, c0, a) for a in ((None,) if form == "columns" else range(NT))]
    last_of = {u[0]: n for n, u in enumerate(units)}
    by_act = [n % 2 == 1 for n in range(len(units))]
    act_upto = [sum(by_act[:n]) for n in range(len(units) + 1)]

    with phase(nc, "slab_in0 slab_in1 unit_done squares mean_sq rstd_root rstd_done rows_scaled "
                   "transposed cols_top cols_done slab_top slab_low unit_dve unit_act loaded") as (
            memory, slab_in0, slab_in1, unit_done, squares, mean_sq, rstd_root, rstd_done, rows_scaled,
            transposed, cols_top, cols_done, slab_top, slab_low, unit_dve, unit_act, loaded):
        if slabs:
            cols = sbuf(nc, memory, f"{name}_cols", [P, 2, KD, T])
            top = sbuf(nc, memory, f"{name}_top", [P, RING, KD, WIDE])
            low = sbuf(nc, memory, f"{name}_low", [P, RING, KD, WIDE])
            if raw is None:
                raw = sbuf(nc, memory, f"{name}_raw", [P, RING, KD, WIDE])
        if scaled is None:
            scaled = sbuf(nc, memory, f"{name}_scaled", [P, NT, D]) if norm_scale is not None else rows
        stat = sbuf(nc, memory, f"{name}_stat", [P, 4, NT])
        slab_in = (slab_in0, slab_in1)
        w = weights.rearrange("(k p) n -> p k n", p=P)

        with nc.Block() as block:
            @block.sync
            def _(sp):
                share = -(-len(loads) // max(1, len(slabs) - RING))
                for s, (c0, form) in enumerate(slabs):
                    if s >= RING:
                        sp.wait_ge(slab_low, s - RING + 1)
                    sp.dma_start(raw[:, s % RING, :, :], w[:, :, c0:c0 + WIDE]).then_inc(slab_in[s % RING], 16)
                    if s >= RING:
                        for buffer, src in loads[(s - RING) * share:(s - RING + 1) * share]:
                            sp.dma_start(buffer, src).then_inc(loaded, 16)
                if loads:
                    sp.wait_ge(loaded, 16 * len(loads))

            @block.scalar
            def _(act):
                def top_of_slab(s):
                    act.wait_ge(slab_in[s % RING], 16 * (s // RING + 1))
                    if s >= RING:
                        act.wait_ge(unit_done, last_of[s - RING] + 1)
                    nc.scalar.activation(r32(top[:, s % RING, :, :]), raw[:, s % RING, :, :], ACT.Copy).then_inc(slab_top, 1)

                if norm_scale is not None:
                    for a in range(NT):
                        nc.scalar.activation(scaled[:, a, :], rows[:, a, :], ACT.Square,
                                             accum_out=stat[:, 0, a:a + 1]).then_inc(squares, 1)
                    act.wait_ge(mean_sq, 1)
                    nc.scalar.activation(stat[:, 2, :], stat[:, 1, :], ACT.Sqrt).then_inc(rstd_root, 1)
                for k in range(KD):
                    act.wait_ge(transposed, k + 1)
                    by_channel = {} if norm_scale is None else {"scale": norm_scale[:, k:k + 1]}
                    out = r32(cols[:, 0, k, :]) if slabs else cols[:, k, :]
                    nc.scalar.activation(out, PS[:, k, 0:T], ACT.Copy, **by_channel).then_inc(cols_top, 1)
                for s in range(min(RING, len(slabs))):
                    top_of_slab(s)
                for n, (s, form, c0, a) in enumerate(units):
                    if n == last_of[s] and s + RING < len(slabs):
                        top_of_slab(s + RING)
                    if by_act[n]:
                        act.wait_ge(unit_done, n + 1)
                        out = PS[:, n % BANKS, 0:BANK if form == "columns" else WIDE]
                        evacuate("act", act, form, out, c0, a).then_inc(unit_act, 1)

            @block.vector
            def _(dve):
                def low_of_slab(s):
                    dve.wait_ge(slab_top, s + 1)
                    nc.vector.tensor_tensor(r32(low[:, s % RING, :, :]), raw[:, s % RING, :, :], top[:, s % RING, :, :],
                                            ALU.subtract).then_inc(slab_low, 1)

                if norm_scale is not None:
                    dve.wait_ge(squares, NT)
                    nc.vector.tensor_scalar(stat[:, 1, :], stat[:, 0, :], 1.0 / D, NORM_EPS, ALU.mult,
                                            ALU.add).then_inc(mean_sq, 1)
                    dve.wait_ge(rstd_root, 1)
                    nc.vector.reciprocal(stat[:, 3, :], stat[:, 2, :]).then_inc(rstd_done, 1)
                    dve.wait_ge(rstd_done, 1)
                    for a in range(NT):
                        nc.vector.tensor_scalar(scaled[:, a, :], rows[:, a, :], stat[:, 3, a:a + 1], None,
                                                ALU.mult).then_inc(rows_scaled, 1)
                if slabs:
                    for k in range(KD):
                        dve.wait_ge(cols_top, k + 1)
                        whole, out = PS[:, k, 0:T], r32(cols[:, 1, k, :])
                        if norm_scale is None:
                            nc.vector.tensor_tensor(out, whole, cols[:, 0, k, :], ALU.subtract).then_inc(cols_done, 1)
                        else:
                            nc.vector.scalar_tensor_tensor(out, whole, norm_scale[:, k:k + 1], cols[:, 0, k, :], ALU.mult,
                                                           ALU.subtract).then_inc(cols_done, 1)
                for s in range(min(RING, len(slabs))):
                    low_of_slab(s)
                for n, (s, form, c0, a) in enumerate(units):
                    if not by_act[n]:
                        dve.wait_ge(unit_done, n + 1)
                        out = PS[:, n % BANKS, 0:BANK if form == "columns" else WIDE]
                        evacuate("dve", dve, form, out, c0, a).then_inc(unit_dve, 1)
                    if n == last_of[s] and s + RING < len(slabs):
                        low_of_slab(s + RING)

            @block.tensor
            def _(pe):
                if norm_scale is not None:
                    pe.wait_ge(rows_scaled, NT)
                for k in range(KD):
                    for a in range(NT):
                        last = nc.tensor.transpose(PS[:, k, a * P:(a + 1) * P], scaled[:, a, k * P:(k + 1) * P], C["ident"])
                    last.then_inc(transposed, 1)
                if slabs:
                    pe.wait_ge(cols_done, KD)
                for n, (s, form, c0, a) in enumerate(units):
                    if n == 0 or units[n - 1][0] != s:
                        pe.wait_ge(slab_low, s + 1)
                    if n >= BANKS:
                        m = n - BANKS
                        if by_act[m]:
                            pe.wait_ge(unit_act, act_upto[m + 1])
                        else:
                            pe.wait_ge(unit_dve, m + 1 - act_upto[m + 1])
                    for half in range(2 if form == "columns" else 1):
                        for k in range(KD):
                            for i, (x, y) in enumerate(((0, 0), (0, 1), (1, 0))):
                                slab, o = (top, low), slice(half * P, (half + 1) * P)
                                if form == "columns":
                                    lhs, rhs = slab[x][:, s % RING, k, o], cols[:, y, k, :]
                                else:
                                    lhs, rhs = cols[:, x, k, a * P:(a + 1) * P], slab[y][:, s % RING, k, :]
                                last = nc.tensor.matmul(PS[:, n % BANKS, half * T:(half + 1) * T], r32(lhs), r32(rhs),
                                                        start=(k == 0 and i == 0), stop=(k == KD - 1 and i == 2))
                    last.then_inc(unit_done, 1)



def rwkv_prepare(nc, S):
    PS, C, W, R = S["psum"], S["const"], S["weights"], S["rwkv"]
    u, mixed = S["u_rwkv"], R["mixed"]
    r, k, v = (mixed[:, i * RT:(i + 1) * RT, :] for i in range(3))
    LORA, GATE = 3 * RT, 3 * RT + 1

    with phase(nc, "dve_step act_step mixed_done lora_ready unit_done unit_act key_sq norm_sq norm_done "
                   "scan_done exp_done bonus_in bonus_done v_done kb_ready kb_rows rows_out kappa_done") as (
            memory, dve_step, act_step, mixed_done, lora_ready, unit_done, unit_act, key_sq, norm_sq, norm_done,
            scan_done, exp_done, bonus_in, bonus_done, v_done, kb_ready, kb_rows, rows_out, kappa_done):
        c0 = sbuf(nc, memory, "mix_self", [P, RWKV_TILES])
        tanh_w = sbuf(nc, memory, "tanh_w", [P, T])
        sig_g = sbuf(nc, memory, "sig_g", [P, T])
        sig_w = sbuf(nc, memory, "sig_w", [P, 2, RT, T])
        a_gate = sbuf(nc, memory, "a_gate", [P, 2, RT, T])
        kappa = sbuf(nc, memory, "kappa", [P, RT, T])
        sq = sbuf(nc, memory, "key_squares", [P, RT, T])
        total = sbuf(nc, memory, "decay_sum", [P, 2, RT, T])
        before = sbuf(nc, memory, "decay_before", [P, 2, RT, T])
        norm = before[:, 1]
        mid = sbuf(nc, memory, "decay_mid", [P, 2, RT, NT])
        nmid = sbuf(nc, memory, "decay_negmid", [P, 2, RT, NT])
        grow, back, shrx = R["r"], R["b"], R["a"]
        one_k = sbuf(nc, memory, "one_minus_ka", [P, RT])
        carry_in = sbuf(nc, memory, "carry_exponent", [P, 2, RT])

        units = [("g", 0, c) for c in (0, 2)] + [(kind, d, c) for d in range(2) for kind in "wa" for c in (0, 2)]
        FIRST = (0, 1)
        END = (P - 1, P)

        with nc.Block() as block:
            @block.vector
            def _(dve):
                step = chain(dve, dve_step)
                step(nc.vector.tensor_tensor(c0[:, :], W["mu_prev"], W["mu_next"], ALU.add))
                step(nc.vector.tensor_scalar(c0[:, :], c0[:, :], -1.0, 1.0, ALU.mult, ALU.add))
                order = [LORA, GATE] + list(range(3 * RT))
                for i, (part, to) in enumerate(((order[:2], 1), (order[2:], 2))):
                    for c in part:
                        last = nc.vector.tensor_scalar(mixed[:, c, :], u[:, c, 1:T + 1], c0[:, c:c + 1], None, ALU.mult)
                    step(last)
                    for c in part:
                        last = nc.vector.scalar_tensor_tensor(mixed[:, c, :], u[:, c, 0:T], W["mu_prev"][:, c:c + 1],
                                                              mixed[:, c, :], ALU.mult, ALU.add)
                    step(last)
                    for c in part:
                        last = nc.vector.scalar_tensor_tensor(mixed[:, c, :], u[:, c, 2:T + 2],
                                                              W["mu_next"][:, c:c + 1], mixed[:, c, :],
                                                              ALU.mult, ALU.add)
                    last.then_inc(mixed_done, 1)
                    dve.wait_ge(mixed_done, to)
                for c in range(RT):
                    last = nc.vector.tensor_scalar(kappa[:, c, :], k[:, c, :], W["k_k"][:, c:c + 1], None, ALU.mult)
                step(last)
                nc.vector.tensor_tensor(sq[:, :, :], kappa[:, :, :], kappa[:, :, :], ALU.mult).then_inc(key_sq, 1)
                step(nc.vector.tensor_scalar(one_k[:, :], W["k_a"], -1.0, 1.0, ALU.mult, ALU.add))
                dve.wait_ge(norm_done, 1)
                step(nc.vector.tensor_scalar(norm[:, :, :], norm[:, :, :], 1e-12, None, ALU.max))
                step(nc.vector.reciprocal(norm[:, :, :], norm[:, :, :]))
                nc.vector.tensor_tensor(kappa[:, :, :], kappa[:, :, :], norm[:, :, :], ALU.mult).then_inc(kappa_done, 1)
                for d in range(2):
                    dve.wait_ge(unit_act, 4 + 4 * d)
                    for c in range(RT):
                        for a in range(NT):
                            src, dst = sig_w[:, d, c, a * P:(a + 1) * P], total[:, d, c, a * P:(a + 1) * P]
                            if d:
                                src, dst = src[:, ::-1], dst[:, ::-1]
                            last = nc.vector.tensor_tensor_scan(dst, C["ones"], src, 0.0, ALU.mult, ALU.add)
                    step(last)
                    nc.vector.tensor_tensor(before[:, d, :, :], total[:, d, :, :], sig_w[:, d, :, :], ALU.subtract)
                    m = P // 2 - 1 if d == 0 else P // 2
                    by_chunk = total[:, d, :, :].rearrange("p c (a n) -> p c a n", n=P)
                    step(nc.vector.tensor_scalar(mid[:, d, :, :], by_chunk[:, :, :, m], DECAY, None, ALU.mult))
                    step(nc.vector.tensor_scalar(nmid[:, d, :, :], mid[:, d, :, :], -1.0, None, ALU.mult))
                    f = FIRST[d]
                    step(nc.vector.tensor_tensor(carry_in[:, d, :], mid[:, d, :, f], mid[:, d, :, 1 - f], ALU.subtract))
                    nc.vector.scalar_tensor_tensor(carry_in[:, d, :], total[:, d, :, END[d]], -DECAY, carry_in[:, d, :],
                                                   ALU.mult, ALU.add).then_inc(scan_done, 1)
                for d in range(2):
                    dve.wait_ge(unit_act, 6 + 4 * d)
                    dve.wait_ge(exp_done, 2 * d + 1)
                    dve.wait_ge(kappa_done, 1)
                    step(nc.vector.tensor_tensor(sq[:, :, :], kappa[:, :, :], a_gate[:, d, :, :], ALU.mult))
                    for c in range(RT):
                        last = nc.vector.tensor_scalar(a_gate[:, d, c, :], a_gate[:, d, c, :], W["k_a"][:, c:c + 1],
                                                       one_k[:, c:c + 1], ALU.mult, ALU.add)
                    step(last)
                    step(nc.vector.tensor_tensor(a_gate[:, d, :, :], a_gate[:, d, :, :], k, ALU.mult))
                    step(nc.vector.tensor_tensor(R["k"][:, d, :, :], a_gate[:, d, :, :], back[:, d, :, :], ALU.mult))
                    step(nc.vector.tensor_tensor(R["b"][:, d, :, :], sq[:, :, :], back[:, d, :, :], ALU.mult))
                    nc.vector.tensor_tensor(R["r"][:, d, :, :], r, grow[:, d, :, :], ALU.mult)
                    nc.vector.scalar_tensor_tensor(R["a"][:, d, :, :], kappa[:, :, :], -1.0, shrx[:, d, :, :],
                                                   ALU.mult, ALU.mult).then_inc(kb_ready, 1)
                step(nc.vector.tensor_tensor(sq[:, :, :], a_gate[:, 0, :, :], a_gate[:, 1, :, :], ALU.add))
                step(nc.vector.tensor_tensor(sq[:, :, :], sq[:, :, :], r, ALU.mult))
                for c in range(RT):
                    last = nc.vector.tensor_scalar(sq[:, c, :], sq[:, c, :], W["r_k"][:, c:c + 1], None, ALU.mult)
                last.then_inc(bonus_in, 1)
                dve.wait_ge(bonus_done, 1)
                nc.vector.tensor_tensor(R["bonus"][:, :, :], PS[:, 0:2, :].rearrange("p b (c t) -> p (b c) t", t=T), v,
                                        ALU.mult)

            @block.scalar
            def _(act):
                step = chain(act, act_step)
                act.wait_ge(mixed_done, 1)
                nc.scalar.activation(tanh_w[0:HD, :], mixed[0:HD, LORA, :], ACT.Tanh)
                nc.scalar.activation(sig_g[:, :], mixed[:, GATE, :], ACT.Sigmoid).then_inc(lora_ready, 1)
                for n, (kind, d, c) in enumerate(units):
                    act.wait_ge(unit_done, n + 1)
                    for h in range(2):
                        src = PS[:, n % BANKS, h * T:(h + 1) * T]
                        i = d * RT + c + h
                        if kind == "g":
                            last = nc.scalar.activation(R["gate"][:, c + h, :], src, ACT.Copy)
                        elif kind == "w":
                            last = nc.scalar.activation(sig_w[:, d, c + h, :], src, ACT.Sigmoid,
                                                        bias=W["w_decay0"][:, i:i + 1])
                        else:
                            last = nc.scalar.activation(a_gate[:, d, c + h, :], src, ACT.Sigmoid,
                                                        bias=W["a_gate0"][:, i:i + 1])
                    last.then_inc(unit_act, 1)
                act.wait_ge(norm_sq, 1)
                nc.scalar.activation(norm[:, :, :], PS[:, 4:6, :].rearrange("p b (c t) -> p (b c) t", t=T),
                                     ACT.Sqrt).then_inc(norm_done, 1)
                for d in range(2):
                    act.wait_ge(scan_done, d + 1)
                    for c in range(RT):
                        for a in range(NT):
                            s = slice(a * P, (a + 1) * P)
                            nc.scalar.activation(grow[:, d, c, s], total[:, d, c, s], ACT.Exp, scale=-DECAY,
                                                 bias=mid[:, d, c, a:a + 1])
                            nc.scalar.activation(back[:, d, c, s], total[:, d, c, s], ACT.Exp, scale=DECAY,
                                                 bias=nmid[:, d, c, a:a + 1])
                            last = nc.scalar.activation(shrx[:, d, c, s], before[:, d, c, s], ACT.Exp, scale=-DECAY,
                                                        bias=mid[:, d, c, a:a + 1])
                    last.then_inc(exp_done, 1)
                    nc.scalar.activation(R["carry"][:, d, :], carry_in[:, d, :], ACT.Exp).then_inc(exp_done, 1)
                act.wait_ge(v_done, 1)
                nc.scalar.activation(R["v_rows"][:, :, :], PS[:, 2:4, :], ACT.Copy)
                for d in range(2):
                    act.wait_ge(kb_rows, d + 1)
                    nc.scalar.activation(R["b_rows"][:, d, :], PS[:, 6, :], ACT.Copy)
                    nc.scalar.activation(R["k_rows"][:, d, :], PS[:, 7, :], ACT.Copy).then_inc(rows_out, 1)

            @block.tensor
            def _(pe):
                pe.wait_ge(lora_ready, 1)
                for n, (kind, d, c) in enumerate(units):
                    if n >= BANKS:
                        pe.wait_ge(unit_act, n - BANKS + 1)
                    for h in range(2):
                        out, s = PS[:, n % BANKS, h * T:(h + 1) * T], slice((c + h) * P, (c + h + 1) * P)
                        if kind == "g":
                            last = nc.tensor.matmul(out, W["g_up"][:, s], sig_g[:, :], start=True, stop=True)
                        elif kind == "w":
                            last = nc.tensor.matmul(out, W["lora_up"][0:HD, d, s], tanh_w[0:HD, :],
                                                    start=True, stop=True)
                        else:
                            last = nc.tensor.matmul(out, W["lora_up"][HD:P, d, s], mixed[HD:P, LORA, :],
                                                    start=True, stop=True)
                    last.then_inc(unit_done, 1)
                pe.wait_ge(key_sq, 1)
                pe.wait_ge(unit_act, len(units))
                for c in range(RT):
                    last = nc.tensor.matmul(PS[:, 4 + c // 2, (c % 2) * T:(c % 2 + 1) * T], C["head_ones"], sq[:, c, :],
                                            start=True, stop=True)
                last.then_inc(norm_sq, 1)
                pe.wait_ge(mixed_done, 2)
                for a in range(NT):
                    for c in range(RT):
                        last = nc.tensor.transpose(PS[:, 2 + a, c * P:(c + 1) * P], v[:, c, a * P:(a + 1) * P],
                                                   C["ident"])
                last.then_inc(v_done, 1)
                for d in range(2):
                    pe.wait_ge(kb_ready, d + 1)
                    if d:
                        pe.wait_ge(rows_out, d)
                    s = slice(FIRST[d] * P, (FIRST[d] + 1) * P)
                    for c in range(RT):
                        nc.tensor.transpose(PS[:, 6, c * P:(c + 1) * P], R["b"][:, d, c, s], C["ident"])
                        last = nc.tensor.transpose(PS[:, 7, c * P:(c + 1) * P], R["k"][:, d, c, s], C["ident"])
                    last.then_inc(kb_rows, 1)
                pe.wait_ge(bonus_in, 1)
                for c in range(RT):
                    last = nc.tensor.matmul(PS[:, c // 2, (c % 2) * T:(c % 2 + 1) * T], C["head_ones"], sq[:, c, :],
                                            start=True, stop=True)
                last.then_inc(bonus_done, 1)


def rwkv_scan(nc, S):
    PS, C, R = S["psum"], S["const"], S["rwkv"]
    pairs = [[(d, t, g) for g in range(2)] for d, t in ((0, 0), (1, 1), (0, 1), (1, 0))]
    NL = len(LEVELS) - 1

    with phase(nc, "dve_step products_done l_copied first_done w_done w_copied x_done x_added masked cross_done cross_copied "
                   "rhs_done rhs_copied u_done u_copied state_done state_scaled y_done y_added") as (
            memory, dve_step, products_done, l_copied, first_done, w_done, w_copied, x_done, x_added, masked, cross_done,
            cross_copied, rhs_done, rhs_copied, u_done, u_copied, state_done, state_scaled, y_done, y_added):
        between = sbuf(nc, memory, "between", [P, 2, NL, BANK])
        low = sbuf(nc, memory, "low", [P, 2, BANK])
        x = sbuf(nc, memory, "inv_t", [P, 2, BANK])
        xt = sbuf(nc, memory, "inv", [P, 2, BANK])
        w = sbuf(nc, memory, "half_w", [P, 2, BANK])
        lak = sbuf(nc, memory, "lak", [P, 2, BANK])
        mrb = sbuf(nc, memory, "mrb", [P, 2, BANK])
        mrk = sbuf(nc, memory, "mrk", [P, 2, BANK])
        rhs = sbuf(nc, memory, "rhs", [P, 2, 4 * HD])
        uu = sbuf(nc, memory, "uu", [P, 2, 4 * HD])
        state = sbuf(nc, memory, "state", [P, 2, RT, HD])

        def four(ap):
            return ap.rearrange("p (i n) -> p i n", n=P)

        def mask(name):
            return C[name].unsqueeze(1).to_broadcast([P, 4, P])

        def head(g, i):
            h = 2 * i + g
            return i, slice(g * HD, (g + 1) * HD), slice(h * HD, (h + 1) * HD)

        with nc.Block() as block:
            @block.tensor
            def _(pe):
                for n, pair in enumerate(pairs):
                    first = n < 2
                    for q, (d, t, g) in enumerate(pair):
                        m = 2 * n + q
                        if m >= 2:
                            pe.wait_ge(y_added, m - 1)
                            pe.wait_ge(u_copied, m - 1)
                        ts = slice(t * P, (t + 1) * P)
                        for i in range(4):
                            c, rows, _ = head(g, i)
                            s = slice(i * P, (i + 1) * P)
                            a_, b_ = R["a"][rows, d, c, ts], R["b"][rows, d, c, ts]
                            nc.tensor.matmul(PS[:, 4 * q, s], a_, b_, start=True, stop=True)
                            last = nc.tensor.matmul(PS[:, 4 * q + 1, s], b_, a_, start=True, stop=True)
                        last.then_inc(products_done, 1)
                    for j in range(3):
                        for q, (d, t, g) in enumerate(pair):
                            m = 2 * n + q
                            if j:
                                pe.wait_ge(cross_copied, 3 * 2 * n + 2 * (j - 1) + q + 1)
                            ts = slice(t * P, (t + 1) * P)
                            for i in range(4):
                                c, rows, _ = head(g, i)
                                one, two = (("k", "a"), ("b", "r"), ("k", "r"))[j]
                                last = nc.tensor.matmul(PS[:, 4 * q + 3, i * P:(i + 1) * P], R[one][rows, d, c, ts],
                                                        R[two][rows, d, c, ts], start=True, stop=True)
                            last.then_inc(cross_done, 1)
                    for l in range(NL):
                        for q in range(2):
                            m = 2 * n + q
                            if l == 0:
                                pe.wait_ge(first_done, m + 1)
                                pe.wait_ge(masked, NL * 2 * n + q + 1)
                                pe.wait_ge(l_copied, m + 1)
                            else:
                                pe.wait_ge(masked, NL * 2 * n + 2 * l + q + 1)
                                pe.wait_ge(x_added, NL * 2 * n + 2 * (l - 1) + q + 1)
                            for i in range(4):
                                s = slice(i * P, (i + 1) * P)
                                last = nc.tensor.matmul(PS[:, 4 * q, s], between[:, q, l, s], x[:, q, s],
                                                        start=True, stop=True)
                            last.then_inc(w_done, 1)
                        for q in range(2):
                            pe.wait_ge(w_copied, NL * 2 * n + 2 * l + q + 1)
                            for i in range(4):
                                s = slice(i * P, (i + 1) * P)
                                nc.tensor.matmul(PS[:, 4 * q + 1, s], xt[:, q, s], w[:, q, s], start=True, stop=True)
                                last = nc.tensor.matmul(PS[:, 4 * q + 2, s], w[:, q, s], xt[:, q, s],
                                                        start=True, stop=True)
                            last.then_inc(x_done, 1)
                    for q, (d, t, g) in enumerate(pair):
                        m = 2 * n + q
                        ts = slice(t * P, (t + 1) * P)
                        pe.wait_ge(cross_copied, 3 * 2 * (n + 1) - 2 + q + 1)
                        pe.wait_ge(x_added, NL * 2 * (n + 1) - 2 + q + 1)
                        if not first:
                            pe.wait_ge(state_scaled, 2 * (n - 2) + q + 1)
                        for i in range(4):
                            c, rows, cols = head(g, i)
                            o = PS[:, 4 * q, i * HD:(i + 1) * HD]
                            last = nc.tensor.matmul(o, lak[:, q, i * P:(i + 1) * P], R["v_rows"][:, t, cols],
                                                    start=True, stop=first)
                            if not first:
                                last = nc.tensor.matmul(o, R["a"][rows, d, c, ts], state[rows, d, c, :],
                                                        start=False, stop=True)
                        last.then_inc(rhs_done, 1)
                    for q in range(2):
                        m = 2 * n + q
                        pe.wait_ge(rhs_copied, m + 1)
                        for i in range(4):
                            last = nc.tensor.matmul(PS[:, 4 * q + 1, i * HD:(i + 1) * HD], x[:, q, i * P:(i + 1) * P],
                                                    rhs[:, q, i * HD:(i + 1) * HD], start=True, stop=True)
                        last.then_inc(u_done, 1)
                    for q, (d, t, g) in enumerate(pair):
                        m = 2 * n + q
                        pe.wait_ge(u_copied, m + 1)
                        ts = slice(t * P, (t + 1) * P)
                        for i in range(4):
                            c, rows, cols = head(g, i)
                            if first:
                                o = PS[rows, 4 * q + 2, i * HD:(i + 1) * HD]
                                nc.tensor.matmul(o, R["b_rows"][:, d, cols], uu[:, q, i * HD:(i + 1) * HD],
                                                 start=True, stop=False)
                                last = nc.tensor.matmul(o, R["k_rows"][:, d, cols], R["v_rows"][:, t, cols],
                                                        start=False, stop=True)
                        if first:
                            last.then_inc(state_done, 1)
                        for i in range(4):
                            c, rows, cols = head(g, i)
                            o = PS[rows, 4 * q + 3, i * P:(i + 1) * P]
                            nc.tensor.matmul(o, uu[:, q, i * HD:(i + 1) * HD], mrb[:, q, i * P:(i + 1) * P],
                                             start=True, stop=False)
                            last = nc.tensor.matmul(o, R["v_rows"][:, t, cols], mrk[:, q, i * P:(i + 1) * P],
                                                    start=False, stop=first)
                            if not first:
                                last = nc.tensor.matmul(o, state[rows, d, c, :], R["r"][rows, d, c, ts],
                                                        start=False, stop=True)
                        last.then_inc(y_done, 1)

            @block.scalar
            def _(act):
                for n, pair in enumerate(pairs):
                    for q in range(2):
                        act.wait_ge(products_done, 2 * n + q + 1)
                        if n:
                            act.wait_ge(masked, NL * 2 * n)
                            act.wait_ge(first_done, 2 * n)
                        nc.scalar.activation(low[:, q, :], PS[:, 4 * q, :], ACT.Copy).then_inc(l_copied, 1)
                    for l in range(NL):
                        for q in range(2):
                            act.wait_ge(w_done, NL * 2 * n + 2 * l + q + 1)
                            nc.scalar.activation(w[:, q, :], PS[:, 4 * q, :], ACT.Copy).then_inc(w_copied, 1)
                    for q in range(2):
                        act.wait_ge(rhs_done, 2 * n + q + 1)
                        nc.scalar.activation(rhs[:, q, :], PS[:, 4 * q, 0:4 * HD], ACT.Copy).then_inc(rhs_copied, 1)
                    for q in range(2):
                        act.wait_ge(u_done, 2 * n + q + 1)
                        nc.scalar.activation(uu[:, q, :], PS[:, 4 * q + 1, 0:4 * HD], ACT.Copy).then_inc(u_copied, 1)
                    if n < 2:
                        for q, (d, t, g) in enumerate(pair):
                            act.wait_ge(state_done, 2 * n + q + 1)
                            for i in range(4):
                                c, rows, _ = head(g, i)
                                last = nc.scalar.activation(state[rows, d, c, :],
                                                            PS[rows, 4 * q + 2, i * HD:(i + 1) * HD],
                                                            ACT.Copy, scale=R["carry"][rows, d, c:c + 1])
                            last.then_inc(state_scaled, 1)

            @block.gpsimd
            def _(pool):
                for n, pair in enumerate(pairs):
                    for l in range(NL):
                        for q, (d, t, g) in enumerate(pair):
                            if l == 0:
                                pool.wait_ge(l_copied, 2 * n + q + 1)
                            if n:
                                pool.wait_ge(w_done, NL * 2 * (n - 1) + 2 * l + q + 1)
                            name = ("low", "up")[d] + str(LEVELS[l + 1])
                            nc.gpsimd.tensor_tensor(four(between[:, q, l, :]), four(low[:, q, :]), mask(name),
                                                    ALU.mult).then_inc(masked, 1)

            @block.vector
            def _(dve):
                step = chain(dve, dve_step)
                for n, pair in enumerate(pairs):
                    for q, (d, t, g) in enumerate(pair):
                        m = 2 * n + q
                        dve.wait_ge(products_done, m + 1)
                        lo, up = (("low1", "up1"), ("up1", "low1"))[d]
                        dve.wait_ge(l_copied, m + 1)
                        nc.vector.tensor_tensor(four(xt[:, q, :]), four(low[:, q, :]), mask(lo), ALU.mult)
                        step(nc.vector.tensor_tensor(four(x[:, q, :]), four(PS[:, 4 * q + 1, :]), mask(up), ALU.mult))
                        step(nc.vector.tensor_tensor(four(xt[:, q, :]), four(xt[:, q, :]), mask("ident"), ALU.add))
                        nc.vector.tensor_tensor(four(x[:, q, :]), four(x[:, q, :]), mask("ident"),
                                                ALU.add).then_inc(first_done, 1)
                    for j in range(3):
                        for q, (d, t, g) in enumerate(pair):
                            dve.wait_ge(cross_done, 3 * 2 * n + 2 * j + q + 1)
                            name = (("p<q", "p<=q", "p<=q"), ("p>q", "p>=q", "p>=q"))[d][j]
                            nc.vector.tensor_tensor(four((lak, mrb, mrk)[j][:, q, :]), four(PS[:, 4 * q + 3, :]),
                                                    mask(name), ALU.mult).then_inc(cross_copied, 1)
                    for l in range(NL):
                        for q in range(2):
                            dve.wait_ge(x_done, NL * 2 * n + 2 * l + q + 1)
                            nc.vector.tensor_tensor(xt[:, q, :], xt[:, q, :], PS[:, 4 * q + 2, :], ALU.add)
                            nc.vector.tensor_tensor(x[:, q, :], x[:, q, :], PS[:, 4 * q + 1, :],
                                                    ALU.add).then_inc(x_added, 1)
                    for q, (d, t, g) in enumerate(pair):
                        dve.wait_ge(y_done, 2 * n + q + 1)
                        rows = head(g, 0)[1]
                        out = R["y"][rows, :, t * P:(t + 1) * P]
                        src = PS[rows, 4 * q + 3, :].rearrange("p (c t) -> p c t", t=P)
                        if n < 2:
                            nc.vector.tensor_copy(out, src).then_inc(y_added, 1)
                        else:
                            dve.wait_ge(y_added, 4)
                            nc.vector.tensor_tensor(out, out, src, ALU.add).then_inc(y_added, 1)


def rwkv_finish(nc, S):
    PS, C, W, R = S["psum"], S["const"], S["weights"], S["rwkv"]
    y = R["y"]
    flat = "p b (c t) -> p (b c) t"
    with phase(nc, "dve_step mean_done centred squared var_done root_done") as (
            memory, dve_step, mean_done, centred, squared, var_done, root_done):
        sq = sbuf(nc, memory, "gn_squares", [P, RT, T])
        root = sbuf(nc, memory, "gn_root", [P, RT, T])
        eps = sbuf(nc, memory, "gn_eps", [P, 1])

        with nc.Block() as block:
            @block.tensor
            def _(pe):
                for c in range(RT):
                    last = nc.tensor.matmul(PS[:, c // 2, (c % 2) * T:(c % 2 + 1) * T], C["head_ones"], y[:, c, :],
                                            start=True, stop=True)
                last.then_inc(mean_done, 1)
                pe.wait_ge(squared, 1)
                for c in range(RT):
                    last = nc.tensor.matmul(PS[:, 2 + c // 2, (c % 2) * T:(c % 2 + 1) * T], C["head_ones"], sq[:, c, :],
                                            start=True, stop=True)
                last.then_inc(var_done, 1)

            @block.scalar
            def _(act):
                act.wait_ge(centred, 1)
                nc.scalar.activation(sq[:, :, :], y[:, :, :], ACT.Square).then_inc(squared, 1)
                act.wait_ge(var_done, 1)
                nc.scalar.activation(root[:, :, :], PS[:, 2:4, :].rearrange(flat, t=T), ACT.Sqrt, scale=1.0 / HD,
                                     bias=eps[:, 0:1]).then_inc(root_done, 1)
                nc.scalar.activation(S["gates"][:, :, :], S["gates"][:, :, :], ACT.Sigmoid)

            @block.vector
            def _(dve):
                step = chain(dve, dve_step)
                step(nc.vector.memset(eps[:, :], GN_EPS))
                dve.wait_ge(mean_done, 1)
                nc.vector.scalar_tensor_tensor(y[:, :, :], PS[:, 0:2, :].rearrange(flat, t=T), -1.0 / HD, y[:, :, :],
                                               ALU.mult, ALU.add).then_inc(centred, 1)
                dve.wait_ge(root_done, 1)
                step(nc.vector.reciprocal(root[:, :, :], root[:, :, :]))
                step(nc.vector.tensor_tensor(root[:, :, :], root[:, :, :], y[:, :, :], ALU.mult))
                for c in range(RT):
                    last = nc.vector.tensor_scalar(root[:, c, :], root[:, c, :], W["gn_w"][:, c:c + 1],
                                                   W["gn_b"][:, c:c + 1], ALU.mult, ALU.add)
                step(last)
                step(nc.vector.tensor_tensor(root[:, :, :], root[:, :, :], R["bonus"][:, :, :], ALU.add))
                nc.vector.tensor_tensor(y[:, :, :], root[:, :, :], R["gate"][:, :, :], ALU.mult)



def attention(nc, S):
    PS, C, W = S["psum"], S["const"], S["weights"]
    qkv = S["qkv"]
    NH = 2 * AH
    scale = HD ** -0.5
    work = [(s, a) for s in range(SLOTS) for a in range(NT)]

    with phase(nc, "merge_in dve_step act_step squared mean_sq root_done normed angles sines transposed copied scores_done "
                   "max_done exp_done probs_t probs_copied_act probs_copied_dve out_done out_scaled out_t") as (
            memory, merge_in, dve_step, act_step, squared, mean_sq, root_done, normed, angles, sines, transposed, copied,
            scores_done, max_done, exp_done, probs_t, probs_copied_act, probs_copied_dve, out_done, out_scaled,
            out_t):
        sq = sbuf(nc, memory, "qk_squares", [P, NT, 2 * AC])
        ss = sbuf(nc, memory, "qk_sums", [P, NT, NH])
        pos = sbuf(nc, memory, "pos", [P, NT])
        ang = sbuf(nc, memory, "angle", [P, 2, NT, ROT // 2])
        turns = sbuf(nc, memory, "turns", [P, 2, NT, ROT // 2])
        turns_i = sbuf(nc, memory, "turns_int", [P, 2, NT, ROT // 2], I32)
        sc = sbuf(nc, memory, "sin_cos", [P, 2, NT, ROT // 2])
        rot = sbuf(nc, memory, "rotated", [P, 4, NH, ROT // 2])
        qk_t = sbuf(nc, memory, "qk_t", [P, NH // 2, T])
        scores = sbuf(nc, memory, "scores", [P, 2, GROUPS, T])
        probs_sb = sbuf(nc, memory, "probs_t", [P, 2, 2 * GROUPS, P])
        top = sbuf(nc, memory, "score_max", [P, 2, len(work)])
        den = sbuf(nc, memory, "den", [P, 2, len(work)])
        out = sbuf(nc, memory, "attn_rows", [P, NT, SLOTS * HD])
        TWO_PI = 2 * math.pi
        p1 = 6.28125
        p2 = float(np.float32(np.floor((TWO_PI - p1) * 2 ** 20) / 2 ** 20))
        p3 = TWO_PI - p1 - p2

        with nc.Block() as block:
            @block.sync
            def _(sp):
                sp.dma_start(S["w_rwkv_out"][:, :, :], S["dram"]["w_rwkv_out"].rearrange("(k p) n -> p k n", p=P)).then_inc(merge_in, 16)
                sp.dma_start(S["w_attn_out"][:, :, :], S["dram"]["w_attn_out"].rearrange("(k p) n -> p k n", p=P)).then_inc(merge_in, 16)
                sp.dma_start(S["w_out"][:, :, :], S["dram"]["w_out"].rearrange("(k p) n -> p k n", p=P)).then_inc(merge_in, 16)
                sp.wait_ge(merge_in, 48)

            @block.scalar
            def _(act):
                step = chain(act, act_step)
                nc.scalar.activation(sq[:, :, :], qkv[:, :, 0:2 * AC], ACT.Square).then_inc(squared, 1)
                act.wait_ge(angles, 1)
                nc.scalar.activation(sc[:, :, :, :], ang[:, :, :, :], ACT.Sin).then_inc(sines, 1)
                act.wait_ge(mean_sq, 1)
                nc.scalar.activation(ss[:, :, :], ss[:, :, :], ACT.Sqrt).then_inc(root_done, 1)
                for a in range(NT):
                    act.wait_ge(transposed, 3 * (a + 1))
                    for b in range(3):
                        last = nc.scalar.activation(qk_t[:, 4 * b:4 * b + 4, a * P:(a + 1) * P],
                                                    PS[:, 3 * a + b, :].rearrange("p (c t) -> p c t", t=P), ACT.Copy)
                    last.then_inc(copied, 1)
                for n, (s, a) in enumerate(work):
                    act.wait_ge(max_done, n + 1)
                    nc.scalar.activation(scores[:, n % 2, :, :], scores[:, n % 2, :, :], ACT.Exp, scale=scale,
                                         bias=top[:, 1, n:n + 1], accum_out=den[:, 0, n:n + 1]).then_inc(exp_done, 1)
                    act.wait_ge(probs_t, n + 1)
                    nc.scalar.activation(probs_sb[:, n % 2, 0:4, :],
                                         PS[:, 4 + n % 2, :].rearrange("p (c t) -> p c t", t=P),
                                         ACT.Copy).then_inc(probs_copied_act, 1)
                act.wait_ge(out_t, 1)
                nc.scalar.activation(S["attn_cols"][:, :, :], PS[:, 0, :].rearrange("p (c t) -> p c t", t=T), ACT.Copy)

            @block.vector
            def _(dve):
                step = chain(dve, dve_step)
                step(nc.vector.tensor_copy(pos[:, :], W["positions"]))
                for a in range(NT):
                    nc.vector.tensor_scalar(ang[:, 0, a, :], C["inv_freq"], pos[:, a:a + 1], None, ALU.mult)
                    last = nc.vector.tensor_scalar(ang[:, 1, a, :], C["inv_freq"], pos[:, a:a + 1], None, ALU.mult)
                step(last)
                step(nc.vector.tensor_scalar(turns[:, 0], ang[:, 0], 1 / TWO_PI, None, ALU.mult))
                step(nc.vector.tensor_scalar(turns[:, 1], ang[:, 1], 1 / TWO_PI, 0.25, ALU.mult, ALU.add))
                step(nc.vector.tensor_copy(turns_i[:, :, :, :], turns[:, :, :, :]))
                step(nc.vector.tensor_copy(turns[:, :, :, :], turns_i[:, :, :, :]))
                for part in (p1, p2, p3):
                    step(nc.vector.scalar_tensor_tensor(ang[:, :, :, :], turns[:, :, :, :], -part, ang[:, :, :, :],
                                                        ALU.mult, ALU.add))
                step(nc.vector.tensor_scalar(ang[:, 1], ang[:, 1], math.pi / 2, None, ALU.add))
                for above, by in ((math.pi, -TWO_PI), (-math.pi, TWO_PI)):
                    op = ALU.is_gt if above > 0 else ALU.is_lt
                    step(nc.vector.tensor_scalar(turns[:, :, :, :], ang[:, :, :, :], above, by, op, ALU.mult))
                    step(nc.vector.tensor_tensor(ang[:, :, :, :], ang[:, :, :, :], turns[:, :, :, :], ALU.add))
                nc.vector.tensor_scalar(ang[:, :, :, :], ang[:, :, :, :], 3.1415925, -3.1415925, ALU.min,
                                        ALU.max).then_inc(angles, 1)
                dve.wait_ge(squared, 1)
                for a in range(NT):
                    last = nc.vector.tensor_reduce(ss[:, a, :], sq[:, a, :].rearrange("p (h d) -> p h d", d=HD), X,
                                                   ALU.add)
                step(last)
                nc.vector.tensor_scalar(ss[:, :, :], ss[:, :, :], 1.0 / HD, NORM_EPS, ALU.mult,
                                        ALU.add).then_inc(mean_sq, 1)
                dve.wait_ge(root_done, 1)
                step(nc.vector.reciprocal(ss[:, :, :], ss[:, :, :]))
                dve.wait_ge(sines, 1)
                for a in range(NT):
                    v = qkv[:, a, 0:2 * AC].rearrange("p (h d) -> p h d", d=HD)
                    step(nc.vector.tensor_tensor(v, v, ss[:, a, :].unsqueeze(2).to_broadcast([P, NH, HD]), ALU.mult))
                    for i, g in enumerate((W["q_norm_g"], W["k_norm_g"])):
                        part = v[:, i * AH:(i + 1) * AH, :]
                        last = nc.vector.tensor_tensor(part, part, g.unsqueeze(1).to_broadcast([P, AH, HD]), ALU.mult)
                    step(last)
                    t1, t2 = v[:, :, 0:ROT // 2], v[:, :, ROT // 2:ROT]
                    sin = sc[:, 0, a, :].unsqueeze(1).to_broadcast([P, NH, ROT // 2])
                    cos = sc[:, 1, a, :].unsqueeze(1).to_broadcast([P, NH, ROT // 2])
                    for i, (x1, f) in enumerate(((t1, cos), (t2, sin), (t2, cos), (t1, sin))):
                        last = nc.vector.tensor_tensor(rot[:, i, :, :], x1, f, ALU.mult)
                    step(last)
                    nc.vector.tensor_tensor(t1, rot[:, 0, :, :], rot[:, 1, :, :], ALU.subtract)
                    nc.vector.tensor_tensor(t2, rot[:, 2, :, :], rot[:, 3, :, :], ALU.add).then_inc(normed, 1)
                    dve.wait_ge(normed, a + 1)
                def finish(n):
                    s, a = work[n]
                    dve.wait_ge(probs_t, n + 1)
                    nc.vector.tensor_copy(probs_sb[:, n % 2, 4:6, :],
                                          PS[:, 6, 2 * P * (n % 2):2 * P * (n % 2 + 1)].rearrange("p (c t) -> p c t", t=P)
                                          ).then_inc(probs_copied_dve, 1)
                    step(nc.vector.reciprocal(den[:, 1, n:n + 1], den[:, 0, n:n + 1]))
                    dve.wait_ge(out_done, n + 1)
                    nc.vector.tensor_scalar(out[:, a, s * HD:(s + 1) * HD], PS[:, 7, (n % 2) * HD:(n % 2 + 1) * HD],
                                            den[:, 1, n:n + 1], None, ALU.mult).then_inc(out_scaled, 1)

                for n, (s, a) in enumerate(work):
                    dve.wait_ge(scores_done, n + 1)
                    src = PS[:, 2 * (n % 2):2 * (n % 2) + 2, :].rearrange("p b (g t) -> p (b g) t", t=T)[:, 0:GROUPS, :]
                    if n >= 2:
                        dve.wait_ge(probs_t, n - 1)
                    step(nc.vector.tensor_tensor(scores[:, n % 2, :, :], src, C["band"][:, a], ALU.add))
                    step(nc.vector.tensor_reduce(top[:, 0, n:n + 1], scores[:, n % 2, :, :].rearrange("p g t -> p (g t)"),
                                                 X, ALU.max))
                    nc.vector.tensor_scalar(top[:, 1, n:n + 1], top[:, 0, n:n + 1], -scale, None,
                                            ALU.mult).then_inc(max_done, 1)
                    if n:
                        finish(n - 1)
                finish(len(work) - 1)

            @block.tensor
            def _(pe):
                for a in range(NT):
                    pe.wait_ge(normed, a + 1)
                    for b in range(3):
                        for c in range(4):
                            last = nc.tensor.transpose(PS[:, 3 * a + b, c * P:(c + 1) * P],
                                                       qkv[:, a, (4 * b + c) * P:(4 * b + c + 1) * P], C["ident"])
                        last.then_inc(transposed, 1)

                def score(n):
                    s, a = work[n]
                    if n == 0:
                        pe.wait_ge(copied, NT)
                    if n >= 2:
                        pe.wait_ge(max_done, n - 1)
                    for g in range(GROUPS):
                        h = g * SLOTS + s
                        rows = slice((h % 2) * HD, (h % 2 + 1) * HD)
                        last = nc.tensor.matmul(PS[:, 2 * (n % 2) + g // 2, (g % 2) * T:(g % 2 + 1) * T],
                                                qk_t[rows, h // 2, a * P:(a + 1) * P], qk_t[rows, AH // 2 + h // 2, :],
                                                start=True, stop=True)
                    last.then_inc(scores_done, 1)

                score(0)
                for n, (s, a) in enumerate(work):
                    if n + 1 < len(work):
                        score(n + 1)
                    pe.wait_ge(exp_done, n + 1)
                    if n >= 2:
                        pe.wait_ge(probs_copied_act, n - 1)
                        pe.wait_ge(probs_copied_dve, n - 1)
                    for i in range(2 * GROUPS):
                        to = (PS[:, 4 + n % 2, i * P:(i + 1) * P] if i < 4 else
                              PS[:, 6, (2 * (n % 2) + i - 4) * P:(2 * (n % 2) + i - 3) * P])
                        last = nc.tensor.transpose(to, scores[:, n % 2, i // 2, (i % 2) * P:(i % 2 + 1) * P], C["ident"])
                    last.then_inc(probs_t, 1)
                    pe.wait_ge(probs_copied_act, n + 1)
                    pe.wait_ge(probs_copied_dve, n + 1)
                    if n:
                        pe.wait_ge(out_scaled, n)
                    for i in range(2 * GROUPS):
                        h = (i // 2) * SLOTS + s
                        c0 = 2 * AC + h * HD
                        last = nc.tensor.matmul(PS[:, 7, (n % 2) * HD:(n % 2 + 1) * HD], probs_sb[:, n % 2, i, :],
                                                qkv[:, i % 2, c0:c0 + HD], start=(i == 0), stop=(i == 2 * GROUPS - 1))
                    last.then_inc(out_done, 1)
                pe.wait_ge(out_scaled, len(work))
                for a in range(NT):
                    for c in range(2):
                        last = nc.tensor.transpose(PS[:, 0, c * T + a * P:c * T + (a + 1) * P],
                                                   out[:, a, c * P:(c + 1) * P], C["ident"])
                last.then_inc(out_t, 1)


def merge(nc, S):
    PS, R = S["psum"], S["rwkv"]
    gates = S["gates"]
    with phase(nc, "both_done gated added x_done") as (memory, both_done, gated, added, x_done):
        merged = sbuf(nc, memory, "merged", [P, KD, T])
        other = sbuf(nc, memory, "merged_attn", [P, KD, T])

        with nc.Block() as block:
            @block.tensor
            def _(pe):
                for k in range(KD):
                    if k >= 4:
                        pe.wait_ge(added, k - 3)
                    s = slice(k * P, (k + 1) * P)
                    for c in range(RT):
                        nc.tensor.matmul(PS[:, k % 4, 0:T], S["w_rwkv_out"][:, c, s], R["y"][:, c, :],
                                         start=(c == 0), stop=(c == RT - 1))
                    for c in range(2):
                        last = nc.tensor.matmul(PS[:, k % 4, T:2 * T], S["w_attn_out"][:, c, s],
                                                S["attn_cols"][:, c, :], start=(c == 0), stop=(c == 1))
                    last.then_inc(both_done, 1)
                pe.wait_ge(added, KD)
                for a in range(NT):
                    for h in range(2):
                        for k in range(KD):
                            last = nc.tensor.matmul(PS[:, 4 + 2 * a + h, :], merged[:, k, a * P:(a + 1) * P],
                                                    S["w_out"][:, k, h * BANK:(h + 1) * BANK],
                                                    start=(k == 0), stop=(k == KD - 1))
                        last.then_inc(x_done, 1)

            @block.vector
            def _(dve):
                for k in range(KD):
                    dve.wait_ge(both_done, k + 1)
                    nc.vector.tensor_tensor(merged[:, k, :], PS[:, k % 4, 0:T], gates[:, k, :], ALU.mult)
                    nc.vector.tensor_tensor(other[:, k, :], PS[:, k % 4, T:2 * T], gates[:, KD + k, :],
                                            ALU.mult).then_inc(gated, 1)
                    dve.wait_ge(gated, k + 1)
                    nc.vector.tensor_tensor(merged[:, k, :], merged[:, k, :], other[:, k, :],
                                            ALU.add).then_inc(added, 1)
                for a in range(NT):
                    for h in range(2):
                        dve.wait_ge(x_done, 2 * a + h + 1)
                        o = S["x"][:, a, h * BANK:(h + 1) * BANK]
                        nc.vector.tensor_tensor(o, o, PS[:, 4 + 2 * a + h, :], ALU.add)



def route(nc, S):
    PS, C, W = S["psum"], S["const"], S["weights"]
    N = MOE_GROUPS + EXPERTS
    with phase(nc, "dve_step logits_done exp_ready exp_done exp2_ready exp2_done chosen_done ranks_done") as (
            memory, dve_step, logits_done, exp_ready, exp_done, exp2_ready, exp2_done, chosen_done, ranks_done):
        logits = sbuf(nc, memory, "logits", [P, NT, N])
        grp = sbuf(nc, memory, "group_logits", [P, NT, 8])
        best = sbuf(nc, memory, "group_best", [P, NT, 8])
        index = sbuf(nc, memory, "group_index", [P, NT, 8], U32)
        chosen = sbuf(nc, memory, "group_chosen", [P, NT, 8])
        ex = sbuf(nc, memory, "group_exp", [P, NT, 8])
        gp = sbuf(nc, memory, "group_prob", [P, NT, 4])
        mine = sbuf(nc, memory, "expert_logits", [P, NT, EXPERTS])
        hot = sbuf(nc, memory, "expert_hot", [P, NT, 2, EXPERTS])
        picked = sbuf(nc, memory, "expert_picked", [P, NT, EXPERTS])
        over = sbuf(nc, memory, "expert_over", [P, EXPERTS])
        over_best = sbuf(nc, memory, "over_best", [P, 8])
        over_id = sbuf(nc, memory, "over_id", [P, 2, OVERFLOW])
        over_hot = sbuf(nc, memory, "over_hot", [P, OVERFLOW, EXPERTS])
        over_part = sbuf(nc, memory, "over_part", [P, NT, OVERFLOW, EXPERTS])
        top = sbuf(nc, memory, "expert_top", [P, NT, 8])
        ti = sbuf(nc, memory, "expert_top_i", [P, NT, 8], U32)
        tf = sbuf(nc, memory, "expert_top_f", [P, NT, 8])
        slots, shares = S["slots"], S["shares"]
        with nc.Block() as block:
            @block.tensor
            def _(pe):
                for a in range(NT):
                    for k in range(KD):
                        last = nc.tensor.matmul(PS[:, a, 0:N], S["h_cols"][:, k, a * P:(a + 1) * P],
                                                W["router"][:, k, :], start=(k == 0), stop=(k == KD - 1))
                last.then_inc(logits_done, 1)
                pe.wait_ge(chosen_done, 1)
                nc.tensor.matmul(PS[:, 2, 0:EXPERTS], C["p<q"], picked[:, 0, :], start=True, stop=True)
                nc.tensor.matmul(PS[:, 2, EXPERTS:2 * EXPERTS], C["ones"], picked[:, 0, :], start=True, stop=False)
                nc.tensor.matmul(PS[:, 2, EXPERTS:2 * EXPERTS], C["p<q"], picked[:, 1, :], start=False, stop=True)
                nc.tensor.matmul(PS[:, 2, 2 * EXPERTS:3 * EXPERTS], C["ones"], picked[:, 0, :], start=True, stop=False)
                nc.tensor.matmul(PS[:, 2, 2 * EXPERTS:3 * EXPERTS], C["ones"], picked[:, 1, :], start=False,
                                 stop=True).then_inc(ranks_done, 1)

            @block.scalar
            def _(act):
                act.wait_ge(exp_ready, 1)
                for a in range(NT):
                    last = nc.scalar.activation(ex[:, a, 0:4], grp[:, a, 0:4], ACT.Exp, bias=gp[:, a, 0:1],
                                                accum_out=gp[:, a, 1:2])
                last.then_inc(exp_done, 1)
                act.wait_ge(exp2_ready, 1)
                nc.scalar.activation(gp[:, :, 2:3], gp[:, :, 2:3], ACT.Exp).then_inc(exp2_done, 1)

            @block.vector
            def _(dve):
                step = chain(dve, dve_step)
                step(nc.vector.memset(grp[:, :, :], NEG))
                dve.wait_ge(logits_done, 1)
                for a in range(NT):
                    last = nc.vector.tensor_tensor(logits[:, a, :], PS[:, a, 0:N], W["router_bias"], ALU.add)
                step(last)
                step(nc.vector.tensor_copy(grp[:, :, 0:4], logits[:, :, 0:4]))
                for a in range(NT):
                    step(nc.vector.max(best[:, a, :], grp[:, a, :]))
                    step(nc.vector.max_index(index[:, a, :], best[:, a, :], grp[:, a, :]))
                step(nc.vector.tensor_copy(chosen[:, :, :], index[:, :, :]))
                nc.vector.tensor_scalar(gp[:, :, 0:1], best[:, :, 0:1], -1.0, None, ALU.mult).then_inc(exp_ready, 1)
                for a in range(NT):
                    step(nc.vector.tensor_scalar(hot[:, a, 0, 0:4], C["iota"][:, 0:4], chosen[:, a, 0:1], NEG,
                                                 ALU.not_equal, ALU.mult))
                    step(nc.vector.tensor_tensor(
                        mine[:, a, :].rearrange("p (g e) -> p g e", e=PER_GROUP),
                        logits[:, a, 4:N].rearrange("p (g e) -> p g e", e=PER_GROUP),
                        hot[:, a, 0, 0:4].unsqueeze(2).to_broadcast([P, 4, PER_GROUP]), ALU.add))
                    step(nc.vector.max(top[:, a, :], mine[:, a, :]))
                    step(nc.vector.max_index(ti[:, a, :], top[:, a, :], mine[:, a, :]))
                step(nc.vector.tensor_copy(tf[:, :, :], ti[:, :, :]))
                for a in range(NT):
                    for j in range(2):
                        last = nc.vector.tensor_scalar(hot[:, a, j, :], C["iota"][:, 0:EXPERTS], tf[:, a, j:j + 1],
                                                       None, ALU.is_equal)
                step(last)
                nc.vector.tensor_tensor(picked[:, :, :], hot[:, :, 0, :], hot[:, :, 1, :], ALU.add).then_inc(chosen_done, 1)
                dve.wait_ge(exp_done, 1)
                nc.vector.tensor_tensor(gp[:, :, 2:3], top[:, :, 1:2], top[:, :, 0:1],
                                        ALU.subtract).then_inc(exp2_ready, 1)
                dve.wait_ge(exp2_done, 1)
                step(nc.vector.tensor_scalar(gp[:, :, 3:4], gp[:, :, 2:3], 1.0, None, ALU.add))
                step(nc.vector.tensor_tensor(gp[:, :, 3:4], gp[:, :, 3:4], gp[:, :, 1:2], ALU.mult))
                step(nc.vector.reciprocal(gp[:, :, 3:4], gp[:, :, 3:4]))
                step(nc.vector.tensor_tensor(gp[:, :, 2:3], gp[:, :, 2:3], gp[:, :, 3:4], ALU.mult))
                for a in range(NT):
                    for j in range(2):
                        last = nc.vector.tensor_scalar(hot[:, a, j, :], hot[:, a, j, :], gp[:, a, 3 - j:4 - j], None, ALU.mult)
                step(last)
                step(nc.vector.tensor_tensor(shares[:, :, 0:EXPERTS], hot[:, :, 0, :], hot[:, :, 1, :], ALU.add))
                dve.wait_ge(ranks_done, 1)
                ranks = PS[:, 2, 0:NT * EXPERTS].rearrange("p (a e) -> p a e", e=EXPERTS)
                step(nc.vector.scalar_tensor_tensor(slots[:, :, 0:EXPERTS], ranks, 1.0, picked[:, :, :], ALU.add, ALU.mult))
                step(nc.vector.tensor_scalar(over[:, :], C["iota"][:, 0:EXPERTS], -1.0, float(EXPERTS), ALU.mult, ALU.add))
                step(nc.vector.scalar_tensor_tensor(over[:, :], PS[:, 2, NT * EXPERTS:(NT + 1) * EXPERTS], float(P),
                                                    over[:, :], ALU.is_gt, ALU.mult))
                step(nc.vector.max(over_best[:, :], over[:, :]))
                step(nc.vector.tensor_scalar(over_id[:, 0, :], over_best[:, 0:OVERFLOW], -1.0, float(EXPERTS), ALU.mult,
                                             ALU.add))
                step(nc.vector.tensor_scalar(over_id[:, 1, :], over_id[:, 0, :], float(EXPERTS - 1), None, ALU.min))
                step(nc.vector.tensor_copy(S["over_expert"][:, :], over_id[:, 1, :]))
                step(nc.vector.tensor_tensor(over_hot[:, :, :],
                                             C["iota"][:, 0:EXPERTS].unsqueeze(1).to_broadcast([P, OVERFLOW, EXPERTS]),
                                             over_id[:, 0, :].unsqueeze(2).to_broadcast([P, OVERFLOW, EXPERTS]),
                                             ALU.is_equal))
                for table in (slots, shares):
                    for a in range(NT):
                        last = nc.vector.tensor_tensor(over_part[:, a, :, :], over_hot[:, :, :],
                                                       table[:, a, 0:EXPERTS].unsqueeze(1).to_broadcast(
                                                           [P, OVERFLOW, EXPERTS]), ALU.mult)
                    step(last)
                    step(nc.vector.tensor_reduce(table[:, :, EXPERTS:], over_part[:, :, :, :], X, ALU.add))
                nc.vector.tensor_scalar(slots[:, :, 0:EXPERTS], slots[:, :, 0:EXPERTS], -1.0, None, ALU.add)
                nc.vector.tensor_scalar(slots[:, :, EXPERTS:], slots[:, :, EXPERTS:], -1.0 - P, None, ALU.add)


def experts(nc, S):
    PS, C = S["psum"], S["const"]
    FC = DE // P
    HALF = KD // 2
    N = EXPERTS + OVERFLOW
    PIECES, RING = 6, 4
    GATE, UP, DOWN = (0, 1), (2, 3), (4, 5)
    wg, wu, wd = (S["dram"][n] for n in ("w_gate", "w_up", "w_down"))

    def pieces(i, j):
        return i * (2 * PIECES) + j

    def all_blocks(eng, step):
        step(0, 0, first=True)
        step(0, 1, second=True)
        with eng.Fori(1, N // 2) as i:
            for k in range(2):
                step(i, k)
        step(N // 2, 0, last=True)

    with phase(nc, "dve_step scale_in piece_in0 piece_in1 piece_in2 piece_in3 rows_done hot_done turned "
                   "share_out gather1_done gather2_done gathered_top gathered piece_used silu_done hidden_done "
                   "hidden_turned hidden_top hidden_low piece_top piece_low y_top y_low scattered") as (
            memory, dve_step, scale_in, piece_in0, piece_in1, piece_in2, piece_in3, rows_done, hot_done, turned,
            share_out, gather1_done, gather2_done, gathered_top, gathered, piece_used, silu_done,
            hidden_done, hidden_turned, hidden_top, hidden_low, piece_top, piece_low, y_top, y_low, scattered):
        raw = sbuf(nc, memory, "piece_raw", [P, RING, 4, BANK])
        top = sbuf(nc, memory, "piece_tops", [P, RING, 4, BANK])
        low = sbuf(nc, memory, "piece_lows", [P, RING, 4, BANK])
        h_rows = sbuf(nc, memory, "h_row_parts", [P, 2, NT, D])
        hot = sbuf(nc, memory, "slot_hot", [P, NT, P])
        hot_t = sbuf(nc, memory, "slot_hot_turned", [P, 2, T])
        share = sbuf(nc, memory, "slot_share", [P, 2])
        g_cols = sbuf(nc, memory, "gathered_cols", [P, 2, KD, P])
        silu = sbuf(nc, memory, "silu", [P, DE])
        hid = sbuf(nc, memory, "hidden", [P, DE])
        hid_cols = sbuf(nc, memory, "hidden_cols", [P, 2, FC, P])
        y = sbuf(nc, memory, "block_result", [P, 2, D])
        scale = sbuf(nc, memory, "norm2_g_row", [P, D])
        piece_in = (piece_in0, piece_in1, piece_in2, piece_in3)

        def arrived(i, j):
            return i * (2 * PIECES // RING * 16) + (j // RING + 1) * 16

        def tiles(ap):
            return ap.rearrange("p (c s) -> p c s", s=P)

        with nc.Block() as block:
            @block.sync
            def _(sp):
                def load(e, i, j, first=False):
                    q = j % PIECES
                    if not first:
                        sp.wait_ge(piece_low, pieces(i, j - RING + 1))
                    if q in DOWN:
                        src = wd[bass.ds(e, 1), :, (q - 4) * BANK:(q - 3) * BANK]
                    else:
                        src = (wg if q in GATE else wu)[bass.ds(e, 1), q % 2 * BANK:(q % 2 + 1) * BANK, :]
                    sp.dma_start(raw[:, j % RING, :, :], src.rearrange("o (c p) n -> p (o c) n", p=P)).then_inc(
                        piece_in[j % RING], 16)

                sp.dma_start(scale[:, :], S["dram"]["norm2_g_row"].partition_broadcast(P)).then_inc(scale_in, 16)
                for j in range(2 * PIECES):
                    load(j // PIECES, 0, j, first=j < RING)
                over = [sp.value_load(S["over_expert"][0:1, j:j + 1], min_val=0, max_val=EXPERTS - 1)
                        for j in range(OVERFLOW)]
                with sp.Fori(1, EXPERTS // 2) as i:
                    for j in range(2 * PIECES):
                        load(i * 2 + j // PIECES, i, j)
                for n, e in enumerate(over):
                    for q in range(PIECES):
                        load(e, (EXPERTS + n) // 2, n % 2 * PIECES + q)

            @block.tensor
            def _(pe):
                def three_passes(out, lhs, rhs, start, stop):
                    for n, (a, b) in enumerate(((0, 0), (0, 1), (1, 0))):
                        last = nc.tensor.matmul(out, r32(lhs[a]), r32(rhs[b]), start=start and n == 0,
                                                stop=stop and n == 2)
                    return last

                def times_weights(i, j, bank, cols, start, stop):
                    pe.wait_ge(piece_low, pieces(i, j + 1))
                    for c in range(4):
                        last = three_passes(PS[:, bank, :], (cols[:, 0, c, :], cols[:, 1, c, :]),
                                            (top[:, j % RING, c, :], low[:, j % RING, c, :]), start and c == 0,
                                            stop and c == 3)
                    last.then_inc(piece_used, 1)

                def turn_hot(i, k):
                    pe.wait_ge(hot_done, i * 2 + (k + 1))
                    for a in range(NT):
                        nc.tensor.transpose(PS[:, 3, a * P:(a + 1) * P], hot[:, a, :], C["ident"])
                    for a in range(NT):
                        last = nc.tensor.matmul(PS[:, 3, T:T + 1], hot[:, a, :], S["shares"][:, a, bass.ds(i * 2 + k, 1)],
                                                start=(a == 0), stop=(a == NT - 1))
                    last.then_inc(turned, 1)

                def gather(half, bank):
                    for c in range(HALF):
                        s = slice((half * HALF + c) * P, (half * HALF + c + 1) * P)
                        for n, (part, a) in enumerate((part, a) for part in range(2) for a in range(NT)):
                            last = nc.tensor.matmul(PS[:, bank, c * P:(c + 1) * P], r32(h_rows[:, part, a, s]),
                                                    r32(hot[:, a, :]), start=(n == 0), stop=(n == 2 * NT - 1))
                    return last

                def scatter(k, opens=False, closes=False):
                    for a in range(NT):
                        for n in range(2):
                            for part in range(2):
                                last = nc.tensor.matmul(PS[:, 4 + 2 * a + n, :], r32(hot_t[:, k, a * P:(a + 1) * P]),
                                                        r32(y[:, part, n * BANK:(n + 1) * BANK]),
                                                        start=opens and part == 0, stop=closes and part == 1,
                                                        skip_group_check=True)
                    last.then_inc(scattered, 1)

                def block_step(i, k, first=False, second=False, last=False):
                    j = k * PIECES
                    for bank, (one, two) in ((0, GATE), (1, UP)):
                        if not first:
                            pe.wait_ge(y_low, i * 4 + (2 * k - 1 + bank))
                        if bank == 0:
                            pe.wait_ge(gathered, i * 4 + (2 * k + 1))
                        times_weights(i, j + one, bank, g_cols[:, :, 0:HALF, :], True, False)
                        if bank == 0:
                            pe.wait_ge(gathered, i * 4 + (2 * k + 2))
                        times_weights(i, j + two, bank, g_cols[:, :, HALF:KD, :], False, True)
                    if not first:
                        scatter(1 - k, opens=second)
                    if not last:
                        turn_hot(i, k + 1)
                    pe.wait_ge(hidden_done, i * 2 + (k + 1))
                    for f in range(FC):
                        mm = nc.tensor.transpose(PS[:, 2, f * P:(f + 1) * P], hid[:, f * P:(f + 1) * P], C["ident"])
                    mm.then_inc(hidden_turned, 1)
                    if not last:
                        pe.wait_ge(share_out, i * 2 + (k + 2))
                        gather(0, 3).then_inc(gather1_done, 1)
                    pe.wait_ge(hidden_low, i * 2 + (k + 1))
                    for n in range(2):
                        times_weights(i, j + DOWN[n], n, hid_cols, True, True)
                    if not last:
                        gather(1, 2).then_inc(gather2_done, 1)

                pe.wait_ge(rows_done, 1)
                turn_hot(0, 0)
                pe.wait_ge(share_out, 1)
                gather(0, 3).then_inc(gather1_done, 1)
                gather(1, 2).then_inc(gather2_done, 1)
                all_blocks(pe, block_step)
                pe.wait_ge(y_low, 2 * N)
                scatter(0, closes=True)

            @block.scalar
            def _(act):
                def piece(i, j, new=True):
                    act.wait_ge(piece_in[j % RING], arrived(i, j))
                    if new:
                        act.wait_ge(piece_used, pieces(i, j - RING + 1))
                    nc.scalar.activation(r32(top[:, j % RING, :, :]), raw[:, j % RING, :, :], ACT.Copy).then_inc(piece_top, 1)

                def take_turned(i, k):
                    act.wait_ge(turned, i * 2 + (k + 1))
                    nc.scalar.activation(r32(hot_t[:, k % 2, :]), PS[:, 3, 0:T], ACT.Copy)
                    nc.scalar.activation(share[:, k % 2:k % 2 + 1], PS[:, 3, T:T + 1], ACT.Copy).then_inc(share_out, 1)

                def take_gathered(i, k, half, bank):
                    act.wait_ge((gather1_done, gather2_done)[half], i * 2 + (k + 1))
                    nc.scalar.activation(r32(g_cols[:, 0, half * HALF:(half + 1) * HALF, :]), tiles(PS[:, bank, :]),
                                         ACT.Copy).then_inc(gathered_top, 1)

                def block_step(i, k, first=False, second=False, last=False):
                    j, after = k * PIECES, (k + 1) * PIECES
                    piece(i, j + DOWN[0])
                    act.wait_ge(piece_used, pieces(i, j + UP[0]))
                    nc.scalar.activation(silu[:, :], PS[:, 0, :], ACT.Silu).then_inc(silu_done, 1)
                    piece(i, j + DOWN[1])
                    if not last:
                        take_turned(i, k + 1)
                    act.wait_ge(hidden_turned, i * 2 + (k + 1))
                    nc.scalar.activation(r32(hid_cols[:, 0, :, :]), tiles(PS[:, 2, :]), ACT.Copy).then_inc(hidden_top, 1)
                    if not last:
                        piece(i, after + GATE[0])
                        take_gathered(i, k + 1, 0, 3)
                        piece(i, after + GATE[1])
                    for n in range(2):
                        act.wait_ge(piece_used, pieces(i, j + DOWN[n] + 1))
                        nc.scalar.activation(r32(y[:, 0, n * BANK:(n + 1) * BANK]), PS[:, n, :], ACT.Copy).then_inc(y_top, 1)
                    if not last:
                        take_gathered(i, k + 1, 1, 2)
                        piece(i, after + UP[0])
                        piece(i, after + UP[1])

                piece(0, 0, new=False)
                take_turned(0, 0)
                take_gathered(0, 0, 0, 3)
                piece(0, 1, new=False)
                take_gathered(0, 0, 1, 2)
                for j in range(2, RING):
                    piece(0, j, new=False)
                all_blocks(act, block_step)

            @block.vector
            def _(dve):
                step = chain(dve, dve_step)

                def piece(i, j):
                    dve.wait_ge(piece_top, pieces(i, j + 1))
                    nc.vector.tensor_tensor(r32(low[:, j % RING, :, :]), raw[:, j % RING, :, :], top[:, j % RING, :, :],
                                            ALU.subtract).then_inc(piece_low, 1)

                def build_hot(i, k):
                    for a in range(NT):
                        last = nc.vector.tensor_scalar(r32(hot[:, a, :]), C["iota"],
                                                       S["slots"][:, a, bass.ds(i * 2 + k, 1)], None, ALU.is_equal)
                    last.then_inc(hot_done, 1)

                def take_gathered(i, k, half, bank):
                    dve.wait_ge(gathered_top, i * 4 + (2 * k + half + 1))
                    s = slice(half * HALF, (half + 1) * HALF)
                    nc.vector.tensor_tensor(r32(g_cols[:, 1, s, :]), tiles(PS[:, bank, :]), g_cols[:, 0, s, :],
                                            ALU.subtract).then_inc(gathered, 1)

                def block_step(i, k, first=False, second=False, last=False):
                    j, after = k * PIECES, (k + 1) * PIECES
                    if not last:
                        build_hot(i, k + 1)
                    piece(i, j + DOWN[0])
                    piece(i, j + DOWN[1])
                    dve.wait_ge(piece_used, pieces(i, j + DOWN[0]))
                    dve.wait_ge(silu_done, i * 2 + (k + 1))
                    dve.wait_ge(share_out, i * 2 + (k + 1))
                    nc.vector.scalar_tensor_tensor(hid[:, :], silu[:, :], share[:, k:k + 1], PS[:, 1, :], ALU.mult,
                                                   ALU.mult).then_inc(hidden_done, 1)
                    dve.wait_ge(hidden_top, i * 2 + (k + 1))
                    nc.vector.tensor_tensor(r32(hid_cols[:, 1, :, :]), tiles(PS[:, 2, :]), hid_cols[:, 0, :, :],
                                            ALU.subtract).then_inc(hidden_low, 1)
                    if not last:
                        piece(i, after + GATE[0])
                        take_gathered(i, k + 1, 0, 3)
                    for n in range(2):
                        dve.wait_ge(y_top, i * 4 + (2 * k + n + 1))
                        s = slice(n * BANK, (n + 1) * BANK)
                        nc.vector.tensor_tensor(r32(y[:, 1, s]), PS[:, n, :], y[:, 0, s], ALU.subtract).then_inc(y_low, 1)
                        if not last and n == 0:
                            piece(i, after + GATE[1])
                    if not last:
                        take_gathered(i, k + 1, 1, 2)
                        piece(i, after + UP[0])
                        piece(i, after + UP[1])

                build_hot(0, 0)
                dve.wait_ge(scale_in, 16)
                rows = S["h_rows"]
                step(nc.vector.tensor_tensor(rows[:, :, :], rows[:, :, :],
                                             scale[:, :].unsqueeze(1).to_broadcast([P, NT, D]), ALU.mult))
                step(nc.vector.tensor_copy(r32(h_rows[:, 0]), rows[:, :, :]))
                nc.vector.tensor_tensor(r32(h_rows[:, 1]), rows[:, :, :], h_rows[:, 0], ALU.subtract).then_inc(rows_done, 1)
                piece(0, 0)
                take_gathered(0, 0, 0, 3)
                piece(0, 1)
                take_gathered(0, 0, 1, 2)
                for j in range(2, RING):
                    piece(0, j)
                all_blocks(dve, block_step)
                dve.wait_ge(scattered, N)
                for a in range(NT):
                    for n in range(2):
                        o = S["x"][:, a, n * BANK:(n + 1) * BANK]
                        nc.vector.tensor_tensor(o, o, PS[:, 4 + 2 * a + n, :], ALU.add)



def differential(nc, S):
    PS, C, L = S["psum"], S["const"], S["layer"]
    scale = HD ** -0.5
    work = [(h, a) for h in range(DH) for a in range(NT)]
    with phase(nc, "dve_step act_step lam_in lam_exp scores_done masked max_done exp_done mixed_done probs_t "
                   "probs_copied out_done squared root_done finished") as (
            memory, dve_step, act_step, lam_in, lam_exp, scores_done, masked, max_done, exp_done, mixed_done, probs_t,
            probs_copied, out_done, squared, root_done, finished):
        prod = sbuf(nc, memory, "lam_products", [P, 2, HD])
        lam = sbuf(nc, memory, "lam", [P, 4])
        sc = sbuf(nc, memory, "diff_scores", [P, 2, 2, T])
        top = sbuf(nc, memory, "diff_max", [P, 2, len(work), 2])
        den = sbuf(nc, memory, "diff_den", [P, 2, len(work), 2])
        pt = sbuf(nc, memory, "diff_probs_t", [P, 2, NT, P])
        sq = sbuf(nc, memory, "diff_sq", [P, 2, P])
        ss = sbuf(nc, memory, "diff_ss", [P, len(work)])
        eps = sbuf(nc, memory, "diff_eps", [P, 1])

        with nc.Block() as block:
            @block.tensor
            def _(pe):
                def score(n):
                    h, a = work[n]
                    if n >= 2:
                        pe.wait_ge(masked, n - 1)
                    for m in range(2):
                        rows = slice(m * HD, (m + 1) * HD)
                        last = nc.tensor.matmul(PS[:, 2 * (n % 2) + m, 0:(a + 1) * P],
                                                S["dqk"][rows, h, a * P:(a + 1) * P],
                                                S["dqk"][rows, DH + h, 0:(a + 1) * P], start=True, stop=True)
                    last.then_inc(scores_done, 1)

                score(0)
                for n, (h, a) in enumerate(work):
                    if n + 1 < len(work):
                        score(n + 1)
                    pe.wait_ge(mixed_done, n + 1)
                    if n >= 2:
                        pe.wait_ge(probs_copied, n - 1)
                    for i in range(a + 1):
                        last = nc.tensor.transpose(PS[:, 4 + n % 2, i * P:(i + 1) * P],
                                                   sc[:, n % 2, 0, i * P:(i + 1) * P], C["ident"])
                    last.then_inc(probs_t, 1)
                    pe.wait_ge(probs_copied, n + 1)
                    if n >= 2:
                        pe.wait_ge(finished, n - 1)
                    for i in range(a + 1):
                        last = nc.tensor.matmul(PS[:, 6 + n % 2, 0:P], pt[:, n % 2, i, :],
                                                S["dv"][:, i, h * P:(h + 1) * P], start=(i == 0), stop=(i == a))
                    last.then_inc(out_done, 1)

            @block.scalar
            def _(act):
                step = chain(act, act_step)
                act.wait_ge(lam_in, 1)
                nc.scalar.activation(lam[:, 0:2], lam[:, 0:2], ACT.Exp).then_inc(lam_exp, 1)
                for n, (h, a) in enumerate(work):
                    act.wait_ge(max_done, n + 1)
                    for m in range(2):
                        last = nc.scalar.activation(sc[:, n % 2, m, 0:(a + 1) * P], sc[:, n % 2, m, 0:(a + 1) * P],
                                                    ACT.Exp, scale=scale, bias=top[:, 1, n, m:m + 1],
                                                    accum_out=den[:, 0, n, m:m + 1])
                    last.then_inc(exp_done, 1)
                    act.wait_ge(probs_t, n + 1)
                    nc.scalar.activation(pt[:, n % 2, 0:a + 1, :],
                                         PS[:, 4 + n % 2, 0:(a + 1) * P].rearrange("p (i q) -> p i q", q=P),
                                         ACT.Copy).then_inc(probs_copied, 1)
                act.wait_ge(squared, 1)
                nc.scalar.activation(ss[:, :], ss[:, :], ACT.Sqrt, scale=1.0 / P, bias=eps[:, 0:1]).then_inc(root_done, 1)

            @block.vector
            def _(dve):
                step = chain(dve, dve_step)
                step(nc.vector.memset(eps[:, :], RMS_EPS))
                for m in range(2):
                    step(nc.vector.tensor_tensor(prod[:, m, :], L["lam"][:, 2 * m, :], L["lam"][:, 2 * m + 1, :], ALU.mult))
                nc.vector.tensor_reduce(lam[:, 0:2], prod[:, :, :], X, ALU.add).then_inc(lam_in, 1)
                dve.wait_ge(lam_exp, 1)
                step(nc.vector.tensor_tensor(lam[:, 2:3], lam[:, 1:2], lam[:, 0:1], ALU.subtract))
                step(nc.vector.tensor_tensor(lam[:, 3:4], lam[:, 2:3], L["lambda_init"][:, 0:1], ALU.subtract))

                def finish(n):
                    h, a = work[n]
                    dve.wait_ge(out_done, n + 1)
                    to = S["mixed"][:, a, h * P:(h + 1) * P]
                    step(nc.vector.tensor_copy(to, PS[:, 6 + n % 2, 0:P]))
                    step(nc.vector.tensor_tensor(sq[:, n % 2, :], to, to, ALU.mult))
                    nc.vector.tensor_reduce(ss[:, n:n + 1], sq[:, n % 2, :], X, ALU.add).then_inc(finished, 1)

                for n, (h, a) in enumerate(work):
                    w = (a + 1) * P
                    dve.wait_ge(scores_done, n + 1)
                    if n >= 2:
                        dve.wait_ge(probs_t, n - 1)
                    slope = 2.0 ** (-8.0 * (h + 1) / DH)
                    for m in range(2):
                        last = nc.vector.scalar_tensor_tensor(sc[:, n % 2, m, 0:w], C["dist"][:, a, 0:w],
                                                              -slope / scale, PS[:, 2 * (n % 2) + m, 0:w],
                                                              ALU.mult, ALU.add)
                    last.then_inc(masked, 1)
                    dve.wait_ge(masked, n + 1)
                    step(nc.vector.tensor_reduce(top[:, 0, n, :], sc[:, n % 2, :, 0:w], X, ALU.max))
                    nc.vector.tensor_scalar(top[:, 1, n, :], top[:, 0, n, :], -scale, None, ALU.mult).then_inc(max_done, 1)
                    if n:
                        finish(n - 1)
                    dve.wait_ge(exp_done, n + 1)
                    step(nc.vector.reciprocal(den[:, 1, n, :], den[:, 0, n, :]))
                    step(nc.vector.tensor_tensor(den[:, 1, n, 1:2], den[:, 1, n, 1:2], lam[:, 3:4], ALU.mult))
                    step(nc.vector.tensor_scalar(sc[:, n % 2, 0, 0:w], sc[:, n % 2, 0, 0:w], den[:, 1, n, 0:1], None, ALU.mult))
                    nc.vector.scalar_tensor_tensor(sc[:, n % 2, 0, 0:w], sc[:, n % 2, 1, 0:w], den[:, 1, n, 1:2],
                                                   sc[:, n % 2, 0, 0:w], ALU.mult, ALU.add).then_inc(mixed_done, 1)
                finish(len(work) - 1)
                dve.wait_ge(finished, len(work))
                nc.vector.tensor_scalar(ss[:, :], ss[:, :], 1.0, None, ALU.mult).then_inc(squared, 1)
                dve.wait_ge(root_done, 1)
                step(nc.vector.reciprocal(ss[:, :], ss[:, :]))
                for n, (h, a) in enumerate(work):
                    to = S["mixed"][:, a, h * P:(h + 1) * P]
                    last = nc.vector.scalar_tensor_tensor(to, to, ss[:, n:n + 1], L["subln_g"], ALU.mult, ALU.mult)
                step(last)
                nc.vector.tensor_scalar(S["mixed"][:, :, 0:DH * P], S["mixed"][:, :, 0:DH * P],
                                        L["lambda_init"][:, 1:2], None, ALU.mult)


def stick_breaking(nc, S):
    PS, C = S["psum"], S["const"]
    scale = HD ** -0.5
    B3 = 3 * P
    with phase(nc, "dve_step act_step z_done log_done fail_done later_done logw_done w_exp w_done out_done") as (
            memory, dve_step, act_step, z_done, log_done, fail_done, later_done, logw_done, w_exp, w_done, out_done):
        z = sbuf(nc, memory, "sb_abs", [P, 2, B3])
        l = sbuf(nc, memory, "sb_log", [P, 2, B3])
        fail = sbuf(nc, memory, "sb_fail", [P, 2, B3])
        lw = sbuf(nc, memory, "sb_logw", [P, 2, B3])

        def diagonal(ap, n):
            return ap[:, n % 2, :].rearrange("p (b q) -> p b q", q=P)[:, 0:3:2, :]

        with nc.Block() as block:
            @block.tensor
            def _(pe):
                def logits(h):
                    rows = slice((h % 2) * HD, (h % 2 + 1) * HD)
                    c = h // 2
                    if h >= 2:
                        pe.wait_ge(logw_done, h - 1)
                    nc.tensor.matmul(PS[:, h % 2, 0:T], S["sqk"][rows, SH // 2 + c, 0:P], S["sqk"][rows, c, :],
                                     start=True, stop=True)
                    nc.tensor.matmul(PS[:, h % 2, T:B3], S["sqk"][rows, SH // 2 + c, P:T], S["sqk"][rows, c, P:T],
                                     start=True, stop=True).then_inc(z_done, 1)

                def times_v(h):
                    pe.wait_ge(w_done, h + 1)
                    s = slice(h * HD, (h + 1) * HD)
                    nc.tensor.matmul(PS[:, 4, s], lw[:, h % 2, 0:P], S["sv"][:, 0, s], start=True, stop=True)
                    nc.tensor.matmul(PS[:, 5, s], lw[:, h % 2, P:T], S["sv"][:, 0, s], start=True, stop=False)
                    nc.tensor.matmul(PS[:, 5, s], lw[:, h % 2, T:B3], S["sv"][:, 1, s], start=False,
                                     stop=True).then_inc(out_done, 1)

                logits(0)
                for h in range(SH):
                    if h + 1 < SH:
                        logits(h + 1)
                    pe.wait_ge(fail_done, h + 1)
                    o = PS[:, 2 + h % 2, :]
                    nc.tensor.matmul(o[:, 0:P], C["p>q"], fail[:, h % 2, 0:P], start=True, stop=True)
                    nc.tensor.matmul(o[:, P:T], C["p>q"], fail[:, h % 2, P:T], start=True, stop=False)
                    nc.tensor.matmul(o[:, P:T], C["ones"], fail[:, h % 2, T:B3], start=False, stop=True)
                    nc.tensor.matmul(o[:, T:B3], C["p>q"], fail[:, h % 2, T:B3], start=True,
                                     stop=True).then_inc(later_done, 1)
                    if h:
                        times_v(h - 1)
                times_v(SH - 1)

            @block.scalar
            def _(act):
                step = chain(act, act_step)
                for h in range(SH):
                    act.wait_ge(z_done, h + 1)
                    if h >= 2:
                        act.wait_ge(logw_done, h - 1)
                    step(nc.scalar.activation(z[:, h % 2, :], PS[:, h % 2, 0:B3], ACT.Abs))
                    step(nc.scalar.activation(z[:, h % 2, :], z[:, h % 2, :], ACT.Exp, scale=-scale))
                    nc.scalar.activation(l[:, h % 2, :], z[:, h % 2, :], ACT.Ln, bias=1.0).then_inc(log_done, 1)
                    if h:
                        act.wait_ge(logw_done, h)
                        nc.scalar.activation(lw[:, (h - 1) % 2, :], lw[:, (h - 1) % 2, :], ACT.Exp).then_inc(w_exp, 1)
                act.wait_ge(logw_done, SH)
                nc.scalar.activation(lw[:, (SH - 1) % 2, :], lw[:, (SH - 1) % 2, :], ACT.Exp).then_inc(w_exp, 1)
                act.wait_ge(out_done, SH)
                for a in range(NT):
                    nc.scalar.activation(S["mixed"][:, a, DH * P:D], PS[:, 4 + a, :], ACT.Copy)

            @block.vector
            def _(dve):
                step = chain(dve, dve_step)
                before = C["p<q"].unsqueeze(1).to_broadcast([P, 2, P])

                def weights(h):
                    dve.wait_ge(w_exp, h + 1)
                    nc.vector.tensor_tensor(diagonal(lw, h), diagonal(lw, h), before, ALU.mult).then_inc(w_done, 1)

                for h in range(SH):
                    zp = PS[:, h % 2, 0:B3]
                    dve.wait_ge(log_done, h + 1)
                    if h >= 2:
                        dve.wait_ge(later_done, h - 1)
                    step(nc.vector.tensor_scalar(fail[:, h % 2, :], zp, 0.0, scale, ALU.max, ALU.mult))
                    step(nc.vector.tensor_tensor(fail[:, h % 2, :], fail[:, h % 2, :], l[:, h % 2, :], ALU.add))
                    nc.vector.tensor_tensor(diagonal(fail, h), diagonal(fail, h), before, ALU.mult).then_inc(fail_done, 1)
                    if h >= 2:
                        dve.wait_ge(out_done, h - 1)
                    step(nc.vector.tensor_scalar(lw[:, h % 2, :], zp, 0.0, scale, ALU.min, ALU.mult))
                    step(nc.vector.tensor_tensor(lw[:, h % 2, :], lw[:, h % 2, :], l[:, h % 2, :], ALU.subtract))
                    dve.wait_ge(later_done, h + 1)
                    nc.vector.tensor_tensor(lw[:, h % 2, :], lw[:, h % 2, :], PS[:, 2 + h % 2, 0:B3],
                                            ALU.subtract).then_inc(logw_done, 1)
                    if h:
                        weights(h - 1)
                weights(SH - 1)


def layer_norm(dve, nc, step, rows, stats, psum_halves, g, b, ready, root_ready, root_done):
    for a in range(NT):
        for n in range(2):
            s = slice(n * BANK, (n + 1) * BANK)
            ready(a, n)
            step(nc.vector.scalar_tensor_tensor(rows[:, a, s], rows[:, a, s], ALPHA, psum_halves(a, n), ALU.mult, ALU.add))
            step(nc.vector.bn_stats(stats[:, a, 6 * n:6 * n + 6], rows[:, a, s]))
        step(nc.vector.bn_aggr(stats[:, a, 12:14], stats[:, a, 0:12]))
    nc.vector.tensor_scalar(stats[:, :, 14:15], stats[:, :, 13:14], LN_EPS, None, ALU.add).then_inc(root_ready, 1)
    dve.wait_ge(root_done, 1)
    step(nc.vector.reciprocal(stats[:, :, 15:16], stats[:, :, 14:15]))
    for a in range(NT):
        step(nc.vector.tensor_scalar(rows[:, a, :], rows[:, a, :], stats[:, a, 12:13], stats[:, a, 15:16], ALU.subtract,
                                     ALU.mult))
        step(nc.vector.tensor_tensor(rows[:, a, :], rows[:, a, :], g, ALU.mult))
        step(nc.vector.tensor_tensor(rows[:, a, :], rows[:, a, :], b, ALU.add))


def one_row(S, name, layer):
    return S["dram"][name][bass.ds(layer, 1), :].rearrange("l n -> (l n)").partition_broadcast(P)


def mix_out(nc, S):
    PS, C, L = S["psum"], S["const"], S["layer"]
    with phase(nc, "dve_step transposed copied_dve copied_act products root_ready root_done") as (
            memory, dve_step, transposed, copied_dve, copied_act, products, root_ready, root_done):
        w, ln = L["w_o"], L["ln1"]
        cols = sbuf(nc, memory, "mixed_cols", [P, KD, T])
        stats = sbuf(nc, memory, "ln_stats", [P, NT, 16])
        with nc.Block() as block:
            @block.tensor
            def _(pe):
                for k in range(KD):
                    for a in range(NT):
                        last = nc.tensor.transpose(PS[:, k // 2, (k % 2) * T + a * P:(k % 2) * T + (a + 1) * P],
                                                   S["mixed"][:, a, k * P:(k + 1) * P], C["ident"])
                    if k % 2:
                        last.then_inc(transposed, 1)
                pe.wait_ge(copied_dve, 2)
                pe.wait_ge(copied_act, 2)
                for a in range(NT):
                    for n in range(2):
                        for k in range(KD):
                            last = nc.tensor.matmul(PS[:, 4 + 2 * a + n, :], cols[:, k, a * P:(a + 1) * P],
                                                    w[:, k, n * BANK:(n + 1) * BANK], start=(k == 0), stop=(k == KD - 1))
                        last.then_inc(products, 1)

            @block.scalar
            def _(act):
                for j in (1, 3):
                    act.wait_ge(transposed, j + 1)
                    nc.scalar.activation(cols[:, 2 * j:2 * j + 2, :], PS[:, j, :].rearrange("p (k t) -> p k t", t=T),
                                         ACT.Copy).then_inc(copied_act, 1)
                act.wait_ge(root_ready, 1)
                nc.scalar.activation(stats[:, :, 14:15], stats[:, :, 14:15], ACT.Sqrt).then_inc(root_done, 1)

            @block.vector
            def _(dve):
                step = chain(dve, dve_step)
                for j in (0, 2):
                    dve.wait_ge(transposed, j + 1)
                    nc.vector.tensor_copy(cols[:, 2 * j:2 * j + 2, :],
                                          PS[:, j, :].rearrange("p (k t) -> p k t", t=T)).then_inc(copied_dve, 1)
                layer_norm(dve, nc, step, S["x"], stats, lambda a, n: PS[:, 4 + 2 * a + n, :],
                           ln[:, 0, :], ln[:, 1, :], lambda a, n: dve.wait_ge(products, 2 * a + n + 1), root_ready, root_done)


def peer_select(nc, S, spare):
    PS, C = S["psum"], S["const"]
    HP = 2 * PH
    with phase(nc, "dve_step scores_done scores_out exp_ready exp_done gates_done idx_t idx_out gates_t "
                   "gates_out") as (
            memory, dve_step, scores_done, scores_out, exp_ready, exp_done, gates_done, idx_t, idx_out,
            gates_t, gates_out):
        keys = S["keys"]
        sc = spare([P, NT, HP, NKEYS])
        val = spare([P, HP, TOPK])
        idx = spare([P, HP, TOPK]).bitcast(U32)
        idx_f = spare([P, NT, 2, PH, TOPK])
        cand = spare([P, PH, TOPK * TOPK])
        rest = spare([P, PH, TOPK * TOPK])
        best = spare([P, PH, TOPK])
        minus_best = spare([P, PH])
        powers = spare([P, PH, TOPK * TOPK])
        gate = spare([P, NT, TOPK, PH, TOPK])
        stat = spare([P, 2, PH])
        with nc.Block() as block:
            @block.tensor
            def _(pe):
                for a in range(NT):
                    if a:
                        pe.wait_ge(scores_out, a)
                    for i in range(HP):
                        last = nc.tensor.matmul(PS[:, i // 4, (i % 4) * P:(i % 4 + 1) * P],
                                                S["q_cols"][:, i, a * P:(a + 1) * P], keys[:, i, :], start=True, stop=True)
                    last.then_inc(scores_done, 1)
                for a in range(NT):
                    pe.wait_ge(gates_done, a + 1)
                    if a:
                        pe.wait_ge(idx_out, a)
                    for half in range(2):
                        last = nc.tensor.transpose(PS[:, 4, half * T + a * P:half * T + (a + 1) * P],
                                                   idx_f[:, a, half, :, :], C["ident"])
                    last.then_inc(idx_t, 1)
                    for r in range(0, TOPK, 4):
                        n = a * 4 + r // 4
                        if n >= 2:
                            pe.wait_ge(gates_out, n - 1)
                        for j in range(4):
                            last = nc.tensor.transpose(PS[:, 5 + n % 2, j * P:(j + 1) * P], gate[:, a, r + j, :, :],
                                                       C["ident"])
                        last.then_inc(gates_t, 1)

            @block.scalar
            def _(act):
                for a in range(NT):
                    act.wait_ge(scores_done, a + 1)
                    nc.scalar.activation(sc[:, a, :, :], PS[:, 0:4, :].rearrange("p b (i n) -> p (b i) n", n=NKEYS),
                                         ACT.Copy).then_inc(scores_out, 1)
                for a in range(NT):
                    act.wait_ge(exp_ready, a + 1)
                    for e in range(PH):
                        last = nc.scalar.activation(powers[:, e, :], cand[:, e, :], ACT.Exp, bias=minus_best[:, e:e + 1])
                    last.then_inc(exp_done, 1)
                    act.wait_ge(idx_t, a + 1)
                    t = slice(a * P, (a + 1) * P)
                    nc.scalar.activation(S["idx_cols"][:, :, t], PS[:, 4, :].rearrange("p (h t) -> p h t", t=T)[:, :, t],
                                         ACT.Copy).then_inc(idx_out, 1)
                    for r in range(0, TOPK, 4):
                        n = a * 4 + r // 4
                        act.wait_ge(gates_t, n + 1)
                        nc.scalar.activation(S["gate_cols"][:, r:r + 4, t], PS[:, 5 + n % 2, :].rearrange(
                            "p (r t) -> p r t", t=P), ACT.Copy).then_inc(gates_out, 1)

            @block.vector
            def _(dve):
                step = chain(dve, dve_step)
                for a in range(NT):
                    dve.wait_ge(scores_out, a + 1)
                    for i in range(HP):
                        last = nc.vector.max(val[:, i, 0:8], sc[:, a, i, :])
                    step(last)
                    for i in range(HP):
                        last = nc.vector.max_index(idx[:, i, 0:8], val[:, i, 0:8], sc[:, a, i, :])
                    step(last)
                    for i in range(HP):
                        last = nc.vector.match_replace(sc[:, a, i, :], val[:, i, 0:8], sc[:, a, i, :], NEG)
                    step(last)
                    for i in range(HP):
                        last = nc.vector.max(val[:, i, 8:16], sc[:, a, i, :])
                    step(last)
                    for i in range(HP):
                        last = nc.vector.max_index(idx[:, i, 8:16], val[:, i, 8:16], sc[:, a, i, :])
                    step(last)
                    step(nc.vector.tensor_copy(idx_f[:, a, :, :, :].rearrange("p h e k -> p e h k"),
                                               idx[:, :, :].rearrange("p (e h) k -> p e h k", h=2)))
                    v = val[:, :, :].rearrange("p (e h) k -> p e h k", h=2)
                    for e in range(PH):
                        last = nc.vector.tensor_tensor(cand[:, e, :].rearrange("p (r s) -> p r s", s=TOPK),
                                                       v[:, e, 0, :].unsqueeze(2).to_broadcast([P, TOPK, TOPK]),
                                                       v[:, e, 1, :].unsqueeze(1).to_broadcast([P, TOPK, TOPK]), ALU.add)
                    step(last)
                    for e in range(PH):
                        last = nc.vector.max(best[:, e, 0:8], cand[:, e, :])
                    step(last)
                    nc.vector.tensor_scalar(minus_best[:, :], best[:, :, 0], -1.0, None, ALU.mult).then_inc(exp_ready, 1)
                    for e in range(PH):
                        last = nc.vector.match_replace(rest[:, e, :], best[:, e, 0:8], cand[:, e, :], NEG)
                    step(last)
                    for e in range(PH):
                        last = nc.vector.max(best[:, e, 8:16], rest[:, e, :])
                    step(last)
                    for e in range(PH):
                        last = nc.vector.match_replace(rest[:, e, :], best[:, e, 8:16], rest[:, e, :], NEG)
                    step(last)
                    dve.wait_ge(exp_done, a + 1)
                    g = gate[:, a, :, :, :].rearrange("p r e s -> p e r s")
                    step(nc.vector.scalar_tensor_tensor(cand[:, :, :], rest[:, :, :], NEG, powers[:, :, :], ALU.is_equal,
                                                        ALU.mult))
                    step(nc.vector.tensor_reduce(stat[:, 0, :], cand[:, :, :], X, ALU.add))
                    step(nc.vector.reciprocal(stat[:, 1, :], stat[:, 0, :]))
                    nc.vector.tensor_tensor(g, cand[:, :, :].rearrange("p e (r s) -> p e r s", s=TOPK),
                                            stat[:, 1, :].unsqueeze(2).unsqueeze(3).to_broadcast([P, PH, TOPK, TOPK]),
                                            ALU.mult).then_inc(gates_done, 1)
                    dve.wait_ge(gates_done, a + 1)


def peer_spread(nc, S):
    PS, C = S["psum"], S["const"]
    G4 = 4
    STEPS = T // G4
    with phase(nc, "hot_i_done diag_done r_done r_out g_done g_out") as (
            memory, hot_i_done, diag_done, r_done, r_out, g_done, g_out):
        hot_i = sbuf(nc, memory, "hot_i", [P, 2, G4, P])
        hot_j = sbuf(nc, memory, "hot_j", [P, 2, G4, P])
        diag = sbuf(nc, memory, "diag", [P, 2, G4, PH, TOPK])
        r = sbuf(nc, memory, "r_rows", [P, 2, G4, P])
        iota = C["iota"].unsqueeze(1).to_broadcast([P, G4, P])
        mask = C["head_of_row"].unsqueeze(1).unsqueeze(3).to_broadcast([P, G4, PH, TOPK])

        def index(half, t0):
            return S["idx_cols"][:, half, bass.ds(t0, G4)].unsqueeze(2).to_broadcast([P, G4, P])

        with nc.Block() as block:
            def diagonal(n, b):
                gates = S["gate_cols"][:, :, bass.ds(n * G4, G4)].rearrange("p r t -> p t r").unsqueeze(2) \
                    .to_broadcast([P, G4, PH, TOPK])
                return nc.vector.tensor_tensor(diag[:, b], gates, mask, ALU.mult)

            @block.vector
            def _(dve):
                def for_first(n, b):
                    diagonal(n, b)
                    nc.vector.tensor_tensor(hot_j[:, b], iota, index(1, n * G4), ALU.is_equal).then_inc(diag_done, 1)

                def for_second(n, b):
                    nc.vector.tensor_tensor(hot_i[:, b], iota, index(0, n * G4), ALU.is_equal).then_inc(hot_i_done, 1)

                for b in range(2):
                    for_first(b, b)
                    for_second(b, b)
                with dve.Fori(1, STEPS // 2) as i:
                    for b in range(2):
                        dve.wait_ge(r_done, i * 2 + (b - 1))
                        for_first(i * 2 + b, b)
                        dve.wait_ge(g_done, i * 2 + (b - 1))
                        for_second(i * 2 + b, b)

            @block.tensor
            def _(pe):
                def first(n, b, again=True):
                    pe.wait_ge(diag_done, n + 1)
                    if again:
                        pe.wait_ge(r_out, n - 1)
                    for j in range(G4):
                        last = nc.tensor.matmul(PS[:, b, j * P:(j + 1) * P],
                                                diag[:, b, j, :, :].rearrange("p e r -> p (e r)"), hot_j[:, b, j, :],
                                                start=True, stop=True)
                    last.then_inc(r_done, 1)

                def second(n, b, again=True):
                    pe.wait_ge(r_out, n + 1)
                    pe.wait_ge(hot_i_done, n + 1)
                    if again:
                        pe.wait_ge(g_out, n - 1)
                    for j in range(G4):
                        last = nc.tensor.matmul(PS[:, 4 + b, j * P:(j + 1) * P], hot_i[:, b, j, :], r[:, b, j, :],
                                                start=True, stop=True)
                    last.then_inc(g_done, 1)

                first(0, 0, again=False)
                first(1, 1, again=False)
                second(0, 0, again=False)
                first(2, 0)
                second(1, 1, again=False)
                with pe.Fori(1, STEPS // 2 - 1) as i:
                    first(i * 2 + 1, 1)
                    second(i * 2, 0)
                    first(i * 2 + 2, 0)
                    second(i * 2 + 1, 1)
                first(STEPS - 1, 1)
                second(STEPS - 2, 0)
                second(STEPS - 1, 1)

            @block.scalar
            def _(act):
                def take_r(n, b):
                    act.wait_ge(r_done, n + 1)
                    nc.scalar.activation(r[:, b], PS[:, b, :].rearrange("p (t j) -> p t j", j=P), ACT.Copy).then_inc(r_out, 1)

                def take_g(n, b):
                    act.wait_ge(g_done, n + 1)
                    nc.scalar.activation(S["all_gates"][:, :, bass.ds(n * G4, G4)].rearrange("p j t -> p t j"),
                                         PS[:, 4 + b, :].rearrange("p (t j) -> p t j", j=P), ACT.Copy).then_inc(g_out, 1)

                take_r(0, 0)
                with act.Fori(0, STEPS // 2 - 1) as i:
                    take_r(i * 2 + 1, 1)
                    take_g(i * 2, 0)
                    take_r(i * 2 + 2, 0)
                    take_g(i * 2 + 1, 1)
                take_r(STEPS - 1, 1)
                take_g(STEPS - 2, 0)
                take_g(STEPS - 1, 1)


def peer_experts(nc, S, layer):
    PS = S["psum"]
    N, PAIRS = NKEYS, NKEYS // 2
    with phase(nc, "transposed h_top h_low u_in0 u_in1 v_in0 v_in1 ln_in dve_step u_top_done u_low_done v_top_done "
                   "v_low_done gated a_done a_out hid_done y_done root_ready root_done") as (
            memory, transposed, h_top, h_low, u_in0, u_in1, v_in0, v_in1, ln_in, dve_step, u_top_done, u_low_done,
            v_top_done, v_low_done, gated, a_done, a_out, hid_done, y_done, root_ready, root_done):
        raw = sbuf(nc, memory, "uv_raw", [P, 2, 2, D])
        top = sbuf(nc, memory, "uv_top", [P, 2, 2, D])
        low = sbuf(nc, memory, "uv_low", [P, 2, 2, D])
        act_h = sbuf(nc, memory, "gelu", [P, 2, T])
        hid = sbuf(nc, memory, "hid2", [P, 2, 2, T])
        stats = sbuf(nc, memory, "ln_stats2", [P, NT, 16])
        u_in, v_in = (u_in0, u_in1), (v_in0, v_in1)
        ud, vd = S["u_src"], S["v_src"]
        h = sbuf(nc, memory, "h_parts", [P, 2, KD, T])

        def quarter(n):
            return PS[:, n, :].rearrange("p (k t) -> p k t", t=T)

        with nc.Block() as block:
            @block.sync
            def _(sp):
                def load_u(n, k):
                    sp.dma_start(raw[:, k, 0, :], ud(n)).then_inc(u_in[k], 16)

                def load_v(n, k):
                    sp.dma_start(raw[:, k, 1, :], vd(n)).then_inc(v_in[k], 16)

                for k in range(2):
                    load_u(k, k)
                    load_v(k, k)
                with sp.Fori(1, PAIRS) as i:
                    for k in range(2):
                        sp.wait_ge(u_low_done, i * 2 + (k - 1))
                        load_u(i * 2 + k, k)
                        sp.wait_ge(v_low_done, i * 2 + (k - 1))
                        load_v(i * 2 + k, k)
                sp.wait_ge(u_low_done, N)
                sp.dma_start(raw[:, 0, 0, :], one_row(S, "ln2_g_2", layer)).then_inc(ln_in, 16)
                sp.wait_ge(v_low_done, N)
                sp.dma_start(raw[:, 0, 1, :], one_row(S, "ln2_b_2", layer)).then_inc(ln_in, 16)

            @block.scalar
            def _(act):
                def gelu(n, k):
                    act.wait_ge(a_done, n + 1)
                    nc.scalar.activation(act_h[:, k, :], PS[:, k, 0:T], ACT.Gelu).then_inc(a_out, 1)

                def top_of_u(k, times):
                    act.wait_ge(u_in[k], times * 16)
                    nc.scalar.activation(r32(top[:, k, 0, :]), raw[:, k, 0, :], ACT.Copy).then_inc(u_top_done, 1)

                def top_of_v(k, times):
                    act.wait_ge(v_in[k], times * 16)
                    nc.scalar.activation(r32(top[:, k, 1, :]), raw[:, k, 1, :], ACT.Copy).then_inc(v_top_done, 1)

                for n in range(KD // 2):
                    act.wait_ge(transposed, n + 1)
                    nc.scalar.activation(r32(h[:, 0, 2 * n:2 * n + 2, :]), quarter(n), ACT.Copy).then_inc(h_top, 1)
                top_of_u(0, 1)
                top_of_u(1, 1)
                top_of_v(0, 1)
                gelu(0, 0)
                top_of_u(0, 2)
                top_of_v(1, 1)
                gelu(1, 1)
                top_of_u(1, 2)
                act.wait_ge(y_done, 1)
                top_of_v(0, 2)
                with act.Fori(1, PAIRS - 1) as i:
                    gelu(i * 2, 0)
                    top_of_u(0, i + 2)
                    act.wait_ge(y_done, i * 2)
                    top_of_v(1, i + 1)
                    gelu(i * 2 + 1, 1)
                    top_of_u(1, i + 2)
                    act.wait_ge(y_done, i * 2 + 1)
                    top_of_v(0, i + 2)
                gelu(N - 2, 0)
                act.wait_ge(y_done, N - 2)
                top_of_v(1, PAIRS)
                gelu(N - 1, 1)
                act.wait_ge(root_ready, 1)
                nc.scalar.activation(stats[:, :, 14:15], stats[:, :, 14:15], ACT.Sqrt).then_inc(root_done, 1)

            @block.gpsimd
            def _(pool):
                with pool.Fori(0, PAIRS) as i:
                    for k in range(2):
                        pool.wait_ge(u_top_done, i * 2 + (k + 1))
                        nc.gpsimd.tensor_tensor(r32(low[:, k, 0, :]), raw[:, k, 0, :], top[:, k, 0, :],
                                                ALU.subtract).then_inc(u_low_done, 1)

            @block.vector
            def _(dve):
                step = chain(dve, dve_step)

                def hidden_parts(n, k):
                    dve.wait_ge(a_out, n + 1)
                    gates = S["all_gates"][:, bass.ds(n, 1), :].rearrange("p o t -> p (o t)")
                    whole = act_h[:, k, :]
                    nc.vector.tensor_tensor(whole, whole, gates, ALU.mult).then_inc(gated, 1)
                    dve.wait_ge(gated, n * 2 + 1)
                    nc.vector.tensor_copy(r32(hid[:, k, 0, :]), whole).then_inc(gated, 1)
                    dve.wait_ge(gated, n * 2 + 2)
                    nc.vector.tensor_tensor(r32(hid[:, k, 1, :]), whole, hid[:, k, 0, :], ALU.subtract).then_inc(hid_done, 1)

                def low_of_v(n, k):
                    dve.wait_ge(v_top_done, n + 1)
                    nc.vector.tensor_tensor(r32(low[:, k, 1, :]), raw[:, k, 1, :], top[:, k, 1, :],
                                            ALU.subtract).then_inc(v_low_done, 1)

                for n in range(KD // 2):
                    dve.wait_ge(h_top, n + 1)
                    nc.vector.tensor_tensor(r32(h[:, 1, 2 * n:2 * n + 2, :]), quarter(n), h[:, 0, 2 * n:2 * n + 2, :],
                                            ALU.subtract).then_inc(h_low, 1)
                low_of_v(0, 0)
                with dve.Fori(0, PAIRS - 1) as i:
                    hidden_parts(i * 2, 0)
                    low_of_v(i * 2 + 1, 1)
                    hidden_parts(i * 2 + 1, 1)
                    low_of_v(i * 2 + 2, 0)
                hidden_parts(N - 2, 0)
                low_of_v(N - 1, 1)
                hidden_parts(N - 1, 1)
                dve.wait_ge(ln_in, 32)
                layer_norm(dve, nc, step, S["x"], stats, lambda a, n: PS[:, 4 + 2 * a + n, :],
                           raw[:, 0, 0, :], raw[:, 0, 1, :], lambda a, n: dve.wait_ge(y_done, N), root_ready, root_done)

            @block.tensor
            def _(pe):
                def three_passes(out, lhs, rhs, start, stop):
                    for n, (i, j) in enumerate(((0, 0), (0, 1), (1, 0))):
                        last = nc.tensor.matmul(out, r32(lhs[i]), r32(rhs[j]), start=start and n == 0,
                                                stop=stop and n == 2, skip_group_check=True)
                    return last

                def hidden(n, k):
                    pe.wait_ge(u_low_done, n + 1)
                    for c in range(KD):
                        s = slice(c * P, (c + 1) * P)
                        last = three_passes(PS[:, k, 0:T], (top[:, k, 0, s], low[:, k, 0, s]),
                                            (h[:, 0, c, :], h[:, 1, c, :]), c == 0, c == KD - 1)
                    last.then_inc(a_done, 1)

                def back(n, k, opens=False, closes=False):
                    pe.wait_ge(v_low_done, n + 1)
                    pe.wait_ge(hid_done, n + 1)
                    for a in range(NT):
                        for m in range(2):
                            t, d = slice(a * P, (a + 1) * P), slice(m * BANK, (m + 1) * BANK)
                            last = three_passes(PS[:, 4 + 2 * a + m, :], (hid[:, k, 0, t], hid[:, k, 1, t]),
                                                (top[:, k, 1, d], low[:, k, 1, d]), opens, closes)
                    last.then_inc(y_done, 1)

                for n in range(KD // 2):
                    for k in range(2):
                        for a in range(NT):
                            last = nc.tensor.transpose(PS[:, n, k * T + a * P:k * T + (a + 1) * P],
                                                       S["x"][:, a, (2 * n + k) * P:(2 * n + k + 1) * P],
                                                       S["const"]["ident"])
                    last.then_inc(transposed, 1)
                pe.wait_ge(h_low, KD // 2)
                hidden(0, 0)
                hidden(1, 1)
                back(0, 0, opens=True)
                with pe.Fori(1, PAIRS) as i:
                    hidden(i * 2, 0)
                    back(i * 2 - 1, 1)
                    hidden(i * 2 + 1, 1)
                    back(i * 2, 0)
                back(N - 1, 1, closes=True)



def program(nc, dram, out):
    with ExitStack() as whole:
        psum = whole.enter_context(nc.psum_tensor("psum", [P, BANKS, BANK], F32))
        x = sbuf(nc, whole, "x", [P, NT, D])
        S = {"psum": psum, "const": {}, "x": x, "dram": dram}
        S["const_all"] = place_constants(nc, S, whole, ALWAYS)
        first_block(nc, S)
        second_block(nc, S)

        with phase(nc, "stored") as (memory, stored):
            with nc.Block() as block:
                @block.sync
                def _(sp):
                    sp.dma_start(out.rearrange("o (a p) d -> p (o a) d", p=P), x[:, :, :]).then_inc(stored, 16)
                    sp.wait_ge(stored, 16)


def first_block(nc, S):
    dram = S["dram"]
    with ExitStack() as memory:
        const_mixers, const_first = (place_constants(nc, S, memory, pack) for pack in (MIXERS, FIRST))
        small = {"norm1_g": [P, KD], "norm2_g": [P, KD], "mu_prev": [P, RWKV_TILES], "mu_next": [P, RWKV_TILES],
                 "w_decay0": [P, 2 * RT], "a_gate0": [P, 2 * RT], "k_k": [P, RT], "k_a": [P, RT], "r_k": [P, RT],
                 "gn_w": [P, RT], "gn_b": [P, RT], "b_merge": [P, 2 * KD], "g_up": [P, RC],
                 "router": [P, KD, MOE_GROUPS + EXPERTS]}
        buf = {k: sbuf(nc, memory, f"{k}_sb", s) for k, s in small.items()}
        buf["lora_up"] = sbuf(nc, memory, "lora_up_sb", [P, 2, RC])
        buf["positions"] = sbuf(nc, memory, "positions_sb", [P, NT], I32)
        rows = {"q_norm_g": HD, "k_norm_g": HD}
        for k, n in rows.items():
            buf[k] = sbuf(nc, memory, f"{k}_sb", [P, n])
        buf["router_bias"] = sbuf(nc, memory, "router_bias_sb", [P, MOE_GROUPS + EXPERTS])
        S["weights"] = {k: v[:, :] if len(v.shape) == 2 else v for k, v in buf.items()}
        W = S["weights"]

        with phase(nc, "loaded") as (_, loaded):
            with nc.Block() as block:
                @block.sync
                def _(sp):
                    sp.dma_start(S["x"][:, :, :], dram["x"].rearrange("(a p) d -> p a d", p=P)).then_inc(loaded, 16)
                    sp.dma_start(S["const_all"][:, :], dram[ALWAYS]).then_inc(loaded, 16)
                    for k in ("norm1_g", "b_merge"):
                        sp.dma_start(buf[k][:, :], dram[k]).then_inc(loaded, 16)
                    sp.wait_ge(loaded, 16 * 4)

        loads = [(const_mixers[:, :], dram[MIXERS]), (const_first[:, :], dram[FIRST])]
        loads += [(buf[k][:, :], dram[k]) for k in small if k not in ("norm1_g", "b_merge", "router")]
        loads += [(buf["router"][:, :, 0:MOE_GROUPS], dram["w_router_group"]),
                  (buf["router"][:, :, MOE_GROUPS:], dram["w_router_expert"]),
                  (buf["lora_up"][0:HD, :, :], dram["w_decay_up"].rearrange("d k n -> k d n")),
                  (buf["lora_up"][HD:P, :, :], dram["a_gate_up"].rearrange("d k n -> k d n")),
                  (buf["positions"][:, :], dram["positions"]),
                  (buf["router_bias"][:, 0:MOE_GROUPS], dram["b_router_group"].partition_broadcast(P)),
                  (buf["router_bias"][:, MOE_GROUPS:], dram["b_router_expert"].partition_broadcast(P))]
        loads += [(buf[k][:, :], dram[k].partition_broadcast(P)) for k in rows]

        with ExitStack() as mixers:
            R = {}
            S["rwkv"] = R
            R["y"] = sbuf(nc, mixers, "rwkv_y", [P, RT, T])
            R["bonus"] = sbuf(nc, mixers, "rwkv_bonus", [P, RT, T])
            R["gate"] = sbuf(nc, mixers, "rwkv_gate", [P, RT, T])
            S["gates"] = sbuf(nc, mixers, "branch_gates", [P, 2 * KD, T])
            S["qkv"] = sbuf(nc, mixers, "qkv", [P, NT, 3 * AC])
            with ExitStack() as rwkv:
                for k in "abkr":
                    R[k] = sbuf(nc, rwkv, f"rwkv_{k}", [P, 2, RT, T])
                R["v_rows"] = sbuf(nc, rwkv, "rwkv_v_rows", [P, NT, RC])
                R["b_rows"] = sbuf(nc, rwkv, "rwkv_b_rows", [P, 2, RC])
                R["k_rows"] = sbuf(nc, rwkv, "rwkv_k_rows", [P, 2, RC])
                R["carry"] = sbuf(nc, rwkv, "rwkv_carry", [P, 2, RT])
                with ExitStack() as raw:
                    u = S["u_rwkv"] = sbuf(nc, raw, "u_rwkv", [P, RWKV_TILES, T + 2])
                    with phase(nc, "") as (_,):
                        with nc.Block() as block:
                            @block.vector
                            def _(dve):
                                nc.vector.memset(u[:, :, 0:1], 0.0)
                                nc.vector.memset(u[:, :, T + 1:T + 2], 0.0)

                    A0 = RWKV_COLS
                    G0 = RWKV_COLS + 3 * AC
                    slabs = ([(c, 512, "columns") for c in (0, 512, 1024)] + [(1536, 256, "columns")] +
                             [(A0 + c, 512, "rows") for c in range(0, 2048, 512)] + [(A0 + 2048, 256, "rows")] +
                             [(G0 + c, 512, "columns") for c in range(0, 2048, 512)])

                    def evacuate(name, eng, form, bank, c0, a):
                        if form == "rows":
                            out = S["qkv"][:, a, c0 - A0:c0 - A0 + bank.shape[-1]]
                            return (nc.vector.tensor_copy(out, bank) if name == "dve"
                                    else nc.scalar.activation(out, bank, ACT.Copy))
                        two = bank.rearrange("p (c t) -> p c t", t=T)
                        if c0 < A0:
                            out = u[:, c0 // P:c0 // P + 2, 1:T + 1]
                            return (nc.vector.tensor_copy(out, two) if name == "dve"
                                    else nc.scalar.activation(out, two, ACT.Copy))
                        g = (c0 - G0) // P
                        out = S["gates"][:, g:g + 2, :]
                        bias = W["b_merge"][:, g:g + 2].unsqueeze(2).to_broadcast([P, 2, T])
                        if name == "dve":
                            return nc.vector.tensor_tensor(out, two, bias, ALU.add)
                        nc.scalar.activation(out[:, 0, :], two[:, 0, :], ACT.Identity, bias=W["b_merge"][:, g:g + 1])
                        return nc.scalar.activation(out[:, 1, :], two[:, 1, :], ACT.Identity,
                                                    bias=W["b_merge"][:, g + 1:g + 2])

                    project(nc, S, "in1", S["x"], dram["w_in"], slabs, norm_scale=W["norm1_g"],
                            evacuate=evacuate, loads=loads, scaled=S["qkv"][:, :, 0:D])
                    R["mixed"] = sbuf(nc, raw, "mixed_u", [P, RWKV_TILES, T])
                    rwkv_prepare(nc, S)
                rwkv_scan(nc, S)
            rwkv_finish(nc, S)
            with ExitStack() as out_weights:
                S["w_rwkv_out"] = sbuf(nc, out_weights, "w_rwkv_out_sb", [P, RT, D])
                S["w_attn_out"] = sbuf(nc, out_weights, "w_attn_out_sb", [P, 2, D])
                S["w_out"] = sbuf(nc, out_weights, "w_out_sb", [P, KD, D])
                S["attn_cols"] = sbuf(nc, out_weights, "attn_cols", [P, 2, T])
                attention(nc, S)
                merge(nc, S)
        with ExitStack() as moe:
            S["h_cols"] = sbuf(nc, moe, "h_cols", [P, KD, T])
            S["h_rows"] = sbuf(nc, moe, "h_rows", [P, NT, D])
            S["slots"] = sbuf(nc, moe, "slots", [P, NT, EXPERTS + OVERFLOW])
            S["shares"] = sbuf(nc, moe, "shares", [P, NT, EXPERTS + OVERFLOW])
            S["over_expert"] = sbuf(nc, moe, "over_expert", [P, OVERFLOW], I32)
            project(nc, S, "norm2", S["x"], dram["w_in"], [], cols=S["h_cols"], norm_scale=W["norm2_g"], scaled=S["h_rows"])
            route(nc, S)
            experts(nc, S)


def second_block(nc, S):
    dram = S["dram"]
    with nc.Fori(0, LAYERS) as layer:
        def one(name, inner="p n"):
            a, *b = inner.split()
            return dram[name][(bass.ds(layer, 1),) + (slice(None),) * (len(inner.split()))].rearrange(
                f"l {inner} -> (l {a}) {' '.join(b)}")

        with ExitStack() as mixers:
            L = S["layer"] = {k: sbuf(nc, mixers, f"{k}_row", [P, n]) for k, n in
                              (("subln_g", 2 * HD),
                               ("lambda_init", 2))}
            lam = sbuf(nc, mixers, "lam_rows", [P, 4, HD])
            const = place_constants(nc, S, mixers, MIXERS)
            w_o = sbuf(nc, mixers, "w_o", [P, KD, D])
            ln1 = sbuf(nc, mixers, "ln1_rows", [P, 2, D])
            loads = [(L[k][:, :], one_row(S, k + "_2", layer)) for k in L]
            loads += [(lam[:, i, :], one_row(S, k + "_2", layer)) for i, k in enumerate(("lam_q1", "lam_k1", "lam_q2", "lam_k2"))]
            loads += [(ln1[:, i, :], one_row(S, k, layer)) for i, k in enumerate(("ln1_g_2", "ln1_b_2"))]
            loads += [(const[:, :], dram[MIXERS])]
            loads += [(w_o[:, k, :], one("w_o_2", "k n")[k * P:(k + 1) * P, :]) for k in range(KD)]
            for k in list(L):
                L[k] = L[k][:, :]
            L.update(lam=lam, w_o=w_o, ln1=ln1)

            S["mixed"] = sbuf(nc, mixers, "mixed_rows", [P, NT, D])
            S["dqk"] = sbuf(nc, mixers, "dqk", [P, 2 * DH, T])
            S["sqk"] = sbuf(nc, mixers, "sqk", [P, SH, T])
            S["dv"] = sbuf(nc, mixers, "dv", [P, NT, DH * 2 * HD])
            S["sv"] = sbuf(nc, mixers, "sv", [P, NT, SH * HD])
            slabs = [(0, 512, "columns"), (512, 512, "columns"), (1024, 512, "rows"),
                     (1536, 512, "columns"), (2048, 512, "columns"), (2560, 512, "rows")]

            def evacuate(name, eng, form, bank, c0, a):
                if form == "rows":
                    to, at = ("dv", c0 - 1024) if c0 < 1536 else ("sv", c0 - 2560)
                    to, src = S[to][:, a, at:at + bank.shape[-1]], bank
                elif c0 < 1024:
                    to, src = S["dqk"][:, c0 // P:c0 // P + 2, :], bank.rearrange("p (c t) -> p c t", t=T)
                else:
                    c = (c0 - 1536) // P
                    to, src = S["sqk"][:, c:c + 2, :], bank.rearrange("p (c t) -> p c t", t=T)
                return nc.vector.tensor_copy(to, src) if name == "dve" else nc.scalar.activation(to, src, ACT.Copy)

            project(nc, S, "in2", S["x"], one("w_in_2", "k n"), slabs, evacuate=evacuate,
                    loads=loads)
            differential(nc, S)
            stick_breaking(nc, S)
            mix_out(nc, S)

        with ExitStack() as peer:
            S["all_gates"] = sbuf(nc, peer, "all_gates", [P, NKEYS, T])
            with ExitStack() as chosen:
                S["idx_cols"] = sbuf(nc, chosen, "idx_cols", [P, 2, T])
                S["gate_cols"] = sbuf(nc, chosen, "gate_cols", [P, TOPK, T])
                spare = carve(S["all_gates"])
                q = S["q_cols"] = spare([P, 2 * PH, T])
                S["keys"] = spare([P, 2 * PH, NKEYS])

                def evacuate_q(name, eng, form, bank, c0, a):
                    to, src = q[:, c0 // P:c0 // P + 2, :], bank.rearrange("p (c t) -> p c t", t=T)
                    return nc.vector.tensor_copy(to, src) if name == "dve" else nc.scalar.activation(to, src, ACT.Copy)

                project(nc, S, "query", S["x"], one("w_query_2", "k n"),
                        [(c, 512, "columns") for c in range(0, 2048, 512)], evacuate=evacuate_q,
                        raw=spare([P, 2, KD, 2 * P]), loads=[(S["keys"], one("sub_keys_2", "p e n"))])
                peer_select(nc, S, spare)
                peer_spread(nc, S)
            u, v = dram["expert_u_2"], dram["expert_v_2"]
            S["u_src"] = lambda j: u[bass.ds(layer * NKEYS + j, 1), :, :, :].rearrange("j p k i -> (j p) k i")
            S["v_src"] = lambda j: v[bass.ds(layer * NKEYS + j, 1), :, :].rearrange("j i d -> (j i) d")
            peer_experts(nc, S, layer)


def layout(inputs):
    def get(name):
        a = np.asarray(inputs[name])
        return a[0] if name in ONE_LAYER else a

    def channels(a):
        return a.reshape(-1, P).T

    arrays = {"x": get("x"), "positions": np.asarray(inputs["positions"]).reshape(NT, P).T}
    for pack in (ALWAYS, MIXERS, FIRST):
        arrays[pack] = np.concatenate([v for k, v in constants().items() if pack_of(k) == pack], axis=1)
    for k in ("norm1_g", "norm2_g", "mu_prev", "mu_next", "w_decay0", "a_gate0", "k_k", "k_a", "r_k", "gn_w", "gn_b",
              "b_merge"):
        arrays[k] = channels(get(k))
    for k in ("w_in", "w_decay_up", "a_gate_up", "g_up", "w_rwkv_out", "q_norm_g", "k_norm_g", "w_attn_out", "w_out",
              "b_router_group", "b_router_expert", "w_gate", "w_up", "w_down"):
        arrays[k] = get(k)
    arrays["norm2_g_row"] = get("norm2_g")
    for k in ("w_router_group", "w_router_expert"):
        arrays[k] = get(k).reshape(KD, P, -1).transpose(1, 0, 2)
    for k in ("w_in", "lam_q1", "lam_k1", "lam_q2", "lam_k2", "subln_g", "w_o", "ln1_g", "ln1_b", "w_query", "ln2_g",
              "ln2_b"):
        arrays[k + "_2"] = get(k + "_2")
    init = [0.8 - 0.6 * math.exp(-0.3 * l) for l in range(LAYERS)]
    arrays["lambda_init_2"] = np.array([[i, 1 - i] for i in init], np.float32)
    arrays["sub_keys_2"] = get("sub_keys_2").reshape(LAYERS, 2 * PH, NKEYS, P).transpose(0, 3, 1, 2)
    arrays["expert_u_2"] = get("expert_u_2").reshape(LAYERS, NKEYS, NKEYS, KD, P).transpose(0, 2, 4, 3, 1) \
        .reshape(LAYERS * NKEYS, P, KD, NKEYS)
    arrays["expert_v_2"] = get("expert_v_2").reshape(LAYERS, NKEYS, NKEYS, D).transpose(0, 2, 1, 3) \
        .reshape(LAYERS * NKEYS, NKEYS, D)
    return {k: np.ascontiguousarray(v) for k, v in arrays.items()}


ONE_LAYER = {"x", "norm1_g", "w_in", "mu_prev", "mu_next", "w_decay0", "w_decay_up", "a_gate0", "a_gate_up", "g_up",
             "k_k", "k_a", "r_k", "gn_w", "gn_b", "w_rwkv_out", "q_norm_g", "k_norm_g", "w_attn_out", "b_merge",
             "w_out", "norm2_g", "w_router_group", "b_router_group", "w_router_expert", "b_router_expert", "w_gate",
             "w_up", "w_down"}


def kernel(**inputs):
    import concourse.bacc as bacc
    from concourse.bass_utils import run_bass_kernel_spmd

    nc = bacc.Bacc("TRN2", target_bir_lowering=False, num_devices=1)
    arrays = {f"{k}_dram": v for k, v in layout(inputs).items()}
    dram = {k[:-5]: nc.dram_tensor(k, v.shape, mybir.dt.from_np(v.dtype), kind="ExternalInput").ap()
            for k, v in arrays.items()}
    out = nc.dram_tensor("out_dram", (1, T, D), F32, kind="ExternalOutput").ap()
    program(nc, dram, out)
    result = run_bass_kernel_spmd(nc, [arrays], core_ids=[0])
    return result.results[0]["out_dram"]
```
